# Optimizing a Trainium2 kernel written in Bass

```python
import jax, jax.numpy as jnp
from jax import lax
import numpy as np

D_MODEL = 1024
BATCH = 1
SEQ = 128
DEPTH = 2
DEC_BATCH = 1
DEC_SEQ = 256
PAST_LEN = 128

GRID_W = 64
N_MIXERS = 2
N_CONV_LAYERS = (DEPTH + 1) // 2
N_DN_LAYERS = DEPTH // 2
D_FF = 2816
CONV_WIDTH = 31
DN_HEADS = 8
DN_DK = 128
DN_DV = 128
DN_QK = DN_HEADS * DN_DK
DN_VD = DN_HEADS * DN_DV
DN_PROJ = 2 * DN_QK + 2 * DN_VD + 4 * DN_HEADS
DN_SHORT_CONV = 3
DN_CHUNK = 64
N_MOD = 9
DEEPNORM_ALPHA = (2.0 * DEPTH) ** 0.25
DEEPNORM_BETA = (8.0 * DEPTH) ** -0.25
LN_EPS = 1e-5

kernel_name = "hybrid_conv_deltanet_flow_step"

def layer_norm(x, g, b):
    xf = x.astype(jnp.float32)
    xc = xf - jnp.mean(xf, -1, keepdims=True)
    var = jnp.mean(xc * xc, -1, keepdims=True)
    y = xc * lax.rsqrt(var + LN_EPS) * g.astype(jnp.float32) + b.astype(jnp.float32)
    return y.astype(x.dtype)

def rms_norm(x, g):
    xf = x.astype(jnp.float32)
    return xf * lax.rsqrt(jnp.mean(xf * xf, -1, keepdims=True) + LN_EPS) * g.astype(jnp.float32)

def l2_normalize(x):
    return x * lax.rsqrt(jnp.sum(x * x, -1, keepdims=True) + 1e-6)

def adaln_params(cond, w_mod_l, b_mod_l):
    m = jax.nn.silu(cond) @ w_mod_l + b_mod_l
    return m.reshape(cond.shape[0], 1, N_MOD, D_MODEL)

def modulate(x, m, slot):
    return x * (1.0 + m[:, :, 3 * slot + 1]) + m[:, :, 3 * slot]

def swiglu_ffn(h, w_in, w_out):
    a = h @ w_in
    return (jax.nn.silu(a[..., D_FF:]) * a[..., :D_FF]) @ w_out

def dwconv_seq(x, w):
    k, ch = w.shape
    return lax.conv_general_dilated(x, w.astype(x.dtype)[:, None, :], (1,), [(k // 2, k // 2)],
                                    dimension_numbers=("NWC", "WIO", "NWC"), feature_group_count=ch)

def dwconv_grid(x, w):
    bsz, length, ch = x.shape
    rows = length // GRID_W
    k = w.shape[0]
    half = ch // 2
    xg = x.reshape(bsz, rows, GRID_W, ch)
    w = w.astype(x.dtype)
    dn = ("NHWC", "HWIO", "NHWC")
    horiz = lax.conv_general_dilated(xg[..., :half], w[:, :half].reshape(1, k, 1, half), (1, 1),
                                     [(0, 0), (k // 2, k // 2)], dimension_numbers=dn, feature_group_count=half)
    vert = lax.conv_general_dilated(xg[..., half:], w[:, half:].reshape(k, 1, 1, ch - half), (1, 1),
                                    [(k // 2, k // 2), (0, 0)], dimension_numbers=dn, feature_group_count=ch - half)
    return jnp.concatenate([horiz, vert], -1).reshape(bsz, length, ch)

def conv_module(h, w1, b1, dw, dwb, lng, lnb, w2, b2, on_grid):
    a = h @ w1 + b1
    a = a[..., :D_MODEL] * jax.nn.sigmoid(a[..., D_MODEL:])
    a = (dwconv_grid(a, dw) if on_grid else dwconv_seq(a, dw)) + dwb
    a = jax.nn.silu(layer_norm(a, lng, lnb))
    return a @ w2 + b2

def delta_rule_chunked(q, k, v, log_a, beta, s0):
    bsz, nh, length, dk = q.shape
    dv = v.shape[-1]
    n = length // DN_CHUNK
    r = lambda t: t.reshape(bsz, nh, n, DN_CHUNK, *t.shape[3:])
    q, k, v, log_a, beta = r(q), r(k), r(v), r(log_a), r(beta)
    g = jnp.cumsum(log_a, axis=-1)
    diff = g[..., :, None] - g[..., None, :]
    idx = jnp.arange(DN_CHUNK)
    incl = idx[:, None] >= idx[None, :]
    strict = idx[:, None] > idx[None, :]
    dec_incl = jnp.exp(jnp.where(incl, diff, -jnp.inf))
    dec_strict = jnp.where(strict, dec_incl, 0.0)
    a_mat = beta[..., :, None] * jnp.einsum("bhnid,bhnjd->bhnij", k, k) * dec_strict
    eye = jnp.eye(DN_CHUNK, dtype=jnp.float32)
    rhs = jnp.concatenate([beta[..., None] * v, (beta * jnp.exp(g))[..., None] * k], -1)
    sol = lax.linalg.triangular_solve(eye + a_mat, rhs, left_side=True, lower=True, unit_diagonal=True)
    u_t, w_t = sol[..., :dv], sol[..., dv:]
    p_mat = jnp.einsum("bhnid,bhnjd->bhnij", q, k) * dec_incl
    qg = q * jnp.exp(g)[..., None]
    g_last = g[..., -1:]
    kd = k * jnp.exp(g_last - g)[..., None]
    gl = jnp.exp(g_last[..., 0])
    xs = tuple(jnp.moveaxis(t, 2, 0) for t in (u_t, w_t, p_mat, qg, kd, gl))

    def step(s, inp):
        ut, wt, pt, qt, kt, gt = inp
        u = ut - jnp.einsum("bhck,bhkv->bhcv", wt, s)
        o = jnp.einsum("bhck,bhkv->bhcv", qt, s) + jnp.einsum("bhij,bhjv->bhiv", pt, u)
        s = gt[..., None, None] * s + jnp.einsum("bhck,bhcv->bhkv", kt, u)
        return s, o

    s_fin, o = lax.scan(step, s0, xs)
    o = jnp.moveaxis(o, 0, 2).reshape(bsz, nh, length, dv)
    return o, s_fin

def deltanet_mixer(h, w_in, conv_w, a_log, dt_bias, norm_g, w_out, s0):
    bsz, length, _ = h.shape
    proj = h @ w_in
    n_qkv = 2 * DN_QK + DN_VD
    qkv = jax.nn.silu(dwconv_seq(proj[..., :n_qkv], conv_w))
    z = proj[..., n_qkv:n_qkv + DN_VD]
    ab = proj[..., n_qkv + DN_VD:].astype(jnp.float32).reshape(bsz, length, 4, DN_HEADS)

    def heads(t, d):
        return t.reshape(bsz, length, DN_HEADS, d).transpose(0, 2, 1, 3).astype(jnp.float32)

    q = l2_normalize(heads(qkv[..., :DN_QK], DN_DK)) * (DN_DK ** -0.5)
    k = l2_normalize(heads(qkv[..., DN_QK:2 * DN_QK], DN_DK))
    v = heads(qkv[..., 2 * DN_QK:], DN_DV)
    log_alpha = -jnp.exp(a_log.astype(jnp.float32)) * jax.nn.softplus(ab[:, :, :2] + dt_bias.astype(jnp.float32))
    beta = jax.nn.sigmoid(ab[:, :, 2:])
    log_alpha = log_alpha.transpose(2, 0, 3, 1)
    beta = beta.transpose(2, 0, 3, 1)
    s0 = s0.astype(jnp.float32)
    o_f, s_f = delta_rule_chunked(q, k, v, log_alpha[0], beta[0], s0[:, 0])
    rev = lambda t: jnp.flip(t, axis=2)
    o_b, s_b = delta_rule_chunked(rev(q), rev(k), rev(v), rev(log_alpha[1]), rev(beta[1]), s0[:, 1])
    o = (o_f + rev(o_b)).transpose(0, 2, 1, 3)
    o = rms_norm(o, norm_g) * jax.nn.silu(z.reshape(bsz, length, DN_HEADS, DN_DV).astype(jnp.float32))
    out = o.reshape(bsz, length, DN_VD).astype(h.dtype) @ w_out
    return out, jnp.stack([s_f, s_b], axis=1)

def run_trunk(x, cond, dn_state, on_grid, w_mod, b_mod, ln_g, ln_b, ffn_w_in, ffn_w_out,
              cv_w1, cv_b1, cv_dw, cv_dwb, cv_ln_g, cv_ln_b, cv_w2, cv_b2,
              dn_w_in, dn_conv, dn_a_log, dn_dt_bias, dn_norm_g, dn_w_out):
    final_states = []
    for l in range(DEPTH):
        m = adaln_params(cond, w_mod[l], b_mod[l])
        y = swiglu_ffn(modulate(x, m, 0), ffn_w_in[l, 0], ffn_w_out[l, 0])
        x = layer_norm(DEEPNORM_ALPHA * x + 0.5 * m[:, :, 2] * y, ln_g[l, 0], ln_b[l, 0])
        h = modulate(x, m, 1)
        j = l // N_MIXERS
        if l % N_MIXERS == 0:
            y = conv_module(h, cv_w1[j], cv_b1[j], cv_dw[j], cv_dwb[j], cv_ln_g[j], cv_ln_b[j],
                            cv_w2[j], cv_b2[j], on_grid)
        else:
            y, s_fin = deltanet_mixer(h, dn_w_in[j], dn_conv[j], dn_a_log[j], dn_dt_bias[j],
                                      dn_norm_g[j], dn_w_out[j], dn_state[:, j])
            final_states.append(s_fin)
        x = layer_norm(DEEPNORM_ALPHA * x + m[:, :, 5] * y, ln_g[l, 1], ln_b[l, 1])
        y = swiglu_ffn(modulate(x, m, 2), ffn_w_in[l, 1], ffn_w_out[l, 1])
        x = layer_norm(DEEPNORM_ALPHA * x + 0.5 * m[:, :, 8] * y, ln_g[l, 2], ln_b[l, 2])
    return x, final_states

def setup_inputs(seed: int = 0) -> dict:
    key = jax.random.key(seed)
    ks = jax.random.split(key, 32)
    f32 = jnp.float32
    nrm = lambda i, shape, s: jax.random.normal(ks[i], shape, f32) * s
    d = D_MODEL
    dt = jnp.exp(jax.random.uniform(ks[24], (N_DN_LAYERS, 2, DN_HEADS), f32, np.log(1e-3), np.log(1e-1)))
    return {
        "x_prompt": nrm(0, (BATCH, SEQ, d), 1.0),
        "x_sample": nrm(1, (DEC_BATCH, DEC_SEQ, d), 1.0),
        "state_delta": nrm(2, (DEC_BATCH, N_DN_LAYERS, 2, DN_HEADS, DN_DK, DN_DV), 0.3),
        "c": nrm(3, (DEC_BATCH, d), 1.0),
        "c_ctx": nrm(4, (d,), 1.0),
        "w_mod": nrm(5, (DEPTH, d, N_MOD * d), 0.5 * d ** -0.5),
        "b_mod": nrm(6, (DEPTH, N_MOD * d), 0.02),
        "ln_g": 1.0 + nrm(7, (DEPTH, 3, d), 0.02),
        "ln_b": nrm(8, (DEPTH, 3, d), 0.02),
        "ffn_w_in": nrm(9, (DEPTH, 2, d, 2 * D_FF), d ** -0.5),
        "ffn_w_out": nrm(10, (DEPTH, 2, D_FF, d), DEEPNORM_BETA * D_FF ** -0.5),
        "cv_w1": nrm(11, (N_CONV_LAYERS, d, 2 * d), d ** -0.5),
        "cv_b1": nrm(12, (N_CONV_LAYERS, 2 * d), 0.02),
        "cv_dw": nrm(13, (N_CONV_LAYERS, CONV_WIDTH, d), CONV_WIDTH ** -0.5),
        "cv_dwb": nrm(14, (N_CONV_LAYERS, d), 0.02),
        "cv_ln_g": 1.0 + nrm(15, (N_CONV_LAYERS, d), 0.02),
        "cv_ln_b": nrm(16, (N_CONV_LAYERS, d), 0.02),
        "cv_w2": nrm(17, (N_CONV_LAYERS, d, d), DEEPNORM_BETA * d ** -0.5),
        "cv_b2": nrm(18, (N_CONV_LAYERS, d), 0.02),
        "dn_w_in": nrm(19, (N_DN_LAYERS, d, DN_PROJ), d ** -0.5),
        "dn_conv": nrm(20, (N_DN_LAYERS, DN_SHORT_CONV, 2 * DN_QK + DN_VD), DN_SHORT_CONV ** -0.5),
        "dn_a_log": jnp.log(jax.random.uniform(ks[21], (N_DN_LAYERS, 2, DN_HEADS), f32, 1.0, 16.0)),
        "dn_dt_bias": jnp.log(jnp.expm1(dt)),
        "dn_norm_g": 1.0 + nrm(22, (N_DN_LAYERS, DN_DV), 0.02),
        "dn_w_out": nrm(23, (N_DN_LAYERS, DN_VD, d), DEEPNORM_BETA * DN_VD ** -0.5),
    }

def reference(x_prompt, x_sample, state_delta, c, c_ctx, w_mod, b_mod, ln_g, ln_b, ffn_w_in, ffn_w_out,
              cv_w1, cv_b1, cv_dw, cv_dwb, cv_ln_g, cv_ln_b, cv_w2, cv_b2,
              dn_w_in, dn_conv, dn_a_log, dn_dt_bias, dn_norm_g, dn_w_out):
    zero_state = jnp.zeros((x_prompt.shape[0], N_DN_LAYERS, 2, DN_HEADS, DN_DK, DN_DV), jnp.float32)
    y_prompt, ctx_states = run_trunk(x_prompt, c_ctx[None, :], zero_state, False, w_mod, b_mod, ln_g, ln_b,
                                     ffn_w_in, ffn_w_out, cv_w1, cv_b1, cv_dw, cv_dwb, cv_ln_g, cv_ln_b,
                                     cv_w2, cv_b2, dn_w_in, dn_conv, dn_a_log, dn_dt_bias, dn_norm_g, dn_w_out)
    y_sample, _ = run_trunk(x_sample, c, state_delta, True, w_mod, b_mod, ln_g, ln_b,
                            ffn_w_in, ffn_w_out, cv_w1, cv_b1, cv_dw, cv_dwb, cv_ln_g, cv_ln_b,
                            cv_w2, cv_b2, dn_w_in, dn_conv, dn_a_log, dn_dt_bias, dn_norm_g, dn_w_out)
    new_state_delta = jnp.stack(ctx_states, axis=1).astype(state_delta.dtype)
    return (y_prompt, y_sample, new_state_delta)


_drawn_inputs = setup_inputs


def setup_inputs(seed=0):
    import zlib

    import numpy as np

    out = dict(_drawn_inputs(seed))
    spreads = {}
    factors = {'cv_b1': 8.0,
     'cv_dwb': 8.0,
     'cv_ln_g': 31.196,
     'cv_ln_b': 30.938,
     'cv_b2': 8.0,
     'dn_norm_g': 58.929}
    for name, (base, spread) in spreads.items():
        noise = np.random.default_rng([zlib.crc32(name.encode()), seed]).standard_normal(out[name].shape)
        drawn = base * np.exp(spread * noise) if base else spread * noise
        out[name] = __import__('jax').numpy.asarray(drawn.astype(out[name].dtype))
    for name, factor in factors.items():
        out[name] = (out[name] * factor).astype(out[name].dtype)
    return out
```

```python
import numpy as np
import concourse.bass as bass
from concourse import mybir

F32 = mybir.dt.float32
F32R = mybir.dt.float32r
I32 = mybir.dt.int32
ACT = mybir.ActivationFunctionType
ALU = mybir.AluOpType
ds = bass.ds

P = 128
D = 1024
KC = D // P
DEPTH = 2
DFF = 2816
FC = DFF // P
TP, TS = 128, 256
T = TP + TS
NT = T // P
GW = 64
TAPS = 31
H = 8
ALPHA = (2.0 * DEPTH) ** 0.25
LN_EPS = 1e-5
GROUPS = ((0, 0, TP), (1, TP, T))
RING = 4

DN_BLOCKS = 32
UNITS = (2 * FC + 3 * KC, 2 * KC + KC, 2 * FC + 3 * KC, 2 * FC + 3 * KC, DN_BLOCKS + KC, 2 * FC + 3 * KC)
UNIT0 = tuple(sum(UNITS[:s]) for s in range(6))
FFN_THIRDS = ((0, 8), (8, 15), (15, 22))

COL_BMOD = (0, P)
COL_LNG, COL_LNB = 72, P + 72
COL_DW = 2 * P
COL_C = 3 * P + 120
COL_DNCONV = 4 * P
COL_B1, COL_DWB, COL_CLNG, COL_CLNB, COL_B2, COL_CCTX = (4 * P + n for n in (72, 88, 96, 104, 112, 120))

MOD_FIRST = 4
MOD_IN_FFN = {0: 1, 2: 3}



def program(nc, x_prompt, x_sample, state_delta, c, c_ctx, w_mod, b_mod, ln_g, ln_b, ffn_w_in, ffn_w_out,
            cv_w1, cv_b1, cv_dw, cv_dwb, cv_ln_g, cv_ln_b, cv_w2, cv_b2,
            dn_w_in, dn_conv, dn_a_log, dn_dt_bias, dn_norm_g, dn_w_out,
            y_prompt, y_sample, new_state, stages=6):
    from contextlib import ExitStack, contextmanager
    ctx = ExitStack()
    with ctx:
        def sb(name, shape, dt=F32, where=ctx):
            return where.enter_context(nc.sbuf_tensor(name, shape, dt))

        def sem(name):
            return ctx.enter_context(nc.semaphore(name))

        x = sb("x", [P, KC, T])
        r = sb("r", [P, KC, T])
        h_hi = sb("h_hi", [P, KC, T], F32R)
        h_lo = sb("h_lo", [P, KC, T], F32R)
        h_full = sb("h_full", [P, 4, T])
        w_raw = sb("w_raw", [P, RING, 8, P])
        w_hi = sb("w_hi", [P, RING, 8, P], F32R)
        w_lo = sb("w_lo", [P, RING, 8, P], F32R)
        mod = sb("mod", [P, DEPTH * 72, 2])
        scale1 = sb("scale1", [P, KC, 2])
        gate = sb("gate", [P, KC, 2])
        params = sb("params", [P, 5 * P])
        cond = sb("cond", [P, KC, 2])
        ident = sb("ident", [P, P])
        mean_w = sb("mean_w", [P, P])
        eps = sb("eps", [P, 1])
        begun = sb("begun", [P, 4])
        r_sum = sb("r_sum", [P, T])
        square = sb("square", [P, 4, T])
        dev = sb("dev", [P, T])
        rstd = sb("rstd", [P, T])

        with ExitStack() as region:
            mod_raw = sb("mod_raw", [P, 4, 8, P], F32, region)
        with ExitStack() as region:
            qk_decay = sb("qk_decay", [P, 2, NT, P], F32, region)
            step_p = sb("step_p", [P, 2, NT, P], F32, region)
            v_beta = sb("v_beta", [P, 2, NT, P], F32, region)
            k_decay = sb("k_decay", [P, 2, 2, P], F32, region)
            u_sb = sb("u_sb", [P, 2, P], F32, region)
            s_old = sb("s_old", [P, 2, P], F32, region)
            s_new = sb("s_new", [P, 2, P], F32, region)
            s_out = sb("s_out", [P, 2, P], F32, region)
        sb("mod_raw_place", [P, 4, 8, P])

        with ExitStack() as region:
            act_hi = sb("act_hi", [P, FC, T], F32R, region)
            act_lo = sb("act_lo", [P, FC, T], F32R, region)
            silu_g = sb("silu_g", [P, 2, T], F32, region)
            act_full = sb("act_full", [P, 2, T], F32, region)
        with ExitStack() as region:
            x_rows = sb("x_rows", [P, NT, D], F32, region)
            table = sb("table", [P, 5, P], F32, region)

        with ExitStack() as region:
            HALF = TAPS // 2
            GR = TS // GW
            glu_seq = sb("glu_seq", [P, KC, HALF + TP + HALF], F32, region)
            glu_row = sb("glu_row", [P, KC // 2, GR, HALF + GW + HALF], F32, region)
            glu_col = sb("glu_col", [P, KC // 2, TS], F32, region)
            sigm = sb("sigm", [P, 2, T], F32, region)
            conv = sb("conv", [P, KC, T], F32, region)
            row_prod = sb("row_prod", [P, 4, GR, GW], F32, region)
            conv_full = sb("conv_full", [P, 4, T], F32, region)
            y_biased = sb("y_biased", [P, 2, T], F32, region)

        with ExitStack() as region:
            qk = sb("qk", [P, 2 * H, T], F32, region)
            v_tok = sb("v_tok", [P, NT, H, P], F32, region)
            o_all = sb("o_all", [P, H, T], F32, region)
            rows = sb("rows", [H, 4, T], F32, region)
            masks = sb("masks", [P, 14, P], mybir.dt.int8, region)
            tri = sb("tri", [P, 2, P], F32, region)
            never = sb("never", [P, 2, P], F32, region)
            ones = sb("ones", [P, P], F32, region)
            one_hot = sb("one_hot", [P, 4 * H - 1], F32, region)
            sel_q = sb("sel_q", [2 * H, P], F32, region)
            sel_k = sb("sel_k", [2 * H, P], F32, region)
            sel_h = sb("sel_h", [H, P], F32, region)
            qk_norm = sb("qk_norm", [2 * H, T], F32, region)
            qk_rnorm = sb("qk_rnorm", [2 * H, T], F32, region)
            q_scale = sb("q_scale", [2 * H, 2], F32, region)
            w_ab = sb("w_ab", [P, KC, 4 * H], F32, region)
            w_ab_hi = sb("w_ab_hi", [P, KC, 4 * H], F32R, region)
            w_ab_lo = sb("w_ab_lo", [P, KC, 4 * H], F32R, region)
            norm_g = sb("norm_g", [P, 1], F32, region)
            dt_a = sb("dt_a", [P, 2, 2 * H], F32, region)
            small_names = ("exp_a", "tot", "g_col", "end_decay", "g_decay", "tot_decay", "minus_beta_g", "pre", "soft", "pos", "log_a", "beta")
            exp_a, tot, g_col, end_decay, g_decay, tot_decay, minus_beta_g, pre, soft, pos, log_a, beta = (
                sb(n, [P, NT, 2 * H], F32, region) for n in small_names)
            ab = sb("ab", [P, NT, 4 * H], F32, region)
            carrier = sb("carrier", [P, 14], F32, region)
        lin = step_p[:, :, :, :].rearrange("p d t c -> p d (t c)")
        v_silu = v_beta[:, :, :, :].rearrange("p d t c -> p d (t c)")
        z = r
        decay = square[:, 0:2, :].rearrange("p d (t c) -> p d t c", c=P)
        q_decay = square[:, 2:4, :]
        k_head, q_head = dev, rstd
        inv = h_full[:, 0:2, :].rearrange("p d (t c) -> p d t c", c=P)
        inv_t = h_full[:, 2:4, :].rearrange("p d (t c) -> p d t c", c=P)
        SCAN = ((0, 1, 2), (0, 2, 1))
        LEVELS = 7

        bank = [ctx.enter_context(nc.psum_tensor(f"bank{n}", [P, 512], F32)) for n in range(8)]
        mean_ps, var_ps, mod_ps = bank[4], bank[5], bank[6]
        mod_out = mod_ps[:, 0:8].rearrange("p (u c) -> p u c", c=2)

        consts = sem("consts")
        table_in = [sem(f"table_in{n}") for n in range(5)]
        x_in = [sem(f"x_in{n}") for n in range(NT)]
        turned = sem("turned")
        table_out = sem("table_out")
        cond_ready = sem("cond_ready")
        w_in = [sem(f"w_in{n}") for n in range(RING)]
        w_hi_ready = sem("w_hi_ready")
        w_lo_ready = sem("w_lo_ready")
        unit_used = sem("unit_used")
        mod_in = [sem(f"mod_in{n}") for n in range(4)]
        mod_used = sem("mod_used")
        mod_ready = sem("mod_ready")
        small = sem("small")
        silu_ready = sem("silu_ready")
        act_ready = sem("act_ready")
        act_hi_ready = sem("act_hi_ready")
        act_lo_ready = sem("act_lo_ready")
        r_ready = sem("r_ready")
        r_scaled = sem("r_scaled")
        r_summed = sem("r_summed")
        mean_ready = sem("mean_ready")
        centred = sem("centred")
        squared = sem("squared")
        var_added = sem("var_added")
        dev_ready = sem("dev_ready")
        rstd_ready = sem("rstd_ready")
        normed = sem("normed")
        x_ready = sem("x_ready")
        h_ready = sem("h_ready")
        h_hi_ready = sem("h_hi_ready")
        h_lo_ready = sem("h_lo_ready")
        dn_consts = sem("dn_consts")
        dn_small_in = sem("dn_small_in")
        state_in = sem("state_in")
        state_out = sem("state_out")
        lin_step = sem("lin_step")
        silu_done = sem("silu_done")
        v_turned = sem("v_turned")
        v_stored = sem("v_stored")
        qk_squared = sem("qk_squared")
        qk_summed = sem("qk_summed")
        qk_norm_ready = sem("qk_norm_ready")
        w_ab_ready = sem("w_ab_ready")
        ab_ready = sem("ab_ready")
        gate_v = sem("gate_v")
        gate_a = sem("gate_a")
        gate_t = sem("gate_t")
        head_done = sem("head_done")
        sel_ready = sem("sel_ready")
        norm_spread = sem("norm_spread")
        rows_spread = sem("rows_spread")
        qk_ready = sem("qk_ready")
        kk_ready = sem("kk_ready")
        k_turned = sem("k_turned")
        diff_ready = sem("diff_ready")
        decay_ready = sem("decay_ready")
        q_exp_ready = sem("q_exp_ready")
        k_decay_ready = sem("k_decay_ready")
        a_step = sem("a_step")
        q_decay_ready = sem("q_decay_ready")
        inv_begun = sem("inv_begun")
        v_beta_ready = sem("v_beta_ready")
        p_ready = sem("p_ready")
        p_copied = sem("p_copied")
        t_ready = sem("t_ready")
        t_joined = sem("t_joined")
        ks_ready = sem("ks_ready")
        x_set = sem("x_set")
        u_ready = sem("u_ready")
        u_copied = sem("u_copied")
        s_added = sem("s_added")
        s_stored = sem("s_stored")
        s_updated = sem("s_updated")
        o_added = sem("o_added")
        o_squared = sem("o_squared")
        o_summed = sem("o_summed")
        o_norm_ready = sem("o_norm_ready")
        o_rnorm_ready = sem("o_rnorm_ready")
        o_spread = sem("o_spread")
        o_gated = sem("o_gated")
        o_hi = sem("o_hi")
        o_lo = sem("o_lo")
        pads_ready = sem("pads_ready")
        sigm_ready = sem("sigm_ready")
        glu_ready = sem("glu_ready")
        tap_v = sem("tap_v")
        row_tap = sem("row_tap")
        tap_g = sem("tap_g")
        conv_mean = sem("conv_mean")
        conv_centred = sem("conv_centred")
        conv_squared = sem("conv_squared")
        conv_var = sem("conv_var")
        conv_dev = sem("conv_dev")
        conv_rstd = sem("conv_rstd")
        conv_normed = sem("conv_normed")
        conv_act = sem("conv_act")
        conv_hi = sem("conv_hi")
        conv_lo = sem("conv_lo")
        y_ready = sem("y_ready")
        rows_ready = sem("rows_ready")
        out_done = sem("out_done")

        block = ctx.enter_context(nc.Block())

        def in_view(w, cols):
            return w.rearrange("(k p) (b m) -> p k b m", p=P, m=P) if cols else w
        mod_view = [w_mod[l].rearrange("(k p) m -> p k m", p=P) for l in range(DEPTH)]
        x_src = (x_prompt[0, :, :], x_sample[0, 0:P, :], x_sample[0, P:2 * P, :])
        y_dst = (y_prompt[0, :, :], y_sample[0, 0:P, :], y_sample[0, P:2 * P, :])

        DN_CONSTS = 14 + 6 * LEVELS
        GATE_A_BETA = 5
        LAST_UNIT = UNIT0[stages - 1] + UNITS[stages - 1]

        def mod_col(s):
            return 72 * (s // 3) + 24 * (s % 3)

        def ffn_of(s):
            return ffn_w_in[s // 3, (s % 3) // 2], ffn_w_out[s // 3, (s % 3) // 2]

        is_ffn = [s % 3 != 1 for s in range(6)]
        ffns = [sum(is_ffn[:s]) for s in range(7)]
        mod_groups = [MOD_FIRST + sum(FC // 2 + 2 * b + 1 for k, b in MOD_IN_FFN.items() if k < s) for s in range(7)]
        mod_out_groups = [g + FC // 2 for g in mod_groups]
        mod_tail_group = [g + FC // 2 + 2 * MOD_IN_FFN.get(s, 0) for s, g in enumerate(mod_groups)]

        def out_mods(s, q):
            n = 4 * MOD_IN_FFN.get(s, 0)
            return range(n * q // 12, n * (q + 1) // 12)

        @block.sync
        def _(sp):
            def load_unit(u, slot, src, chunks=8, first=False):
                if not first:
                    sp.wait_ge(w_hi_ready, u - RING + 1)
                    sp.wait_ge(w_lo_ready, u - RING + 1)
                sp.dma_start(w_raw[:, slot, 0:chunks], src).then_inc(w_in[slot], 16)

            def load_mod(g0, i, j, first=False):
                if not first:
                    sp.wait_ge(mod_used, 4 * i + (4 * g0 + j - 3))
                l, col = g0 // 18, (g0 % 18 * 4 + j) * P
                sp.dma_start(mod_raw[:, j], mod_view[l][:, :, ds(i * (4 * P) + col, P)]).then_inc(mod_in[j], 16)

            def ffn_in_units(s, i, first=False):
                wv = ffn_of(s)[0].rearrange("(k p) m -> p k m", p=P)
                for j in range(4):
                    col = (j % 2) * DFF + (j // 2) * P
                    load_unit(UNIT0[s] + 4 * i + j, j, wv[:, :, ds(i * (2 * P) + col, P)], first=first)
                    if s in MOD_IN_FFN:
                        load_mod(mod_groups[s], i, j)

            for t in range(5):
                sp.wait_ge(consts, 6)
                rows = {0: ((b_mod[0].rearrange("(r p) -> r p", p=P), 0, 72), (ln_g.rearrange("l j (r p) -> (l j r) p", p=P), 72, 120)),
                        1: ((b_mod[1].rearrange("(r p) -> r p", p=P), 0, 72), (ln_b.rearrange("l j (r p) -> (l j r) p", p=P), 72, 120)),
                        2: ((cv_dw[0].rearrange("t (r p) -> (t r) p", p=P)[0:P], 0, P),),
                        3: ((cv_dw[0].rearrange("t (r p) -> (t r) p", p=P)[P:TAPS * KC], 0, TAPS * KC - P), (c[0].rearrange("(r p) -> r p", p=P), 120, 128)),
                        4: ((dn_conv[0].rearrange("t (r p) -> (t r) p", p=P), 0, 72), (cv_b1[0].rearrange("(r p) -> r p", p=P), 72, 88),
                            (cv_dwb[0].rearrange("(r p) -> r p", p=P), 88, 96), (cv_ln_g[0].rearrange("(r p) -> r p", p=P), 96, 104),
                            (cv_ln_b[0].rearrange("(r p) -> r p", p=P), 104, 112), (cv_b2[0].rearrange("(r p) -> r p", p=P), 112, 120),
                            (c_ctx.rearrange("(r p) -> r p", p=P), 120, 128))}[t]
                for src, a, b in rows:
                    sp.dma_start(table[a:b, t, :], src).then_inc(table_in[t], 16)
            for t in range(NT):
                sp.dma_start(x_rows[:, t, :], x_src[t]).then_inc(x_in[t], 16)
            for j in range(4):
                load_mod(0, 0, j, first=True)
            with sp.Fori(1, MOD_FIRST) as i:
                for j in range(4):
                    load_mod(0, i, j)
            for s in range(stages):
                u0 = UNIT0[s]
                if is_ffn[s]:
                    if s == 0:
                        ffn_in_units(s, 0, first=True)
                        with sp.Fori(1, FC // 2) as i:
                            ffn_in_units(s, i)
                    else:
                        with sp.Fori(0, FC // 2) as i:
                            ffn_in_units(s, i)
                    wv = ffn_of(s)[1].rearrange("(k p) m -> p k m", p=P)
                    with sp.Fori(0, 2) as i:
                        for q in range(12):
                            a, b = FFN_THIRDS[q % 3]
                            load_unit(u0 + 2 * FC + 12 * i + q, q % RING, wv[:, a:b, ds(i * (4 * P) + (q // 3) * P, P)], b - a)
                            for n in out_mods(s, q):
                                load_mod(mod_out_groups[s] + n // 4, i * MOD_IN_FFN[s], n % 4)
                    if s in MOD_IN_FFN:
                        for j in range(4):
                            load_mod(mod_tail_group[s], 0, j)
                elif s == 1:
                    wv = cv_w1[0].rearrange("(k p) m -> p k m", p=P)
                    with sp.Fori(0, KC // 2) as i:
                        for j in range(4):
                            load_unit(u0 + 4 * i + j, j, wv[:, :, ds(i * (2 * P) + ((j % 2) * D + (j // 2) * P), P)])
                    wv = cv_w2[0].rearrange("(k p) m -> p k m", p=P)
                    with sp.Fori(0, KC // 4) as i:
                        for j in range(4):
                            load_unit(u0 + 2 * KC + 4 * i + j, j, wv[:, :, ds(i * (4 * P) + j * P, P)])
                elif s == 4:
                    wv = dn_w_in[0].rearrange("(k p) m -> p k m", p=P)
                    for j in range(RING):
                        load_unit(u0 + j, j, wv[:, :, j * P:(j + 1) * P])
                    sp.wait_ge(mean_ready, s)
                    sp.dma_start(w_ab[:, :, :], dn_w_in[0, :, DN_BLOCKS * P:].rearrange("(k p) m -> p k m", p=P)).then_inc(dn_small_in, 16)
                    sp.dma_start(dt_a[:, 0, :], dn_dt_bias[0].rearrange("d h -> (d h)").partition_broadcast(P)).then_inc(dn_small_in, 16)
                    sp.dma_start(dt_a[:, 1, :], dn_a_log[0].rearrange("d h -> (d h)").partition_broadcast(P)).then_inc(dn_small_in, 16)
                    sp.dma_start(norm_g[:, :], dn_norm_g.rearrange("a p -> p a")).then_inc(dn_small_in, 16)
                    with sp.Fori(1, DN_BLOCKS // 4) as i:
                        for j in range(4):
                            load_unit(u0 + 4 * i + j, j, wv[:, :, ds(i * (4 * P) + j * P, P)])
                    wv = dn_w_out[0].rearrange("(k p) m -> p k m", p=P)
                    for o in range(RING):
                        load_unit(u0 + DN_BLOCKS + o, o, wv[:, :, o * P:(o + 1) * P])
                    s_src = state_delta[0, 0].rearrange("d h k v -> k h d v")
                    s_dst = new_state[0, 0].rearrange("d h k v -> k h d v")
                    for h in range(H):
                        if h:
                            sp.wait_ge(state_out, 16 * h)
                        sp.wait_ge(head_done, h + 1)
                        sp.dma_start(s_old[:, :, :], s_src[:, h]).then_inc(state_in, 16)
                        sp.wait_ge(s_stored, 2 * h + 2)
                        sp.dma_start(s_dst[:, h], s_out[:, :, :]).then_inc(state_out, 16)
                    for o in range(RING, KC):
                        load_unit(u0 + DN_BLOCKS + o, o % RING, wv[:, :, o * P:(o + 1) * P])
            for t in range(NT):
                sp.wait_ge(rows_ready, 2 * (t + 1))
                sp.dma_start(y_dst[t], x_rows[:, t, :]).then_inc(out_done, 16)
            sp.wait_ge(out_done, 16 * NT)
            if stages > 4:
                sp.wait_ge(state_out, 16 * H)

        @block.gpsimd
        def _(pool):
            pool.memset(ident[:, :], 0.0).then_inc(consts, 1)
            pool.wait_ge(consts, 1)
            pool.memset(mean_w[:, :], 1.0 / D).then_inc(consts, 1)
            pool.wait_ge(consts, 2)
            pool.memset(eps[:, :], LN_EPS).then_inc(consts, 1)
            pool.wait_ge(consts, 3)
            pool.memset(table[96:P, 0:2, :], 0.0).then_inc(consts, 1)
            pool.wait_ge(consts, 4)
            pool.memset(r_sum[:, :], 0.0).then_inc(r_summed, 1)
            pool.wait_ge(r_summed, 1)
            pool.affine_select(out=ident[:, :], in_=ident[:, :], compare_op=ALU.not_equal, fill=1.0, base=0,
                               pattern=[[-1, P]], channel_multiplier=1).then_inc(consts, 2)

            def lower_h(k):
                for o in range(KC):
                    pool.wait_ge(h_hi_ready, KC * k + o + 1)
                    pool.tensor_tensor(h_lo[:, o], h_full[:, o % 4], h_hi[:, o].bitcast(F32), ALU.subtract).then_inc(h_lo_ready, 1)

            def conv_on_pool():
                for o in range(KC // 2):
                    out = conv[:, o, TP:T].rearrange("p (g w) -> p g w", w=GW)
                    for tap in range(1, TAPS):
                        n = (TAPS - 1) * o + tap - 1
                        pool.wait_ge(row_tap, n + o + 2)
                        if n:
                            pool.wait_ge(tap_g, n)
                        pool.tensor_tensor(out, out, row_prod[:, n % 4], ALU.add).then_inc(tap_g, 1)
                for o in range(KC):
                    pool.wait_ge(conv_hi, o + 1)
                    pool.tensor_tensor(h_lo[:, o], conv_full[:, o % 4], h_hi[:, o].bitcast(F32), ALU.subtract).then_inc(conv_lo, 1)

            def delta_on_pool():
                done = [0]

                def each(instruction):
                    done[0] += 1
                    instruction.then_inc(dn_consts, 1)
                    pool.wait_ge(dn_consts, done[0])

                each(pool.memset(ones[:, :], 1.0))
                each(pool.memset(one_hot[:, :], 0.0))
                each(pool.memset(one_hot[:, 2 * H - 1:2 * H], 1.0))
                each(pool.memset(q_scale[:, 0:1], 1.0))
                each(pool.memset(q_scale[:, 1:2], 1e-6))
                each(pool.memset(q_scale[0:H, 0:1], float(P)))
                each(pool.memset(q_scale[0:H, 1:2], P * 1e-6))
                each(pool.memset(tri[:, :, :], 1.0))
                each(pool.memset(never[:, :, :], 0.0))
                for d in range(2):
                    sign = 1 - 2 * d
                    for m, fill in ((tri, 0.0), (never, -1e30)):
                        each(pool.affine_select(out=m[:, d], in_=m[:, d], compare_op=ALU.is_ge, fill=fill, base=0,
                                                pattern=[[sign, P]], channel_multiplier=-sign))
                each(pool.memset(masks[:, :, :], 0.0))
                for n in range(LEVELS):
                    b = 1 << n
                    for up in range(2):
                        part = masks[:, 2 * n + up].rearrange("p (a c) -> p a c", c=2 * b)[:, :, up * b:(up + 1) * b]
                        first = (1 - up) * b
                        pairs = P // (2 * b)
                        each(pool.memset(part, 1.0))
                        each(pool.affine_select(out=part, in_=part, compare_op=ALU.is_ge, fill=0.0, base=-first,
                                                pattern=[[-2 * b, pairs], [0, b]], channel_multiplier=1))
                        each(pool.affine_select(out=part, in_=part, compare_op=ALU.is_ge, fill=0.0, base=first + b - 1,
                                                pattern=[[2 * b, pairs], [0, b]], channel_multiplier=-1))
                assert done[0] == DN_CONSTS
                pool.wait_ge(gate_a, GATE_A_BETA)
                pool.wait_ge(v_stored, H)
                with pool.Fori(0, H) as h:
                    pool.wait_ge(head_done, h + 1)
                    for m in (inv, inv_t):
                        for d in range(2):
                            i3 = ident[:, :].unsqueeze(1).to_broadcast([P, NT, P])
                            last = pool.tensor_tensor(m[:, d], i3, i3, ALU.mult)
                    last.then_inc(inv_begun, 1)
                    pool.wait_ge(inv_begun, h + 1)
                    for d in range(2):
                        for t in range(NT):
                            last = pool.tensor_tensor(v_beta[:, d, t:t + 1], v_tok[:, t, ds(h, 1)],
                                                      beta[:, t, ds(h + d * H, 1)].unsqueeze(2).to_broadcast([P, 1, P]), ALU.mult)
                    last.then_inc(v_beta_ready, 1)
                    pool.wait_ge(v_beta_ready, h + 1)
                for o in range(KC):
                    pool.wait_ge(o_hi, o + 1)
                    pool.tensor_tensor(h_lo[:, o], h_full[:, o % 4], h_hi[:, o].bitcast(F32), ALU.subtract).then_inc(o_lo, 1)
                pool.wait_ge(o_gated, 2 * H)

            lower_h(0)
            for s in range(stages):
                if s == 1:
                    pool.wait_ge(mean_ready, s)
                    pool.memset(glu_seq[:, :, :], 0.0).then_inc(pads_ready, 1)
                    pool.wait_ge(pads_ready, 1)
                    pool.memset(glu_row[:, :, :, :], 0.0).then_inc(pads_ready, 1)
                    pool.wait_ge(pads_ready, 2)
                if s:
                    pool.wait_ge(mean_ready, s)
                    pool.memset(r_sum[:, :], 0.0).then_inc(r_summed, 1)
                if s == 4:
                    delta_on_pool()
                pool.wait_ge(x_ready, KC * (s + 1))
                pool.tensor_scalar(r[:, :, :], x[:, :, :], ALPHA, 0.0, ALU.mult, ALU.add).then_inc(r_scaled, 1)
                if s == 1:
                    conv_on_pool()
                for o in range(KC):
                    pool.wait_ge(r_ready, KC * s + o + 2)
                    pool.wait_ge(r_summed, (KC + 1) * s + o + 1)
                    pool.tensor_tensor(r_sum[:, :], r_sum[:, :], r[:, o], ALU.add).then_inc(r_summed, 1)
                if s + 1 < stages:
                    lower_h(s + 1)

        @block.scalar
        def _(act):
            def upper_w(u, slot, lap):
                if not (isinstance(u, int) and u < RING):
                    act.wait_ge(unit_used, u - RING + 1)
                act.wait_ge(w_in[slot], lap * 16)
                act.activation(w_hi[:, slot], w_raw[:, slot], ACT.Copy).then_inc(w_hi_ready, 1)

            def upper_h(k, o):
                act.wait_ge(h_ready, KC * k + o + 1)
                act.activation(h_hi[:, o], h_full[:, o % 4], ACT.Copy).then_inc(h_hi_ready, 1)

            def delta_on_scalar(u0):
                with act.Fori(0, 2 * H // 4) as i:
                    for j in range(4):
                        act.wait_ge(lin_step, 20 * i + 5 * (j + 1))
                        act.activation(qk[:, ds(4 * i + j, 1)], lin[:, j % 2].unsqueeze(1), ACT.Silu).then_inc(silu_done, 1)
                        upper_w(u0 + 4 * i + j + RING, j, i + (u0 // RING + 2))
                for b in range(H + 1):
                    if b < H:
                        n = 2 * H + b
                        act.wait_ge(lin_step, 5 * (n + 1))
                        if b >= 2:
                            act.wait_ge(v_turned, b - 1)
                        act.activation(v_silu[:, b % 2], lin[:, n % 2], ACT.Silu).then_inc(silu_done, 1)
                        upper_w(u0 + n + RING, n % RING, (u0 + n) // RING + 2)
                    if b:
                        act.wait_ge(v_turned, b)
                        act.activation(v_tok[:, :, b - 1], bank[6 + (b - 1) % 2][:, 0:T].rearrange("p (t c) -> p t c", c=P),
                                       ACT.Copy).then_inc(v_stored, 1)
                act.wait_ge(dn_small_in, 64)
                act.activation(w_ab_hi[:, :, :], w_ab[:, :, :], ACT.Copy).then_inc(w_ab_ready, 1)
                for b in range(2 * H):
                    if b >= 4:
                        act.wait_ge(qk_summed, b - 3)
                    act.activation(square[:, b % 4], qk[:, b], ACT.Square).then_inc(qk_squared, 1)
                act.wait_ge(dn_consts, DN_CONSTS)
                act.wait_ge(qk_summed, 2 * H)
                act.activation(qk_norm[:, :], bank[4][0:2 * H, 0:T], ACT.Sqrt, scale=q_scale[:, 0:1], bias=q_scale[:, 1:2]).then_inc(qk_norm_ready, 1)
                act.activation(exp_a[:, 0, :], dt_a[:, 1, :], ACT.Exp).then_inc(gate_a, 1)
                act.wait_ge(gate_v, 2)
                act.activation(soft[:, :, :], pre[:, :, :], ACT.Abs).then_inc(gate_a, 1)
                act.wait_ge(gate_a, 2)
                act.activation(soft[:, :, :], soft[:, :, :], ACT.Exp, scale=-1.0).then_inc(gate_a, 1)
                act.wait_ge(gate_a, 3)
                act.activation(soft[:, :, :], soft[:, :, :], ACT.Ln, bias=1.0).then_inc(gate_a, 1)
                act.activation(beta[:, :, :], ab[:, :, 2 * H:4 * H], ACT.Sigmoid).then_inc(gate_a, 1)
                with act.Fori(0, H // 4) as i:
                    for j in range(4):
                        act.wait_ge(unit_used, u0 + 3 * H + 4 * i + j + 1)
                        act.activation(z[:, ds(4 * i + j, 1)], bank[j][:, 0:T].unsqueeze(1), ACT.Silu).then_inc(silu_done, 1)
                        upper_w(u0 + 3 * H + 4 * i + j + RING, j, i + ((u0 + 3 * H) // RING + 2))
                act.wait_ge(gate_v, 8)
                act.activation(end_decay[:, :, :], end_decay[:, :, :], ACT.Exp).then_inc(gate_a, 1)
                act.activation(g_decay[:, :, :], g_col[:, :, :], ACT.Exp).then_inc(gate_a, 1)
                act.activation(tot_decay[:, :, :], tot[:, :, :], ACT.Exp).then_inc(gate_a, 1)
                act.activation(begun[:, 3:4], eps[:, :], ACT.Copy).then_inc(head_done, 1)
                with act.Fori(0, H) as h:
                    for d in range(2):
                        act.wait_ge(diff_ready, 2 * h + d + 1)
                        act.activation(decay[:, d], decay[:, d], ACT.Exp).then_inc(decay_ready, 1)
                    for d in range(2):
                        act.activation(q_decay[:, d, TP:T], bank[2 + d][:, TP:T], ACT.Exp).then_inc(q_exp_ready, 1)
                    for n in range(1, LEVELS):
                        for d in range(2):
                            act.wait_ge(p_ready, h * (2 * LEVELS) + 2 * n + d + 1)
                            act.activation(step_p[:, d], bank[d][:, 0:T].rearrange("p (t c) -> p t c", c=P), ACT.Copy).then_inc(p_copied, 1)
                    for k in range(NT):
                        for d in range(2):
                            act.wait_ge(u_ready, 6 * h + 2 * k + d + 1)
                            if k:
                                act.wait_ge(o_added, 6 * h + 2 * (k - 1) + d + 1)
                            act.activation(u_sb[:, d], bank[2 + d][:, 0:P], ACT.Copy).then_inc(u_copied, 1)
                        if k == 0:
                            act.wait_ge(state_in, 16 * h + 16)
                            for d in range(2):
                                act.wait_ge(s_added, 4 * h + d + 1)
                                act.activation(s_out[:, d], bank[4 + d][:, 0:P], ACT.Copy).then_inc(s_stored, 1)
                    act.wait_ge(o_added, 6 * h + 6)
                    act.activation(o_all[:, ds(h, 1)], bank[6][:, 0:T].unsqueeze(1), ACT.Copy).then_inc(head_done, 1)
                act.wait_ge(head_done, H + 1)
                for h in range(H):
                    if h >= 4:
                        act.wait_ge(o_summed, h - 3)
                    act.activation(square[:, h % 4], o_all[:, h], ACT.Square).then_inc(o_squared, 1)
                act.wait_ge(o_summed, H)
                act.activation(qk_norm[0:H, :], bank[4][0:H, 0:T], ACT.Sqrt, scale=1.0 / P, bias=eps[0:H, :]).then_inc(o_norm_ready, 1)
                for o in range(KC):
                    act.wait_ge(o_gated, 2 * o + 2)
                    act.activation(h_hi[:, o], h_full[:, o % 4], ACT.Copy).then_inc(o_hi, 1)
                for o in range(KC):
                    u = u0 + DN_BLOCKS + o + RING
                    if u < LAST_UNIT:
                        upper_w(u, o % RING, u // RING + 1)

            act.wait_ge(table_out, 5)
            act.activation(cond[:, :, 0], params[:, COL_CCTX:COL_CCTX + KC], ACT.Silu).then_inc(cond_ready, 1)
            act.activation(cond[:, :, 1], params[:, COL_C:COL_C + KC], ACT.Silu).then_inc(cond_ready, 1)
            for j in range(RING):
                upper_w(j, j, 1)
            for o in range(KC):
                upper_h(0, o)

            for s in range(stages):
                u0 = UNIT0[s]
                if is_ffn[s]:
                    f0 = FC * ffns[s]
                    with act.Fori(0, FC // 2) as i:
                        for q in range(2):
                            act.wait_ge(unit_used, u0 + 4 * i + 2 * q + 2)
                            act.activation(silu_g[:, q], bank[2 + q][:, 0:T], ACT.Silu).then_inc(silu_ready, 1)
                            act.wait_ge(act_ready, f0 + 2 * i + q + 2)
                            act.activation(act_hi[:, ds(2 * i + q, 1)], act_full[:, ds(q, 1)], ACT.Copy).then_inc(act_hi_ready, 1)
                            for j in range(2):
                                upper_w(u0 + 4 * i + 2 * q + j + RING, 2 * q + j, i + (u0 // RING + 2))
                    if s == stages - 1:
                        for q in range(3 * KC - RING):
                            upper_w(u0 + 2 * FC + q + RING, q % RING, (u0 + 2 * FC + q) // RING + 2)
                    else:
                        with act.Fori(0, 2) as i:
                            for q in range(12):
                                upper_w(u0 + 2 * FC + 12 * i + q + RING, q % RING,
                                        i * 3 + ((u0 + 2 * FC + q) // RING + 2))
                elif s == 1:
                    for o in range(KC):
                        act.wait_ge(unit_used, u0 + 2 * o + 2)
                        act.activation(sigm[:, o % 2], bank[2 + o % 2][:, 0:T], ACT.Sigmoid,
                                       bias=params[:, COL_B1 + KC + o:COL_B1 + KC + o + 1]).then_inc(sigm_ready, 1)
                        c = o // 2
                        act.wait_ge(glu_ready, c + 2)
                        for tap in (range(16), range(16, TAPS))[o % 2]:
                            n = (TAPS - 1) * c + tap - 1
                            src = glu_row[:, c, :, tap:tap + GW]
                            w = params[:, COL_DW + tap * KC + c:COL_DW + tap * KC + c + 1]
                            if tap == 0:
                                act.activation(conv[:, c, TP:T].rearrange("p (g w) -> p g w", w=GW), src, ACT.Identity, scale=w,
                                               bias=params[:, COL_DWB + c:COL_DWB + c + 1]).then_inc(row_tap, 1)
                            else:
                                if n > 3:
                                    act.wait_ge(tap_g, n - 3)
                                act.activation(row_prod[:, n % 4], src, ACT.Copy, scale=w).then_inc(row_tap, 1)
                            if tap in (4, 12, 20, 28):
                                u = u0 + 2 * o + (tap in (12, 28)) + RING
                                upper_w(u, u % RING, u // RING + 1)
                    for o in range(KC):
                        act.wait_ge(conv_centred, o + 1)
                        if o >= 4:
                            act.wait_ge(conv_var, o - 3)
                        act.activation(square[:, o % 4], conv[:, o], ACT.Square).then_inc(conv_squared, 1)
                    act.wait_ge(conv_var, KC)
                    act.activation(dev[:, :], var_ps[:, 0:T], ACT.Sqrt, bias=eps[:, :]).then_inc(conv_dev, 1)
                    for o in range(KC):
                        act.wait_ge(conv_normed, o + 1)
                        if o >= 4:
                            act.wait_ge(conv_lo, o - 3)
                        act.activation(conv_full[:, o % 4], conv[:, o], ACT.Silu, scale=params[:, COL_CLNG + o:COL_CLNG + o + 1],
                                       bias=params[:, COL_CLNB + o:COL_CLNB + o + 1]).then_inc(conv_act, 1)
                        act.wait_ge(conv_act, o + 1)
                        act.activation(h_hi[:, o], conv_full[:, o % 4], ACT.Copy).then_inc(conv_hi, 1)
                    for o in range(KC):
                        u = u0 + 2 * KC + o
                        act.wait_ge(unit_used, u + 1)
                        act.activation(y_biased[:, o % 2], bank[o % 2][:, 0:T], ACT.Identity,
                                       bias=params[:, COL_B2 + o:COL_B2 + o + 1]).then_inc(y_ready, 1)
                        if u + RING < LAST_UNIT:
                            upper_w(u + RING, o % RING, (u + RING) // RING + 1)
                elif s == 4:
                    delta_on_scalar(u0)
                for o in range(KC):
                    act.wait_ge(centred, KC * s + o + 1)
                    if o >= 4:
                        act.wait_ge(var_added, KC * s + o - 3)
                    act.activation(square[:, o % 4], r[:, o], ACT.Square).then_inc(squared, 1)
                act.wait_ge(var_added, KC * (s + 1))
                act.activation(dev[:, :], var_ps[:, 0:T], ACT.Sqrt, bias=eps[:, :]).then_inc(dev_ready, 1)
                for o in range(KC + 1):
                    if o < KC:
                        act.wait_ge(normed, KC * s + o + 1)
                        n = (s // 3 * 3 + s % 3) * KC + o
                        act.activation(x[:, o], r[:, o], ACT.Identity, scale=params[:, COL_LNG + n:COL_LNG + n + 1],
                                       bias=params[:, COL_LNB + n:COL_LNB + n + 1]).then_inc(x_ready, 1)
                    if o and s + 1 < stages:
                        upper_h(s + 1, o - 1)

        @block.vector
        def _(dve):
            def lower_w(u, slot):
                dve.wait_ge(w_hi_ready, u + 1)
                dve.tensor_tensor(w_lo[:, slot], w_raw[:, slot], w_hi[:, slot].bitcast(F32), ALU.subtract).then_inc(w_lo_ready, 1)

            def store_mod(g0, i):
                dve.wait_ge(mod_used, 4 * i + 4 * (g0 + 1))
                dve.tensor_tensor(mod[:, ds(4 * i + 4 * g0, 4), :], mod_out[:, :, :],
                                  params[:, ds(4 * i + (COL_BMOD[g0 // 18] + g0 % 18 * 4), 4)].unsqueeze(2).to_broadcast([P, 4, 2]),
                                  ALU.add).then_inc(mod_ready, 1)

            def scale_of(k):
                dve.wait_ge(mod_ready, mod_groups[k])
                dve.tensor_scalar(scale1[:, :, :], mod[:, mod_col(k) + KC:mod_col(k) + 2 * KC, :], 1.0, None,
                                  ALU.add).then_inc(small, 1)

            def modulate(k, o):
                if KC * k + o >= 4:
                    dve.wait_ge(h_lo_ready, KC * k + o - 3)
                dve.wait_ge(x_ready, KC * k + o + 1)
                dve.wait_ge(small, 2 * k + 1)
                for g, a, b in GROUPS:
                    last = dve.tensor_scalar(h_full[:, o % 4, a:b], x[:, o, a:b], scale1[:, o, g:g + 1],
                                             mod[:, mod_col(k) + o, g:g + 1], ALU.mult, ALU.add)
                last.then_inc(h_ready, 1)

            def conv_on_vector(u0):
                dve.wait_ge(pads_ready, 2)
                taps = 0
                for o in range(KC):
                    dve.wait_ge(sigm_ready, o + 1)
                    bias = params[:, COL_B1 + o:COL_B1 + o + 1]
                    dve.scalar_tensor_tensor(glu_seq[:, o, HALF:HALF + TP], bank[o % 2][:, 0:TP], bias, sigm[:, o % 2, 0:TP],
                                             ALU.add, ALU.mult)
                    if o < KC // 2:
                        g3 = lambda ap: ap.rearrange("p (g w) -> p g w", w=GW)
                        dve.scalar_tensor_tensor(glu_row[:, o, :, HALF:HALF + GW], g3(bank[o % 2][:, TP:T]), bias,
                                                 g3(sigm[:, o % 2, TP:T]), ALU.add, ALU.mult).then_inc(glu_ready, 1)
                    else:
                        dve.scalar_tensor_tensor(glu_col[:, o - KC // 2], bank[o % 2][:, TP:T], bias, sigm[:, o % 2, TP:T],
                                                 ALU.add, ALU.mult).then_inc(glu_ready, 1)
                    dve.wait_ge(glu_ready, o + 2)
                    for tap in range(TAPS):
                        w = params[:, COL_DW + tap * KC + o:COL_DW + tap * KC + o + 1]
                        dwb = params[:, COL_DWB + o:COL_DWB + o + 1]
                        src, out = glu_seq[:, o, tap:tap + TP], conv[:, o, 0:TP]
                        if tap == 0:
                            dve.tensor_scalar(out, src, w, dwb, ALU.mult, ALU.add).then_inc(tap_v, 1)
                        else:
                            dve.wait_ge(tap_v, taps)
                            dve.scalar_tensor_tensor(out, src, w, out, ALU.mult, ALU.add).then_inc(tap_v, 1)
                        taps += 1
                        if tap in (7, 23):
                            u = u0 + 2 * o + (tap > 7) + RING
                            lower_w(u, u % RING)
                    if o >= KC // 2:
                        offsets = [0] + [d for d in range(1 - GR, GR) if d]
                        for d in offsets:
                            tap = d + HALF
                            w = params[:, COL_DW + tap * KC + o:COL_DW + tap * KC + o + 1]
                            a, b = max(0, -d), min(GR, GR - d)
                            out = conv[:, o, TP + a * GW:TP + b * GW]
                            src = glu_col[:, o - KC // 2, (a + d) * GW:(b + d) * GW]
                            if d == 0:
                                dve.tensor_scalar(out, src, w, params[:, COL_DWB + o:COL_DWB + o + 1], ALU.mult, ALU.add).then_inc(tap_v, 1)
                            else:
                                dve.wait_ge(tap_v, taps)
                                dve.scalar_tensor_tensor(out, src, w, out, ALU.mult, ALU.add).then_inc(tap_v, 1)
                            taps += 1
                dve.wait_ge(conv_mean, 1)
                for o in range(KC):
                    dve.tensor_tensor(conv[:, o], conv[:, o], mean_ps[:, 0:T], ALU.subtract).then_inc(conv_centred, 1)
                dve.wait_ge(conv_dev, 1)
                dve.reciprocal(rstd[:, :], dev[:, :]).then_inc(conv_rstd, 1)
                dve.wait_ge(conv_rstd, 1)
                for o in range(KC):
                    dve.tensor_tensor(conv[:, o], conv[:, o], rstd[:, :], ALU.mult).then_inc(conv_normed, 1)

            def delta_on_vector(u0):
                with dve.Fori(0, 3 * H // 4) as i:
                    for j in range(4):
                        dve.wait_ge(unit_used, u0 + 4 * i + j + 1)
                        w = [params[:, ds(4 * i + (COL_DNCONV + tap * 3 * H + j), 1)] for tap in range(3)]
                        out, ps, n = lin[:, j % 2], bank[j], 20 * i + 5 * j
                        dve.tensor_scalar(out, ps[:, 0:T], w[1], None, ALU.mult).then_inc(lin_step, 1)
                        dve.wait_ge(lin_step, n + 1)
                        for _, a, b in GROUPS:
                            dve.scalar_tensor_tensor(out[:, a + 1:b], ps[:, a:b - 1], w[0], out[:, a + 1:b], ALU.mult, ALU.add).then_inc(lin_step, 1)
                        for g, a, b in GROUPS:
                            dve.wait_ge(lin_step, n + 2 + g)
                            dve.scalar_tensor_tensor(out[:, a:b - 1], ps[:, a + 1:b], w[2], out[:, a:b - 1], ALU.mult, ALU.add).then_inc(lin_step, 1)
                        lower_w(u0 + 4 * i + j + RING, j)
                        dve.wait_ge(silu_done, 4 * i + j + 1)
                dve.wait_ge(w_ab_ready, 1)
                dve.tensor_tensor(w_ab_lo[:, :, :], w_ab[:, :, :], w_ab_hi[:, :, :].bitcast(F32), ALU.subtract).then_inc(w_ab_ready, 1)
                dve.wait_ge(qk_norm_ready, 1)
                dve.reciprocal(qk_rnorm[:, :], qk_norm[:, :]).then_inc(qk_norm_ready, 1)
                dve.wait_ge(ab_ready, 1)
                dve.tensor_copy(ab[:, :, :], bank[5][:, 0:12 * H].rearrange("p (t c) -> p t c", t=NT)).then_inc(gate_v, 1)
                dve.wait_ge(gate_v, 1)
                dve.tensor_tensor(pre[:, :, :], ab[:, :, 0:2 * H], dt_a[:, 0:1, :].to_broadcast([P, NT, 2 * H]), ALU.add).then_inc(gate_v, 1)
                dve.wait_ge(gate_v, 2)
                dve.tensor_scalar(pos[:, :, :], pre[:, :, :], 0.0, None, ALU.max).then_inc(gate_v, 1)
                dve.wait_ge(gate_v, 3)
                dve.wait_ge(gate_a, 4)
                dve.tensor_tensor(pos[:, :, :], pos[:, :, :], soft[:, :, :], ALU.add).then_inc(gate_v, 1)
                dve.wait_ge(gate_v, 4)
                dve.scalar_tensor_tensor(log_a[:, :, :], pos[:, :, :], -1.0, exp_a[:, 0:1, :].to_broadcast([P, NT, 2 * H]),
                                         ALU.mult, ALU.mult).then_inc(gate_v, 1)
                with dve.Fori(0, H // 4) as i:
                    for j in range(4):
                        lower_w(u0 + 3 * H + 4 * i + j + RING, j)
                dve.wait_ge(gate_t, 1)
                dve.tensor_copy(g_col[:, :, :], bank[5][:, 0:6 * H].rearrange("p (t c) -> p t c", t=NT)).then_inc(gate_v, 1)
                dve.tensor_copy(tot[:, :, :], bank[6][:, 0:6 * H].rearrange("p (t c) -> p t c", t=NT)).then_inc(gate_v, 1)
                dve.wait_ge(gate_v, 7)
                dve.tensor_tensor(end_decay[:, :, :], tot[:, :, :], g_col[:, :, :], ALU.subtract).then_inc(gate_v, 1)
                dve.wait_ge(gate_t, 2)
                for n in range(4):
                    dve.tensor_copy(rows[:, n], bank[n][0:H, 0:T]).then_inc(gate_v, 1)
                dve.wait_ge(gate_a, 8)
                dve.scalar_tensor_tensor(minus_beta_g[:, :, :], beta[:, :, :], -1.0, g_decay[:, :, :], ALU.mult, ALU.mult).then_inc(gate_v, 1)
                dve.wait_ge(gate_v, 13)
                dve.wait_ge(dn_consts, DN_CONSTS)
                tiles = lambda ap: ap[:, 0:T].rearrange("p (t c) -> p t c", c=P)
                with dve.Fori(0, H) as h:
                    dve.wait_ge(head_done, h + 1)
                    dve.tensor_copy(sel_k[:, :].unsqueeze(1), ident[0:2 * H, ds(h + H, 1)].unsqueeze(1).to_broadcast([2 * H, 1, P]))
                    dve.tensor_copy(sel_q[:, :].unsqueeze(1), ident[0:2 * H, ds(h, 1)].unsqueeze(1).to_broadcast([2 * H, 1, P]))
                    dve.tensor_copy(sel_h[:, :].unsqueeze(1), ident[0:H, ds(h, 1)].unsqueeze(1).to_broadcast([H, 1, P])).then_inc(sel_ready, 1)
                    dve.wait_ge(norm_spread, h + 1)
                    dve.tensor_tensor(k_head[:, :].unsqueeze(1), qk[:, ds(h + H, 1)], bank[0][:, 0:T].unsqueeze(1), ALU.mult).then_inc(qk_ready, 1)
                    dve.tensor_tensor(q_head[:, :].unsqueeze(1), qk[:, ds(h, 1)], bank[1][:, 0:T].unsqueeze(1), ALU.mult).then_inc(qk_ready, 1)
                    dve.wait_ge(rows_spread, h + 1)
                    for d in range(2):
                        for t in range(NT):
                            last = dve.scalar_tensor_tensor(decay[:, d, t], bank[2 + d][:, t * P:(t + 1) * P], g_col[:, t, ds(h + d * H, 1)],
                                                            never[:, d], ALU.subtract, ALU.add)
                        last.then_inc(diff_ready, 1)
                    dve.wait_ge(k_turned, h + 1)
                    for d in range(2):
                        for k in range(2):
                            t = SCAN[d][k]
                            last = dve.tensor_scalar(k_decay[:, d, k], bank[0][:, t * P:(t + 1) * P], end_decay[:, t, ds(h + d * H, 1)],
                                                     None, ALU.mult)
                    last.then_inc(k_decay_ready, 1)
                    dve.wait_ge(kk_ready, h + 1)
                    for d in range(2):
                        dve.wait_ge(decay_ready, 2 * h + d + 1)
                        dve.tensor_tensor(qk_decay[:, d], decay[:, d], tiles(bank[7]), ALU.mult)
                        dve.scalar_tensor_tensor(decay[:, d], decay[:, d], -1.0, tiles(bank[6]), ALU.mult, ALU.mult).then_inc(a_step, 1)
                    for d in range(2):
                        dve.wait_ge(a_step, 4 * h + d + 1)
                        dve.tensor_tensor(decay[:, d], decay[:, d], tiles(bank[4 + d]), ALU.mult).then_inc(a_step, 1)
                    for d in range(2):
                        dve.wait_ge(q_exp_ready, 2 * h + d + 1)
                        dve.tensor_tensor(q_decay[:, d, TP:T], q_decay[:, d, TP:T], q_head[:, TP:T], ALU.mult).then_inc(q_decay_ready, 1)
                    for n in range(LEVELS):
                        for d in range(2):
                            here = masks[:, 2 * n + d].unsqueeze(1).to_broadcast([P, NT, P])
                            there = masks[:, 2 * n + 1 - d].unsqueeze(1).to_broadcast([P, NT, P])
                            if n == 0:
                                dve.wait_ge(inv_begun, h + 1)
                                dve.wait_ge(a_step, 4 * h + 2 + d + 1)
                                dve.wait_ge(p_ready, h * (2 * LEVELS) + d + 1)
                                dve.memset(carrier[:, 2 * n + d:2 * n + d + 1], 0.0)
                                dve.copy_predicated(inv_t[:, d], there, decay[:, d])
                                dve.copy_predicated(inv[:, d], here, tiles(bank[d])).then_inc(t_joined, 1)
                            else:
                                dve.wait_ge(t_ready, h * (2 * (LEVELS - 1)) + 2 * (n - 1) + d + 1)
                                dve.memset(carrier[:, 2 * n + d:2 * n + d + 1], 0.0)
                                last = dve.copy_predicated(inv_t[:, d], there, tiles(bank[4 + d]))
                                if n < LEVELS - 1:
                                    last = dve.copy_predicated(inv[:, d], here, tiles(bank[2 + d]))
                                last.then_inc(t_joined, 1)
                    dve.wait_ge(v_beta_ready, h + 1)
                    for k in (1, 2):
                        for d in range(2):
                            t = SCAN[d][k]
                            dve.wait_ge(ks_ready, 4 * h + 2 * (k - 1) + d + 1)
                            dve.scalar_tensor_tensor(v_beta[:, d, t], bank[d][:, 0:P], minus_beta_g[:, t, ds(h + d * H, 1)],
                                                     v_beta[:, d, t], ALU.mult, ALU.add).then_inc(x_set, 1)
                        if k == 1:
                            for d in range(2):
                                dve.wait_ge(s_added, 4 * h + 2 + d + 1)
                                dve.scalar_tensor_tensor(s_new[:, d], s_old[:, d], tot_decay[:, SCAN[d][1], ds(h + d * H, 1)],
                                                         bank[4 + d][:, 0:P], ALU.mult, ALU.add).then_inc(s_updated, 1)
                dve.wait_ge(head_done, H + 1)
                dve.wait_ge(o_norm_ready, 1)
                dve.reciprocal(qk_rnorm[0:H, :], qk_norm[0:H, :]).then_inc(o_rnorm_ready, 1)
                for h in range(H):
                    dve.wait_ge(o_squared, h + 1)
                    dve.scalar_tensor_tensor(o_all[:, h], o_all[:, h], norm_g[:, :], z[:, h], ALU.mult, ALU.mult).then_inc(o_gated, 1)
                    dve.wait_ge(o_gated, 2 * h + 1)
                    dve.wait_ge(o_spread, h + 1)
                    if h >= 4:
                        dve.wait_ge(o_lo, h - 3)
                    dve.tensor_tensor(h_full[:, h % 4], o_all[:, h], bank[h % 2][:, 0:T], ALU.mult).then_inc(o_gated, 1)

            for n, started in enumerate((act_ready, r_ready, glu_ready)):
                dve.memset(begun[:, n:n + 1], 0.0).then_inc(started, 1)
            for t in range(5):
                dve.wait_ge(turned, t + 1)
                dve.tensor_copy(params[:, t * P:(t + 1) * P], bank[t % 4][:, 0:P]).then_inc(table_out, 1)
            for o in range(KC):
                dve.wait_ge(turned, 5 + o + 1)
                dve.tensor_copy(x[:, o], bank[o % 2][:, 0:T]).then_inc(x_ready, 1)
            with dve.Fori(0, MOD_FIRST) as i:
                store_mod(0, i)
            for j in range(RING):
                lower_w(j, j)
            scale_of(0)
            for o in range(KC):
                modulate(0, o)

            for s in range(stages):
                u0 = UNIT0[s]
                if is_ffn[s]:
                    f0 = FC * ffns[s]
                    with dve.Fori(0, FC // 2) as i:
                        for q in range(2):
                            dve.wait_ge(silu_ready, f0 + 2 * i + q + 1)
                            dve.tensor_tensor(act_full[:, q], silu_g[:, q], bank[q][:, 0:T], ALU.mult).then_inc(act_ready, 1)
                            dve.wait_ge(act_hi_ready, f0 + 2 * i + q + 1)
                            dve.tensor_tensor(act_lo[:, ds(2 * i + q, 1)], act_full[:, ds(q, 1)],
                                              act_hi[:, ds(2 * i + q, 1)].bitcast(F32), ALU.subtract).then_inc(act_lo_ready, 1)
                            for j in range(2):
                                lower_w(u0 + 4 * i + 2 * q + j + RING, 2 * q + j)
                        if s in MOD_IN_FFN:
                            store_mod(mod_groups[s], i)
                elif s == 1:
                    conv_on_vector(u0)
                elif s == 4:
                    delta_on_vector(u0)
                dve.wait_ge(mod_ready, mod_groups[s] + (2 if s == 0 else 0))
                dve.tensor_scalar(gate[:, :, :], mod[:, mod_col(s) + 2 * KC:mod_col(s) + 3 * KC, :],
                                  0.5 if is_ffn[s] else 1.0, None, ALU.mult).then_inc(small, 1)
                dve.wait_ge(small, 2 * s + 2)
                dve.wait_ge(r_scaled, s + 1)

                def add_gated(done, count, o, ps):
                    dve.wait_ge(done, count)
                    for g, a, b in GROUPS:
                        last = dve.scalar_tensor_tensor(r[:, ds(o, 1), a:b], ps[:, a:b].unsqueeze(1), gate[:, ds(o, 1), g:g + 1],
                                                        r[:, ds(o, 1), a:b], ALU.mult, ALU.add)
                    last.then_inc(r_ready, 1)

                if is_ffn[s]:
                    v0 = u0 + 2 * FC
                    def out_body(i, units):
                        for q in range(12):
                            if q % 3 == 2:
                                add_gated(unit_used, v0 + 12 * i + q + 1, 4 * i + q // 3, bank[(q // 3) % 2])
                            if q < units:
                                lower_w(v0 + 12 * i + q + RING, q % RING)
                            for n in out_mods(s, q):
                                if n % 4 == 3:
                                    store_mod(mod_out_groups[s] + n // 4, i * MOD_IN_FFN[s])
                    if s == stages - 1:
                        out_body(0, 12)
                        out_body(1, 12 - RING)
                    else:
                        with dve.Fori(0, 2) as i:
                            out_body(i, 12)

                elif s == 1:
                    for o in range(KC):
                        add_gated(y_ready, o + 1, o, y_biased[:, o % 2])
                        if u0 + 2 * KC + o + RING < LAST_UNIT:
                            lower_w(u0 + 2 * KC + o + RING, o % RING)
                elif s == 4:
                    for o in range(KC):
                        add_gated(unit_used, u0 + DN_BLOCKS + o + 1, o, bank[2 + o % 2])
                        if u0 + DN_BLOCKS + o + RING < LAST_UNIT:
                            lower_w(u0 + DN_BLOCKS + o + RING, o % RING)
                if s in MOD_IN_FFN:
                    store_mod(mod_tail_group[s], 0)
                dve.wait_ge(mean_ready, s + 1)
                for o in range(KC):
                    dve.tensor_tensor(r[:, o], r[:, o], mean_ps[:, 0:T], ALU.subtract).then_inc(centred, 1)
                dve.wait_ge(dev_ready, s + 1)
                dve.reciprocal(rstd[:, :], dev[:, :]).then_inc(rstd_ready, 1)
                if s + 1 < stages:
                    scale_of(s + 1)
                dve.wait_ge(rstd_ready, s + 1)
                dve.wait_ge(squared, KC * (s + 1))
                for o in range(KC + 2):
                    if o < KC:
                        dve.tensor_tensor(r[:, o], r[:, o], rstd[:, :], ALU.mult).then_inc(normed, 1)
                    if o >= 2 and s + 1 < stages:
                        modulate(s + 1, o - 2)

            for t in range(NT):
                for half in range(2):
                    dve.wait_ge(turned, 5 + KC + 2 * t + half + 1)
                    dve.tensor_copy(x_rows[:, t, 512 * half:512 * half + 512], bank[(2 * t + half) % 4][:, :]).then_inc(rows_ready, 1)

        @block.tensor
        def _(pe):
            def split_product(ps, w_slot, k, a_hi, a_lo, start, stop):
                pe.matmul(ps, w_hi[:, w_slot, k], a_hi, start=start, stop=False)
                pe.matmul(ps, w_hi[:, w_slot, k], a_lo, start=False, stop=False)
                return pe.matmul(ps, w_lo[:, w_slot, k], a_hi, start=False, stop=stop)

            def unit(u, slot, ps, hi, lo, chunks, first=True, last=True):
                pe.wait_ge(w_lo_ready, u + 1)
                for n, k in enumerate(chunks):
                    mm = split_product(ps, slot, n, hi[:, k], lo[:, k], first and n == 0, last and n == len(chunks) - 1)
                mm.then_inc(unit_used, 1)

            def mod_block(g0, i, j):
                if j == 0 and not (isinstance(i, int) and g0 + i == 0):
                    pe.wait_ge(mod_ready, i + g0)
                pe.wait_ge(mod_in[j], i * 16 + 16 * (g0 + 1))
                for k in range(KC):
                    mm = pe.matmul(mod_out[:, j, :], mod_raw[:, j, k], cond[:, k, :], start=(k == 0), stop=(k == KC - 1))
                mm.then_inc(mod_used, 1)

            def delta_on_tensor(u0):
                with pe.Fori(0, 2 * H // 4) as i:
                    for j in range(4):
                        unit(u0 + 4 * i + j, j, bank[j][:, 0:T], h_hi, h_lo, range(KC))
                        if j:
                            pe.wait_ge(lin_step, 20 * i + 5 * j)
                for b in range(H + 1):
                    if b < H:
                        n = 2 * H + b
                        unit(u0 + n, n % RING, bank[n % 4][:, 0:T], h_hi, h_lo, range(KC))
                        pe.wait_ge(lin_step, 5 * n)
                    if b:
                        pe.wait_ge(silu_done, 2 * H + b)
                        if b >= 3:
                            pe.wait_ge(v_stored, b - 2)
                        for t in range(NT):
                            mm = pe.transpose(bank[6 + (b - 1) % 2][:, t * P:(t + 1) * P], v_silu[:, (b - 1) % 2, t * P:(t + 1) * P], ident[:, :])
                        mm.then_inc(v_turned, 1)
                pe.wait_ge(dn_consts, DN_CONSTS)
                for b in range(2 * H):
                    pe.wait_ge(qk_squared, b + 1)
                    pe.matmul(bank[4][0:2 * H, 0:T], one_hot[:, 2 * H - 1 - b:4 * H - 1 - b], square[:, b % 4],
                              start=(b == 0), stop=(b == 2 * H - 1)).then_inc(qk_summed, 1)
                pe.wait_ge(w_ab_ready, 2)
                for t in range(NT):
                    out = bank[5][:, t * 4 * H:(t + 1) * 4 * H]
                    for k in range(KC):
                        a_hi, a_lo = h_hi[:, k, t * P:(t + 1) * P], h_lo[:, k, t * P:(t + 1) * P]
                        pe.matmul(out, a_hi, w_ab_hi[:, k], start=(k == 0), stop=False)
                        pe.matmul(out, a_hi, w_ab_lo[:, k], start=False, stop=False)
                        mm = pe.matmul(out, a_lo, w_ab_hi[:, k], start=False, stop=(k == KC - 1))
                mm.then_inc(ab_ready, 1)
                pe.wait_ge(lin_step, 15 * H)
                with pe.Fori(0, H // 4) as i:
                    for j in range(4):
                        unit(u0 + 3 * H + 4 * i + j, j, bank[j][:, 0:T], h_hi, h_lo, range(KC))
                        if j:
                            pe.wait_ge(silu_done, 4 * i + (3 * H + j))
                pe.wait_ge(gate_v, 5)
                pe.wait_ge(v_stored, H)
                cols = bank[5][:, 0:6 * H].rearrange("p (t c) -> p t c", t=NT)
                for d in range(2):
                    pe.matmul(cols[:, :, d * H:(d + 1) * H], tri[:, d], log_a[:, :, d * H:(d + 1) * H], start=True, stop=True)
                pe.matmul(bank[6][:, 0:6 * H], ones[:, :], log_a[:, :, :].rearrange("p t c -> p (t c)"), start=True, stop=True).then_inc(gate_t, 1)
                pe.wait_ge(silu_done, 4 * H)
                pe.wait_ge(gate_a, GATE_A_BETA)
                for n, (m, rhs) in enumerate(((log_a, tri[:, 0]), (log_a, tri[:, 1]), (beta, ident[:, :]), (beta, ident[:, :]))):
                    for t in range(NT):
                        mm = pe.matmul(bank[n][0:H, t * P:(t + 1) * P], m[:, t, (n % 2) * H:(n % 2 + 1) * H], rhs, start=True, stop=True)
                mm.then_inc(gate_t, 1)
                pe.wait_ge(gate_v, 13)
                pe.wait_ge(qk_norm_ready, 2)
                with pe.Fori(0, H) as h:
                    pe.wait_ge(head_done, h + 1)
                    pe.wait_ge(sel_ready, h + 1)
                    pe.matmul(bank[0][:, 0:T], sel_k[:, :], qk_rnorm[:, :], start=True, stop=True)
                    pe.matmul(bank[1][:, 0:T], sel_q[:, :], qk_rnorm[:, :], start=True, stop=True).then_inc(norm_spread, 1)
                    for n in range(4):
                        mm = pe.matmul(bank[2 + n][:, 0:T], sel_h[:, :], rows[:, n], start=True, stop=True)
                    mm.then_inc(rows_spread, 1)
                    pe.wait_ge(qk_ready, 2 * h + 2)
                    for t in range(NT):
                        mm = pe.transpose(bank[0][:, t * P:(t + 1) * P], k_head[:, t * P:(t + 1) * P], ident[:, :])
                    mm.then_inc(k_turned, 1)
                    for ps, m in ((bank[6], k_head), (bank[7], q_head)):
                        for t in range(NT):
                            mm = pe.matmul(ps[:, t * P:(t + 1) * P], k_head[:, t * P:(t + 1) * P], m[:, t * P:(t + 1) * P], start=True, stop=True)
                    mm.then_inc(kk_ready, 1)
                    pe.wait_ge(k_decay_ready, h + 1)
                    pe.wait_ge(inv_begun, h + 1)
                    for n in range(LEVELS):
                        for d in range(2):
                            if n == 0:
                                pe.wait_ge(a_step, 4 * h + 2 + d + 1)
                            else:
                                pe.wait_ge(t_joined, h * (2 * LEVELS) + 2 * (n - 1) + d + 1)
                            for t in range(NT):
                                mm = pe.matmul(bank[d][:, t * P:(t + 1) * P], decay[:, d, t], inv[:, d, t], start=True, stop=True)
                            mm.then_inc(p_ready, 1)
                        if n:
                            for d in range(2):
                                pe.wait_ge(p_copied, h * (2 * (LEVELS - 1)) + 2 * (n - 1) + d + 1)
                                if n == 1:
                                    pe.wait_ge(q_exp_ready, 2 * h + 2)
                                for t in range(NT):
                                    mm = pe.matmul(bank[4 + d][:, t * P:(t + 1) * P], step_p[:, d, t], inv_t[:, d, t], start=True, stop=True)
                                if n < LEVELS - 1:
                                    for t in range(NT):
                                        mm = pe.matmul(bank[2 + d][:, t * P:(t + 1) * P], inv_t[:, d, t], step_p[:, d, t], start=True, stop=True)
                                mm.then_inc(t_ready, 1)
                    pe.wait_ge(v_beta_ready, h + 1)
                    pe.wait_ge(q_decay_ready, 2 * h + 2)
                    for k in range(NT):
                        for d in range(2):
                            t = SCAN[d][k]
                            if k == 0:
                                pe.wait_ge(t_joined, (h + 1) * (2 * LEVELS) - 1 + d)
                            else:
                                pe.wait_ge(x_set, 4 * h + 2 * (k - 1) + d + 1)
                            pe.matmul(bank[2 + d][:, 0:P], inv_t[:, d, t], v_beta[:, d, t], start=True, stop=True).then_inc(u_ready, 1)
                        if k == 0:
                            pe.wait_ge(state_in, 16 * h + 16)
                            for d in range(2):
                                t = SCAN[d][1]
                                pe.matmul(bank[d][:, 0:P], k_head[:, t * P:(t + 1) * P], s_old[:, d], start=True, stop=True).then_inc(ks_ready, 1)
                        for d in range(2):
                            t = SCAN[d][k]
                            pe.wait_ge(u_copied, 6 * h + 2 * k + d + 1)
                            if k < 2:
                                if k:
                                    pe.wait_ge(s_stored, 2 * h + d + 1)
                                pe.matmul(bank[4 + d][:, 0:P], k_decay[:, d, k], u_sb[:, d], start=True, stop=True).then_inc(s_added, 1)
                            out = bank[6][:, t * P:(t + 1) * P]
                            if k:
                                pe.matmul(out, (s_old, s_new)[k - 1][:, d], q_decay[:, d, t * P:(t + 1) * P],
                                          start=False, stop=False, skip_group_check=True)
                            pe.matmul(out, u_sb[:, d], qk_decay[:, d, t], start=(k == 0 and d == 0), stop=False,
                                      skip_group_check=True).then_inc(o_added, 1)
                        if k == 1:
                            for d in range(2):
                                t = SCAN[d][2]
                                pe.wait_ge(s_updated, 2 * h + d + 1)
                                pe.matmul(bank[d][:, 0:P], k_head[:, t * P:(t + 1) * P], s_new[:, d], start=True, stop=True).then_inc(ks_ready, 1)
                for h in range(H):
                    pe.wait_ge(o_squared, h + 1)
                    pe.matmul(bank[4][0:H, 0:T], one_hot[:, 2 * H - 1 - h:3 * H - 1 - h], square[:, h % 4],
                              start=(h == 0), stop=(h == H - 1)).then_inc(o_summed, 1)
                pe.wait_ge(o_rnorm_ready, 1)
                for h in range(H):
                    if h >= 2:
                        pe.wait_ge(o_gated, 2 * (h - 1))
                    pe.matmul(bank[h % 2][:, 0:T], ident[0:H, h:h + 1].to_broadcast([H, P]), qk_rnorm[0:H, :],
                              start=True, stop=True).then_inc(o_spread, 1)
                pe.wait_ge(o_lo, H)
                for o in range(KC):
                    if o >= 2:
                        pe.wait_ge(r_ready, KC * 4 + o)
                    unit(u0 + DN_BLOCKS + o, o % RING, bank[2 + o % 2][:, 0:T], h_hi, h_lo, range(KC))

            pe.wait_ge(consts, 6)
            loads = (2, 2, 1, 2, 7)
            for t in range(5):
                pe.wait_ge(table_in[t], 16 * loads[t])
                if t == 4:
                    pe.wait_ge(table_out, 1)
                pe.transpose(bank[t % 4][:, 0:P], table[:, t, :], ident[:, :]).then_inc(turned, 1)
            pe.wait_ge(table_out, 5)
            for t in range(NT):
                pe.wait_ge(x_in[t], 16)
            for o in range(KC):
                if o >= 2:
                    pe.wait_ge(x_ready, o - 1)
                for t in range(NT):
                    mm = pe.transpose(bank[o % 2][:, t * P:(t + 1) * P], x_rows[:, t, o * P:(o + 1) * P], ident[:, :])
                mm.then_inc(turned, 1)
            pe.wait_ge(cond_ready, 2)
            with pe.Fori(0, MOD_FIRST) as i:
                for j in range(4):
                    mod_block(0, i, j)

            for s in range(stages):
                u0 = UNIT0[s]
                pe.wait_ge(h_lo_ready, KC * (s + 1))
                if is_ffn[s]:
                    f0 = FC * ffns[s]
                    with pe.Fori(0, FC // 2) as i:
                        for q in range(2):
                            for j, ps in ((2 * q, bank[q]), (2 * q + 1, bank[2 + q])):
                                unit(u0 + 4 * i + j, j, ps[:, 0:T], h_hi, h_lo, range(KC))
                                if s in MOD_IN_FFN:
                                    mod_block(mod_groups[s], i, j)
                            pe.wait_ge(act_ready, f0 + 2 * i + q + 1)
                    v0 = u0 + 2 * FC
                    with pe.Fori(0, 2) as i:
                        for q in range(12):
                            a, b = FFN_THIRDS[q % 3]
                            pe.wait_ge(act_lo_ready, f0 + b)
                            unit(v0 + 12 * i + q, q % RING, bank[(q // 3) % 2][:, 0:T], act_hi, act_lo, range(a, b),
                                 first=(a == 0), last=(b == FC))
                            if q % 3 == 2:
                                pe.wait_ge(r_ready, KC * s + 4 * i + q // 3 + 1)
                            for n in out_mods(s, q):
                                mod_block(mod_out_groups[s] + n // 4, i * MOD_IN_FFN[s], n % 4)
                    if s in MOD_IN_FFN:
                        for j in range(4):
                            mod_block(mod_tail_group[s], 0, j)
                elif s == 1:
                    with pe.Fori(0, KC // 2) as i:
                        for q in range(2):
                            for j, ps in ((2 * q, bank[q]), (2 * q + 1, bank[2 + q])):
                                unit(u0 + 4 * i + j, j, ps[:, 0:T], h_hi, h_lo, range(KC))
                            pe.wait_ge(glu_ready, 2 * i + q + 1)
                    for o in range(KC):
                        pe.wait_ge(tap_v, TAPS * (o + 1) + (2 * GR - 1) * max(0, o + 1 - KC // 2))
                        if o < KC // 2:
                            pe.wait_ge(tap_g, (TAPS - 1) * (o + 1))
                        mm = pe.matmul(mean_ps[:, 0:T], mean_w[:, :], conv[:, o], start=(o == 0), stop=(o == KC - 1))
                    mm.then_inc(conv_mean, 1)
                    for o in range(KC):
                        pe.wait_ge(conv_squared, o + 1)
                        pe.matmul(var_ps[:, 0:T], mean_w[:, :], square[:, o % 4], start=(o == 0), stop=(o == KC - 1)).then_inc(conv_var, 1)
                    pe.wait_ge(conv_lo, KC)
                    for o in range(KC):
                        if o:
                            pe.wait_ge(r_ready, KC * s + o)
                            pe.wait_ge(y_ready, o)
                        unit(u0 + 2 * KC + o, o % RING, bank[o % 2][:, 0:T], h_hi, h_lo, range(KC))
                elif s == 4:
                    delta_on_tensor(u0)
                pe.wait_ge(r_summed, (KC + 1) * (s + 1))
                pe.matmul(mean_ps[:, 0:T], mean_w[:, :], r_sum[:, :], start=True, stop=True).then_inc(mean_ready, 1)
                for o in range(KC):
                    pe.wait_ge(squared, KC * s + o + 1)
                    pe.matmul(var_ps[:, 0:T], mean_w[:, :], square[:, o % 4], start=(o == 0), stop=(o == KC - 1)).then_inc(var_added, 1)

            pe.wait_ge(x_ready, KC * (stages + 1))
            for t in range(NT):
                for half in range(2):
                    n = 2 * t + half
                    if n >= 4:
                        pe.wait_ge(rows_ready, n - 3)
                    for o in range(4):
                        mm = pe.transpose(bank[n % 4][:, o * P:(o + 1) * P], x[:, 4 * half + o, t * P:(t + 1) * P], ident[:, :])
                    mm.then_inc(turned, 1)


_INS = ['x_prompt', 'x_sample', 'state_delta', 'c', 'c_ctx', 'w_mod', 'b_mod', 'ln_g', 'ln_b', 'ffn_w_in', 'ffn_w_out',
        'cv_w1', 'cv_b1', 'cv_dw', 'cv_dwb', 'cv_ln_g', 'cv_ln_b', 'cv_w2', 'cv_b2',
        'dn_w_in', 'dn_conv', 'dn_a_log', 'dn_dt_bias', 'dn_norm_g', 'dn_w_out']
_OUTS = [(1, TP, D), (1, TS, D), (1, 1, 2, H, P, P)]


def kernel(**inputs):
    import concourse.bacc as bacc
    from concourse.bass_utils import run_bass_kernel_spmd

    nc = bacc.Bacc("TRN2", target_bir_lowering=False, num_devices=1)
    arrays, args = {}, []
    for name in _INS:
        a = np.ascontiguousarray(inputs[name])
        arrays["in_" + name] = a
        args.append(nc.dram_tensor("in_" + name, a.shape, mybir.dt.from_np(a.dtype), kind="ExternalInput").ap())
    for i, shape in enumerate(_OUTS):
        args.append(nc.dram_tensor(f"out_{i}", shape, F32, kind="ExternalOutput").ap())
    program(nc, *args)
    res = run_bass_kernel_spmd(nc, [arrays], core_ids=[0])
    return tuple(res.results[0][f"out_{i}"] for i in range(len(_OUTS)))
```

```python
import numpy as np
import concourse.bass as bass
from concourse import mybir

F32 = mybir.dt.float32
F32R = mybir.dt.float32r
I32 = mybir.dt.int32
ACT = mybir.ActivationFunctionType
ALU = mybir.AluOpType
ds = bass.ds

P = 128
D = 1024
KC = D // P
DEPTH = 2
DFF = 2816
FC = DFF // P
TP, TS = 128, 256
T = TP + TS
NT = T // P
GW = 64
TAPS = 31
H = 8
ALPHA = (2.0 * DEPTH) ** 0.25
LN_EPS = 1e-5
GROUPS = ((0, 0, TP), (1, TP, T))
RING = 4

DN_BLOCKS = 32
UNITS = (2 * FC + 3 * KC, 2 * KC + KC, 2 * FC + 3 * KC, 2 * FC + 3 * KC, DN_BLOCKS + KC, 2 * FC + 3 * KC)
UNIT0 = tuple(sum(UNITS[:s]) for s in range(6))
FFN_THIRDS = ((0, 8), (8, 15), (15, 22))

COL_BMOD = (0, P)
COL_LNG, COL_LNB = 72, P + 72
COL_DW = 2 * P
COL_C = 3 * P + 120
COL_DNCONV = 4 * P
COL_B1, COL_DWB, COL_CLNG, COL_CLNB, COL_B2, COL_CCTX = (4 * P + n for n in (72, 88, 96, 104, 112, 120))

MOD_FIRST = 2
MOD_BESIDE_IN = {0: 5, 2: 5}
MOD_BESIDE_OUT = {0: 2, 2: 2, 3: 2}
MOD_COLS = 32
MW = D // 4


def program(nc, x_prompt, x_sample, state_delta, c, c_ctx, w_mod, b_mod, ln_g, ln_b, ffn_w_in, ffn_w_out,
            cv_w1, cv_b1, cv_dw, cv_dwb, cv_ln_g, cv_ln_b, cv_w2, cv_b2,
            dn_w_in, dn_conv, dn_a_log, dn_dt_bias, dn_norm_g, dn_w_out,
            y_prompt, y_sample, new_state, stages=6):
    from contextlib import ExitStack, contextmanager
    ctx = ExitStack()
    with ctx:
        def sb(name, shape, dt=F32, where=ctx):
            return where.enter_context(nc.sbuf_tensor(name, shape, dt))

        def sem(name):
            return ctx.enter_context(nc.semaphore(name))

        x = sb("x", [P, KC, T])
        r = sb("r", [P, KC, T])
        h_hi = sb("h_hi", [P, KC, T], F32R)
        h_lo = sb("h_lo", [P, KC, T], F32R)
        h_full = sb("h_full", [P, 4, T])
        w_raw = sb("w_raw", [P, RING, 8, P])
        w_hi = sb("w_hi", [P, RING, 8, P], F32R)
        w_lo = sb("w_lo", [P, RING, 8, P], F32R)
        mod = sb("mod", [P, DEPTH * 72, 2])
        scale1 = sb("scale1", [P, KC, 2])
        gate = sb("gate", [P, KC, 2])
        params = sb("params", [P, 5 * P])
        cond = sb("cond", [P, KC, MOD_COLS])
        ident = sb("ident", [P, P])
        mean_w = sb("mean_w", [P, P])
        eps = sb("eps", [P, 1])
        begun = sb("begun", [P, 4])
        r_sum = sb("r_sum", [P, T])
        square = sb("square", [P, 4, T])
        dev = sb("dev", [P, T])
        rstd = sb("rstd", [P, T])

        with ExitStack() as region:
            mod_raw = sb("mod_raw", [P, 4, D], F32, region)
        with ExitStack() as region:
            qk_decay = sb("qk_decay", [P, 2, NT, P], F32, region)
            step_p = sb("step_p", [P, 2, NT, P], F32, region)
            v_beta = sb("v_beta", [P, 2, NT, P], F32, region)
            k_decay = sb("k_decay", [P, 2, 2, P], F32, region)
            u_sb = sb("u_sb", [P, 2, P], F32, region)
            s_old = sb("s_old", [P, 2, P], F32, region)
            s_new = sb("s_new", [P, 2, P], F32, region)
            s_out = sb("s_out", [P, 2, P], F32, region)
        sb("mod_raw_place", [P, 4, D])

        with ExitStack() as region:
            act_hi = sb("act_hi", [P, FC, T], F32R, region)
            act_lo = sb("act_lo", [P, FC, T], F32R, region)
            silu_g = sb("silu_g", [P, 2, T], F32, region)
            act_full = sb("act_full", [P, 2, T], F32, region)
        with ExitStack() as region:
            x_rows = sb("x_rows", [P, NT, D], F32, region)
            table = sb("table", [P, 5, P], F32, region)

        with ExitStack() as region:
            HALF = TAPS // 2
            GR = TS // GW
            glu_seq = sb("glu_seq", [P, KC, HALF + TP + HALF], F32, region)
            glu_row = sb("glu_row", [P, KC // 2, GR, HALF + GW + HALF], F32, region)
            glu_col = sb("glu_col", [P, KC // 2, TS], F32, region)
            sigm = sb("sigm", [P, 2, T], F32, region)
            conv = sb("conv", [P, KC, T], F32, region)
            row_prod = sb("row_prod", [P, 4, GR, GW], F32, region)
            conv_full = sb("conv_full", [P, 4, T], F32, region)
            y_biased = sb("y_biased", [P, 2, T], F32, region)

        with ExitStack() as region:
            qk = sb("qk", [P, 2 * H, T], F32, region)
            v_tok = sb("v_tok", [P, NT, H, P], F32, region)
            o_all = sb("o_all", [P, H, T], F32, region)
            row_src = sb("row_src", [P, NT, 3, 4 * H], F32, region)
            rows_hi = sb("rows_hi", [4 * H, T], F32R, region)
            rows_lo = sb("rows_lo", [4 * H, T], F32R, region)
            masks = sb("masks", [P, 14, P], mybir.dt.int8, region)
            tri = sb("tri", [P, 2, P], F32, region)
            never = sb("never", [P, 2, P], F32, region)
            ones = sb("ones", [P, P], F32, region)
            one_hot = sb("one_hot", [P, 4 * H - 1], F32, region)
            sel_qk = sb("sel_qk", [2 * H, 2, P], F32R, region)
            sel_row = sb("sel_row", [4 * H, 4, P], F32R, region)
            qk_norm = sb("qk_norm", [2 * H, T], F32, region)
            qk_rnorm_hi = sb("qk_rnorm_hi", [2 * H, T], F32R, region)
            qk_rnorm_lo = sb("qk_rnorm_lo", [2 * H, T], F32R, region)
            q_scale = sb("q_scale", [2 * H, 2], F32, region)
            w_ab = sb("w_ab", [P, KC, 4 * H], F32, region)
            w_ab_hi = sb("w_ab_hi", [P, KC, 4 * H], F32R, region)
            w_ab_lo = sb("w_ab_lo", [P, KC, 4 * H], F32R, region)
            norm_g = sb("norm_g", [P, 1], F32, region)
            dt_a = sb("dt_a", [P, 2, 2 * H], F32, region)
            small_names = ("exp_a", "tot", "g_col", "end_decay", "g_decay", "tot_decay", "minus_beta_g", "pre", "soft", "pos", "log_a", "beta")
            exp_a, tot, g_col, end_decay, g_decay, tot_decay, minus_beta_g, pre, soft, pos, log_a, beta = (
                sb(n, [P, NT, 2 * H], F32, region) for n in small_names)
            ab = sb("ab", [P, NT, 4 * H], F32, region)
            carrier = sb("carrier", [P, 14], F32, region)
        mod_rows = square[:, 0, 0:MW]
        lin = step_p[:, :, :, :].rearrange("p d t c -> p d (t c)")
        v_silu = v_beta[:, :, :, :].rearrange("p d t c -> p d (t c)")
        z = r
        decay = square[:, 0:2, :].rearrange("p d (t c) -> p d t c", c=P)
        q_decay = square[:, 2:4, :]
        k_head, q_head = dev, rstd
        inv = h_full[:, 0:2, :].rearrange("p d (t c) -> p d t c", c=P)
        inv_t = h_full[:, 2:4, :].rearrange("p d (t c) -> p d t c", c=P)
        SCAN = ((0, 1, 2), (0, 2, 1))
        LEVELS = 7

        def every_other(ap, n, side):
            if len(ap.shape) == 2:
                return ap.rearrange("p (a s c) -> p a s c", s=2, c=1 << n)[:, :, side]
            return ap.rearrange("p t (a s c) -> p t a s c", s=2, c=1 << n)[:, :, :, side]

        bank = [ctx.enter_context(nc.psum_tensor(f"bank{n}", [P, 512], F32)) for n in range(8)]
        mean_ps, var_ps = bank[4], bank[5]
        mod_ps = bank[6][:, 0:MW]
        mod_turned_ps = bank[7][:, 0:2 * P]

        consts = sem("consts")
        table_in = [sem(f"table_in{n}") for n in range(5)]
        x_in = [sem(f"x_in{n}") for n in range(NT)]
        turned = sem("turned")
        table_out = sem("table_out")
        cond_ready = sem("cond_ready")
        w_in = [sem(f"w_in{n}") for n in range(RING)]
        w_hi_ready = sem("w_hi_ready")
        w_lo_ready = sem("w_lo_ready")
        unit_used = sem("unit_used")
        mod_in = [sem(f"mod_in{n}") for n in range(4)]
        mod_used = sem("mod_used")
        mod_copied = sem("mod_copied")
        mod_turned = sem("mod_turned")
        mod_ready = sem("mod_ready")
        small = sem("small")
        silu_ready = sem("silu_ready")
        act_ready = sem("act_ready")
        act_hi_ready = sem("act_hi_ready")
        act_lo_ready = sem("act_lo_ready")
        r_ready = sem("r_ready")
        r_scaled = sem("r_scaled")
        r_summed = sem("r_summed")
        mean_ready = sem("mean_ready")
        centred = sem("centred")
        squared = sem("squared")
        var_added = sem("var_added")
        dev_ready = sem("dev_ready")
        rstd_ready = sem("rstd_ready")
        normed = sem("normed")
        x_ready = sem("x_ready")
        h_ready = sem("h_ready")
        h_hi_ready = sem("h_hi_ready")
        h_lo_ready = sem("h_lo_ready")
        dn_consts = sem("dn_consts")
        dn_small_in = sem("dn_small_in")
        state_in = sem("state_in")
        state_out = sem("state_out")
        lin_step = sem("lin_step")
        silu_done = sem("silu_done")
        v_turned = sem("v_turned")
        v_stored = sem("v_stored")
        qk_squared = sem("qk_squared")
        qk_summed = sem("qk_summed")
        qk_norm_ready = sem("qk_norm_ready")
        w_ab_ready = sem("w_ab_ready")
        ab_ready = sem("ab_ready")
        gate_v = sem("gate_v")
        gate_a = sem("gate_a")
        gate_t = sem("gate_t")
        head_done = sem("head_done")
        sel_ready = sem("sel_ready")
        norm_spread = sem("norm_spread")
        rows_spread = sem("rows_spread")
        qk_ready = sem("qk_ready")
        kk_ready = sem("kk_ready")
        k_turned = sem("k_turned")
        diff_ready = sem("diff_ready")
        decay_ready = sem("decay_ready")
        q_exp_ready = sem("q_exp_ready")
        k_decay_ready = sem("k_decay_ready")
        a_step = sem("a_step")
        q_decay_ready = sem("q_decay_ready")
        inv_begun = sem("inv_begun")
        v_beta_ready = sem("v_beta_ready")
        p_ready = sem("p_ready")
        p_copied = sem("p_copied")
        t_ready = sem("t_ready")
        inv_turned = sem("inv_turned")
        inv_copied = sem("inv_copied")
        t_joined = sem("t_joined")
        ks_ready = sem("ks_ready")
        x_set = sem("x_set")
        u_ready = sem("u_ready")
        u_copied = sem("u_copied")
        s_added = sem("s_added")
        s_stored = sem("s_stored")
        s_updated = sem("s_updated")
        o_added = sem("o_added")
        o_squared = sem("o_squared")
        o_summed = sem("o_summed")
        o_norm_ready = sem("o_norm_ready")
        o_rnorm_ready = sem("o_rnorm_ready")
        o_spread = sem("o_spread")
        o_gated = sem("o_gated")
        o_hi = sem("o_hi")
        o_lo = sem("o_lo")
        pads_ready = sem("pads_ready")
        sigm_ready = sem("sigm_ready")
        glu_ready = sem("glu_ready")
        tap_v = sem("tap_v")
        row_tap = sem("row_tap")
        tap_g = sem("tap_g")
        conv_mean = sem("conv_mean")
        conv_centred = sem("conv_centred")
        conv_squared = sem("conv_squared")
        conv_var = sem("conv_var")
        conv_dev = sem("conv_dev")
        conv_rstd = sem("conv_rstd")
        conv_normed = sem("conv_normed")
        conv_act = sem("conv_act")
        conv_hi = sem("conv_hi")
        conv_lo = sem("conv_lo")
        y_ready = sem("y_ready")
        rows_ready = sem("rows_ready")
        out_done = sem("out_done")

        block = ctx.enter_context(nc.Block())

        def in_view(w, cols):
            return w.rearrange("(k p) (b m) -> p k b m", p=P, m=P) if cols else w
        mod_view = [w_mod[l].rearrange("(k p) m -> p k m", p=P) for l in range(DEPTH)]
        x_src = (x_prompt[0, :, :], x_sample[0, 0:P, :], x_sample[0, P:2 * P, :])
        y_dst = (y_prompt[0, :, :], y_sample[0, 0:P, :], y_sample[0, P:2 * P, :])

        DN_CONSTS = 15 + 6 * LEVELS
        GATE_A_BETA = 5
        LAST_UNIT = UNIT0[stages - 1] + UNITS[stages - 1]

        def mod_col(s):
            return 72 * (s // 3) + 24 * (s % 3)

        def ffn_of(s):
            return ffn_w_in[s // 3, (s % 3) // 2], ffn_w_out[s // 3, (s % 3) // 2]

        is_ffn = [s % 3 != 1 for s in range(6)]
        ffns = [sum(is_ffn[:s]) for s in range(7)]
        mod_in_chunk = [MOD_FIRST + sum(MOD_BESIDE_IN.get(k, 0) + MOD_BESIDE_OUT.get(k, 0) for k in range(s)) for s in range(6)]
        mod_out_chunk = [g + MOD_BESIDE_IN.get(s, 0) for s, g in enumerate(mod_in_chunk)]

        def in_slices(q):
            return (range(0, 2), *(range(n, n + 1) for n in range(2, KC)), range(0))[q]

        def out_slices(s, q):
            return range(q, q + 1) if s in MOD_BESIDE_OUT and q < KC else range(0)

        @block.sync
        def _(sp):
            def load_unit(u, slot, src, chunks=8, first=False):
                if not first:
                    sp.wait_ge(w_hi_ready, u - RING + 1)
                    sp.wait_ge(w_lo_ready, u - RING + 1)
                sp.dma_start(w_raw[:, slot, 0:chunks], src).then_inc(w_in[slot], 16)

            def load_mod(g0, i, k, first=False):
                if not first:
                    sp.wait_ge(mod_used, KC * i + (KC * g0 + k - 3))
                src = w_mod[g0 // 9, k * P:(k + 1) * P, ds(i * D + g0 % 9 * D, D)]
                sp.dma_start(mod_raw[:, k % 4], src).then_inc(mod_in[k % 4], 16)

            def ffn_in_units(s, pair, eighth=0, beside=None, first=False):
                wv = ffn_of(s)[0].rearrange("(k p) m -> p k m", p=P)
                for j in range(4):
                    col = (j % 2) * DFF + (j // 2) * P
                    load_unit(UNIT0[s] + 4 * pair + j, j, wv[:, :, ds(pair * (2 * P) + col, P)], first=first)
                    if beside is not None:
                        for k in in_slices(eighth + j):
                            load_mod(mod_in_chunk[s], beside, k)

            for t in range(5):
                sp.wait_ge(consts, 6)
                rows = {0: ((b_mod[0].rearrange("(r p) -> r p", p=P), 0, 72), (ln_g.rearrange("l j (r p) -> (l j r) p", p=P), 72, 120)),
                        1: ((b_mod[1].rearrange("(r p) -> r p", p=P), 0, 72), (ln_b.rearrange("l j (r p) -> (l j r) p", p=P), 72, 120)),
                        2: ((cv_dw[0].rearrange("t (r p) -> (t r) p", p=P)[0:P], 0, P),),
                        3: ((cv_dw[0].rearrange("t (r p) -> (t r) p", p=P)[P:TAPS * KC], 0, TAPS * KC - P), (c[0].rearrange("(r p) -> r p", p=P), 120, 128)),
                        4: ((dn_conv[0].rearrange("t (r p) -> (t r) p", p=P), 0, 72), (cv_b1[0].rearrange("(r p) -> r p", p=P), 72, 88),
                            (cv_dwb[0].rearrange("(r p) -> r p", p=P), 88, 96), (cv_ln_g[0].rearrange("(r p) -> r p", p=P), 96, 104),
                            (cv_ln_b[0].rearrange("(r p) -> r p", p=P), 104, 112), (cv_b2[0].rearrange("(r p) -> r p", p=P), 112, 120),
                            (c_ctx.rearrange("(r p) -> r p", p=P), 120, 128))}[t]
                for src, a, b in rows:
                    sp.dma_start(table[a:b, t, :], src).then_inc(table_in[t], 16)
            for t in range(NT):
                sp.dma_start(x_rows[:, t, :], x_src[t]).then_inc(x_in[t], 16)
            for g in range(MOD_FIRST):
                for k in range(KC):
                    load_mod(g, 0, k, first=(g == 0 and k < 4))
            for s in range(stages):
                u0 = UNIT0[s]
                if is_ffn[s]:
                    if s in MOD_BESIDE_IN:
                        n = 0
                        if s == 0:
                            for half in range(2):
                                ffn_in_units(s, half, 4 * half, 0, first=(half == 0))
                            n = 1
                        with sp.Fori(n, MOD_BESIDE_IN[s]) as i:
                            for half in range(2):
                                ffn_in_units(s, 2 * i + half, 4 * half, i)
                        for pair in range(2 * MOD_BESIDE_IN[s], FC // 2):
                            ffn_in_units(s, pair)
                    else:
                        with sp.Fori(0, FC // 2) as i:
                            ffn_in_units(s, i)
                    wv = ffn_of(s)[1].rearrange("(k p) m -> p k m", p=P)
                    with sp.Fori(0, 2) as i:
                        for q in range(12):
                            a, b = FFN_THIRDS[q % 3]
                            load_unit(u0 + 2 * FC + 12 * i + q, q % RING, wv[:, a:b, ds(i * (4 * P) + (q // 3) * P, P)], b - a)
                            for k in out_slices(s, q):
                                load_mod(mod_out_chunk[s], i, k)
                elif s == 1:
                    wv = cv_w1[0].rearrange("(k p) m -> p k m", p=P)
                    with sp.Fori(0, KC // 2) as i:
                        for j in range(4):
                            load_unit(u0 + 4 * i + j, j, wv[:, :, ds(i * (2 * P) + ((j % 2) * D + (j // 2) * P), P)])
                    wv = cv_w2[0].rearrange("(k p) m -> p k m", p=P)
                    with sp.Fori(0, KC // 4) as i:
                        for j in range(4):
                            load_unit(u0 + 2 * KC + 4 * i + j, j, wv[:, :, ds(i * (4 * P) + j * P, P)])
                elif s == 4:
                    wv = dn_w_in[0].rearrange("(k p) m -> p k m", p=P)
                    for j in range(RING):
                        load_unit(u0 + j, j, wv[:, :, j * P:(j + 1) * P])
                    sp.wait_ge(mean_ready, s)
                    sp.dma_start(w_ab[:, :, :], dn_w_in[0, :, DN_BLOCKS * P:].rearrange("(k p) m -> p k m", p=P)).then_inc(dn_small_in, 16)
                    sp.dma_start(dt_a[:, 0, :], dn_dt_bias[0].rearrange("d h -> (d h)").partition_broadcast(P)).then_inc(dn_small_in, 16)
                    sp.dma_start(dt_a[:, 1, :], dn_a_log[0].rearrange("d h -> (d h)").partition_broadcast(P)).then_inc(dn_small_in, 16)
                    sp.dma_start(norm_g[:, :], dn_norm_g.rearrange("a p -> p a")).then_inc(dn_small_in, 16)
                    with sp.Fori(1, DN_BLOCKS // 4) as i:
                        for j in range(4):
                            load_unit(u0 + 4 * i + j, j, wv[:, :, ds(i * (4 * P) + j * P, P)])
                    wv = dn_w_out[0].rearrange("(k p) m -> p k m", p=P)
                    for o in range(RING):
                        load_unit(u0 + DN_BLOCKS + o, o, wv[:, :, o * P:(o + 1) * P])
                    s_src = state_delta[0, 0].rearrange("d h k v -> k h d v")
                    s_dst = new_state[0, 0].rearrange("d h k v -> k h d v")
                    for h in range(H):
                        if h:
                            sp.wait_ge(state_out, 16 * h)
                        sp.wait_ge(head_done, h + 1)
                        sp.dma_start(s_old[:, :, :], s_src[:, h]).then_inc(state_in, 16)
                        sp.wait_ge(s_stored, 2 * h + 2)
                        sp.dma_start(s_dst[:, h], s_out[:, :, :]).then_inc(state_out, 16)
                    for o in range(RING, KC):
                        load_unit(u0 + DN_BLOCKS + o, o % RING, wv[:, :, o * P:(o + 1) * P])
            for t in range(NT):
                sp.wait_ge(rows_ready, 2 * (t + 1))
                sp.dma_start(y_dst[t], x_rows[:, t, :]).then_inc(out_done, 16)
            sp.wait_ge(out_done, 16 * NT)
            if stages > 4:
                sp.wait_ge(state_out, 16 * H)

        @block.gpsimd
        def _(pool):
            pool.memset(ident[:, :], 0.0).then_inc(consts, 1)
            pool.wait_ge(consts, 1)
            pool.memset(mean_w[:, :], 1.0 / D).then_inc(consts, 1)
            pool.wait_ge(consts, 2)
            pool.memset(eps[:, :], LN_EPS).then_inc(consts, 1)
            pool.wait_ge(consts, 3)
            pool.memset(table[96:P, 0:2, :], 0.0).then_inc(consts, 1)
            pool.wait_ge(consts, 4)
            pool.memset(cond[:, :, :], 0.0).then_inc(consts, 1)
            pool.wait_ge(consts, 5)
            pool.memset(r_sum[:, :], 0.0).then_inc(r_summed, 1)
            pool.wait_ge(r_summed, 1)
            pool.affine_select(out=ident[:, :], in_=ident[:, :], compare_op=ALU.not_equal, fill=1.0, base=0,
                               pattern=[[-1, P]], channel_multiplier=1).then_inc(consts, 1)

            def lower_h(k):
                for o in range(KC):
                    pool.wait_ge(h_hi_ready, KC * k + o + 1)
                    pool.tensor_tensor(h_lo[:, o], h_full[:, o % 4], h_hi[:, o].bitcast(F32), ALU.subtract).then_inc(h_lo_ready, 1)

            def conv_on_pool():
                for o in range(KC // 2):
                    out = conv[:, o, TP:T].rearrange("p (g w) -> p g w", w=GW)
                    for tap in range(1, TAPS):
                        n = (TAPS - 1) * o + tap - 1
                        pool.wait_ge(row_tap, n + o + 2)
                        if n:
                            pool.wait_ge(tap_g, n)
                        pool.tensor_tensor(out, out, row_prod[:, n % 4], ALU.add).then_inc(tap_g, 1)
                for o in range(KC):
                    pool.wait_ge(conv_hi, o + 1)
                    pool.tensor_tensor(h_lo[:, o], conv_full[:, o % 4], h_hi[:, o].bitcast(F32), ALU.subtract).then_inc(conv_lo, 1)

            def delta_on_pool():
                done = [0]

                def each(instruction):
                    done[0] += 1
                    instruction.then_inc(dn_consts, 1)
                    pool.wait_ge(dn_consts, done[0])

                each(pool.memset(ones[:, :], 1.0))
                each(pool.memset(row_src[:, :, :, :], 0.0))
                each(pool.memset(one_hot[:, :], 0.0))
                each(pool.memset(one_hot[:, 2 * H - 1:2 * H], 1.0))
                each(pool.memset(q_scale[:, 0:1], 1.0))
                each(pool.memset(q_scale[:, 1:2], 1e-6))
                each(pool.memset(q_scale[0:H, 0:1], float(P)))
                each(pool.memset(q_scale[0:H, 1:2], P * 1e-6))
                each(pool.memset(tri[:, :, :], 1.0))
                each(pool.memset(never[:, :, :], 0.0))
                for d in range(2):
                    sign = 1 - 2 * d
                    for m, fill in ((tri, 0.0), (never, -1e30)):
                        each(pool.affine_select(out=m[:, d], in_=m[:, d], compare_op=ALU.is_ge, fill=fill, base=0,
                                                pattern=[[sign, P]], channel_multiplier=-sign))
                each(pool.memset(masks[:, :, :], 0.0))
                for n in range(LEVELS):
                    b = 1 << n
                    for up in range(2):
                        part = masks[:, 2 * n + up].rearrange("p (a c) -> p a c", c=2 * b)[:, :, up * b:(up + 1) * b]
                        first = (1 - up) * b
                        pairs = P // (2 * b)
                        each(pool.memset(part, 1.0))
                        each(pool.affine_select(out=part, in_=part, compare_op=ALU.is_ge, fill=0.0, base=-first,
                                                pattern=[[-2 * b, pairs], [0, b]], channel_multiplier=1))
                        each(pool.affine_select(out=part, in_=part, compare_op=ALU.is_ge, fill=0.0, base=first + b - 1,
                                                pattern=[[2 * b, pairs], [0, b]], channel_multiplier=-1))
                assert done[0] == DN_CONSTS
                pool.wait_ge(gate_a, GATE_A_BETA)
                pool.wait_ge(v_stored, H)
                with pool.Fori(0, H) as h:
                    pool.wait_ge(norm_spread, h + 1)
                    for m in (inv, inv_t):
                        for d in range(2):
                            i3 = ident[:, :].unsqueeze(1).to_broadcast([P, NT, P])
                            last = pool.tensor_tensor(m[:, d], i3, i3, ALU.mult)
                    last.then_inc(inv_begun, 1)
                    pool.wait_ge(inv_begun, h + 1)
                    for d in range(2):
                        for t in range(NT):
                            last = pool.tensor_tensor(v_beta[:, d, t:t + 1], v_tok[:, t, ds(h, 1)],
                                                      beta[:, t, ds(h + d * H, 1)].unsqueeze(2).to_broadcast([P, 1, P]), ALU.mult)
                    last.then_inc(v_beta_ready, 1)
                    pool.wait_ge(v_beta_ready, h + 1)
                for o in range(KC):
                    pool.wait_ge(o_hi, o + 1)
                    pool.tensor_tensor(h_lo[:, o], h_full[:, o % 4], h_hi[:, o].bitcast(F32), ALU.subtract).then_inc(o_lo, 1)
                pool.wait_ge(o_gated, 2 * H)

            lower_h(0)
            for s in range(stages):
                if s == 1:
                    pool.wait_ge(mean_ready, s)
                    pool.memset(glu_seq[:, :, :], 0.0).then_inc(pads_ready, 1)
                    pool.wait_ge(pads_ready, 1)
                    pool.memset(glu_row[:, :, :, :], 0.0).then_inc(pads_ready, 1)
                    pool.wait_ge(pads_ready, 2)
                if s:
                    pool.wait_ge(mean_ready, s)
                    pool.memset(r_sum[:, :], 0.0).then_inc(r_summed, 1)
                if s == 4:
                    delta_on_pool()
                pool.wait_ge(x_ready, KC * (s + 1))
                pool.tensor_scalar(r[:, :, :], x[:, :, :], ALPHA, 0.0, ALU.mult, ALU.add).then_inc(r_scaled, 1)
                if s == 1:
                    conv_on_pool()
                for o in range(KC):
                    pool.wait_ge(r_ready, KC * s + o + 2)
                    pool.wait_ge(r_summed, (KC + 1) * s + o + 1)
                    pool.tensor_tensor(r_sum[:, :], r_sum[:, :], r[:, o], ALU.add).then_inc(r_summed, 1)
                if s + 1 < stages:
                    lower_h(s + 1)

        @block.scalar
        def _(act):
            def upper_w(u, slot, lap):
                if not (isinstance(u, int) and u < RING):
                    act.wait_ge(unit_used, u - RING + 1)
                act.wait_ge(w_in[slot], lap * 16)
                act.activation(w_hi[:, slot], w_raw[:, slot], ACT.Copy).then_inc(w_hi_ready, 1)

            def upper_h(k, o):
                act.wait_ge(h_ready, KC * k + o + 1)
                act.activation(h_hi[:, o], h_full[:, o % 4], ACT.Copy).then_inc(h_hi_ready, 1)

            def delta_on_scalar(u0):
                with act.Fori(0, 2 * H // 4) as i:
                    for j in range(4):
                        act.wait_ge(lin_step, 20 * i + 5 * (j + 1))
                        act.activation(qk[:, ds(4 * i + j, 1)], lin[:, j % 2].unsqueeze(1), ACT.Silu).then_inc(silu_done, 1)
                        upper_w(u0 + 4 * i + j + RING, j, i + (u0 // RING + 2))
                for b in range(H + 1):
                    if b < H:
                        n = 2 * H + b
                        act.wait_ge(lin_step, 5 * (n + 1))
                        if b >= 2:
                            act.wait_ge(v_turned, b - 1)
                        act.activation(v_silu[:, b % 2], lin[:, n % 2], ACT.Silu).then_inc(silu_done, 1)
                        upper_w(u0 + n + RING, n % RING, (u0 + n) // RING + 2)
                    if b:
                        act.wait_ge(v_turned, b)
                        act.activation(v_tok[:, :, b - 1], bank[6 + (b - 1) % 2][:, 0:T].rearrange("p (t c) -> p t c", c=P),
                                       ACT.Copy).then_inc(v_stored, 1)
                act.wait_ge(dn_small_in, 64)
                act.activation(w_ab_hi[:, :, :], w_ab[:, :, :], ACT.Copy).then_inc(w_ab_ready, 1)
                for b in range(2 * H):
                    if b >= 4:
                        act.wait_ge(qk_summed, b - 3)
                    act.activation(square[:, b % 4], qk[:, b], ACT.Square).then_inc(qk_squared, 1)
                act.wait_ge(dn_consts, DN_CONSTS)
                act.wait_ge(qk_summed, 2 * H)
                act.activation(qk_norm[:, :], bank[4][0:2 * H, 0:T], ACT.Sqrt, scale=q_scale[:, 0:1], bias=q_scale[:, 1:2]).then_inc(qk_norm_ready, 1)
                act.activation(exp_a[:, 0, :], dt_a[:, 1, :], ACT.Exp).then_inc(gate_a, 1)
                act.wait_ge(gate_v, 2)
                act.activation(soft[:, :, :], pre[:, :, :], ACT.Abs).then_inc(gate_a, 1)
                act.wait_ge(gate_a, 2)
                act.activation(soft[:, :, :], soft[:, :, :], ACT.Exp, scale=-1.0).then_inc(gate_a, 1)
                act.wait_ge(gate_a, 3)
                act.activation(soft[:, :, :], soft[:, :, :], ACT.Ln, bias=1.0).then_inc(gate_a, 1)
                act.activation(beta[:, :, :], ab[:, :, 2 * H:4 * H], ACT.Sigmoid).then_inc(gate_a, 1)
                with act.Fori(0, H // 4) as i:
                    for j in range(4):
                        act.wait_ge(unit_used, u0 + 3 * H + 4 * i + j + 1)
                        act.activation(z[:, ds(4 * i + j, 1)], bank[j][:, 0:T].unsqueeze(1), ACT.Silu).then_inc(silu_done, 1)
                        upper_w(u0 + 3 * H + 4 * i + j + RING, j, i + ((u0 + 3 * H) // RING + 2))
                act.wait_ge(gate_v, 11)
                act.activation(end_decay[:, :, :], end_decay[:, :, :], ACT.Exp).then_inc(gate_a, 1)
                act.activation(g_decay[:, :, :], g_col[:, :, :], ACT.Exp).then_inc(gate_a, 1)
                act.activation(tot_decay[:, :, :], tot[:, :, :], ACT.Exp).then_inc(gate_a, 1)
                act.activation(begun[:, 3:4], eps[:, :], ACT.Copy).then_inc(head_done, 1)
                with act.Fori(0, H) as h:
                    for d in range(2):
                        act.wait_ge(diff_ready, 2 * h + d + 1)
                        act.activation(decay[:, d], qk_decay[:, d], ACT.Exp).then_inc(decay_ready, 1)
                    for d in range(2):
                        act.activation(qk_decay[:, d], qk_decay[:, d], ACT.Exp).then_inc(decay_ready, 1)
                    for d in range(2):
                        act.activation(q_decay[:, d, TP:T], bank[2 + d][:, TP:T], ACT.Exp).then_inc(q_exp_ready, 1)
                    for n in range(1, LEVELS):
                        for d in range(2):
                            act.wait_ge(p_ready, h * (2 * LEVELS) + 2 * n + d + 1)
                            act.activation(every_other(step_p[:, d], n, d), every_other(bank[d][:, 0:T].rearrange("p (t c) -> p t c", c=P), n, d), ACT.Copy).then_inc(p_copied, 1)
                        if n < LEVELS - 1:
                            for d in range(2):
                                act.wait_ge(inv_turned, h * (2 * (LEVELS - 2)) + 2 * (n - 1) + d + 1)
                                act.activation(every_other(inv[:, d], n + 1, d),
                                               every_other(bank[2 + d][:, 0:T].rearrange("p (t c) -> p t c", c=P), n + 1, d), ACT.Copy).then_inc(inv_copied, 1)
                    for k in range(NT):
                        for d in range(2):
                            act.wait_ge(u_ready, 6 * h + 2 * k + d + 1)
                            if k:
                                act.wait_ge(o_added, 6 * h + 2 * (k - 1) + d + 1)
                            act.activation(u_sb[:, d], bank[2 + d][:, 0:P], ACT.Copy).then_inc(u_copied, 1)
                        if k == 0:
                            act.wait_ge(state_in, 16 * h + 16)
                            for d in range(2):
                                act.wait_ge(s_added, 4 * h + d + 1)
                                act.activation(s_out[:, d], bank[4 + d][:, 0:P], ACT.Copy).then_inc(s_stored, 1)
                    act.wait_ge(o_added, 6 * h + 6)
                    act.activation(o_all[:, ds(h, 1)], bank[6][:, 0:T].unsqueeze(1), ACT.Copy).then_inc(head_done, 1)
                act.wait_ge(head_done, H + 1)
                for h in range(H):
                    if h >= 4:
                        act.wait_ge(o_summed, h - 3)
                    act.activation(square[:, h % 4], o_all[:, h], ACT.Square).then_inc(o_squared, 1)
                act.wait_ge(o_summed, H)
                act.activation(qk_norm[0:H, :], bank[4][0:H, 0:T], ACT.Sqrt, scale=1.0 / P, bias=eps[0:H, :]).then_inc(o_norm_ready, 1)
                for o in range(KC):
                    act.wait_ge(o_gated, 2 * o + 2)
                    act.activation(h_hi[:, o], h_full[:, o % 4], ACT.Copy).then_inc(o_hi, 1)
                for o in range(KC):
                    u = u0 + DN_BLOCKS + o + RING
                    if u < LAST_UNIT:
                        upper_w(u, o % RING, u // RING + 1)

            act.wait_ge(table_out, 5)
            act.activation(cond[:, :, 0], params[:, COL_CCTX:COL_CCTX + KC], ACT.Silu).then_inc(cond_ready, 1)
            act.activation(cond[:, :, 1], params[:, COL_C:COL_C + KC], ACT.Silu).then_inc(cond_ready, 1)
            for j in range(RING):
                upper_w(j, j, 1)
            for o in range(KC):
                upper_h(0, o)

            for s in range(stages):
                u0 = UNIT0[s]
                if is_ffn[s]:
                    f0 = FC * ffns[s]
                    with act.Fori(0, FC // 2) as i:
                        for q in range(2):
                            act.wait_ge(unit_used, u0 + 4 * i + 2 * q + 2)
                            act.activation(silu_g[:, q], bank[2 + q][:, 0:T], ACT.Silu).then_inc(silu_ready, 1)
                            act.wait_ge(act_ready, f0 + 2 * i + q + 2)
                            act.activation(act_hi[:, ds(2 * i + q, 1)], act_full[:, ds(q, 1)], ACT.Copy).then_inc(act_hi_ready, 1)
                            for j in range(2):
                                upper_w(u0 + 4 * i + 2 * q + j + RING, 2 * q + j, i + (u0 // RING + 2))
                    if s == stages - 1:
                        for q in range(3 * KC - RING):
                            upper_w(u0 + 2 * FC + q + RING, q % RING, (u0 + 2 * FC + q) // RING + 2)
                    else:
                        with act.Fori(0, 2) as i:
                            for q in range(12):
                                upper_w(u0 + 2 * FC + 12 * i + q + RING, q % RING,
                                        i * 3 + ((u0 + 2 * FC + q) // RING + 2))
                elif s == 1:
                    for o in range(KC):
                        act.wait_ge(unit_used, u0 + 2 * o + 2)
                        act.activation(sigm[:, o % 2], bank[2 + o % 2][:, 0:T], ACT.Sigmoid,
                                       bias=params[:, COL_B1 + KC + o:COL_B1 + KC + o + 1]).then_inc(sigm_ready, 1)
                        c = o // 2
                        act.wait_ge(glu_ready, c + 2)
                        for tap in (range(16), range(16, TAPS))[o % 2]:
                            n = (TAPS - 1) * c + tap - 1
                            src = glu_row[:, c, :, tap:tap + GW]
                            w = params[:, COL_DW + tap * KC + c:COL_DW + tap * KC + c + 1]
                            if tap == 0:
                                act.activation(conv[:, c, TP:T].rearrange("p (g w) -> p g w", w=GW), src, ACT.Identity, scale=w,
                                               bias=params[:, COL_DWB + c:COL_DWB + c + 1]).then_inc(row_tap, 1)
                            else:
                                if n > 3:
                                    act.wait_ge(tap_g, n - 3)
                                act.activation(row_prod[:, n % 4], src, ACT.Copy, scale=w).then_inc(row_tap, 1)
                            if tap in (4, 12, 20, 28):
                                u = u0 + 2 * o + (tap in (12, 28)) + RING
                                upper_w(u, u % RING, u // RING + 1)
                    for o in range(KC):
                        act.wait_ge(conv_centred, o + 1)
                        if o >= 4:
                            act.wait_ge(conv_var, o - 3)
                        act.activation(square[:, o % 4], conv[:, o], ACT.Square).then_inc(conv_squared, 1)
                    act.wait_ge(conv_var, KC)
                    act.activation(dev[:, :], var_ps[:, 0:T], ACT.Sqrt, bias=eps[:, :]).then_inc(conv_dev, 1)
                    for o in range(KC):
                        act.wait_ge(conv_normed, o + 1)
                        if o >= 4:
                            act.wait_ge(conv_lo, o - 3)
                        act.activation(conv_full[:, o % 4], conv[:, o], ACT.Silu, scale=params[:, COL_CLNG + o:COL_CLNG + o + 1],
                                       bias=params[:, COL_CLNB + o:COL_CLNB + o + 1]).then_inc(conv_act, 1)
                        act.wait_ge(conv_act, o + 1)
                        act.activation(h_hi[:, o], conv_full[:, o % 4], ACT.Copy).then_inc(conv_hi, 1)
                    for o in range(KC):
                        u = u0 + 2 * KC + o
                        act.wait_ge(unit_used, u + 1)
                        act.activation(y_biased[:, o % 2], bank[o % 2][:, 0:T], ACT.Identity,
                                       bias=params[:, COL_B2 + o:COL_B2 + o + 1]).then_inc(y_ready, 1)
                        if u + RING < LAST_UNIT:
                            upper_w(u + RING, o % RING, (u + RING) // RING + 1)
                elif s == 4:
                    delta_on_scalar(u0)
                for o in range(KC):
                    act.wait_ge(centred, KC * s + o + 1)
                    if o >= 4:
                        act.wait_ge(var_added, KC * s + o - 3)
                    act.activation(square[:, o % 4], r[:, o], ACT.Square).then_inc(squared, 1)
                act.wait_ge(var_added, KC * (s + 1))
                act.activation(dev[:, :], var_ps[:, 0:T], ACT.Sqrt, bias=eps[:, :]).then_inc(dev_ready, 1)
                for o in range(KC + 1):
                    if o < KC:
                        act.wait_ge(normed, KC * s + o + 1)
                        n = (s // 3 * 3 + s % 3) * KC + o
                        act.activation(x[:, o], r[:, o], ACT.Identity, scale=params[:, COL_LNG + n:COL_LNG + n + 1],
                                       bias=params[:, COL_LNB + n:COL_LNB + n + 1]).then_inc(x_ready, 1)
                    if o and s + 1 < stages:
                        upper_h(s + 1, o - 1)

        @block.vector
        def _(dve):
            def lower_w(u, slot):
                dve.wait_ge(w_hi_ready, u + 1)
                dve.tensor_tensor(w_lo[:, slot], w_raw[:, slot], w_hi[:, slot].bitcast(F32), ALU.subtract).then_inc(w_lo_ready, 1)

            def copy_mod(g0, i):
                dve.wait_ge(mod_used, KC * i + KC * (g0 + 1))
                dve.tensor_copy(mod_rows, mod_ps).then_inc(mod_copied, 1)

            def store_mod(g0, i):
                dve.wait_ge(mod_turned, i + g0 + 1)
                pairs = lambda ap: ap.rearrange("p (j e) c -> p j e c", e=2)
                src = mod_turned_ps.rearrange("p (e j c) -> p j e c", e=2, j=4)[:, :, :, 0:2]
                bias = params[:, ds(KC * i + (COL_BMOD[g0 // 9] + g0 % 9 * KC), KC)].unsqueeze(2).to_broadcast([P, KC, 2])
                dve.tensor_tensor(pairs(mod[:, ds(KC * i + KC * g0, KC), :]), src, pairs(bias), ALU.add).then_inc(mod_ready, 1)

            def scale_of(k):
                dve.wait_ge(mod_ready, 3 * k + 2)
                dve.tensor_scalar(scale1[:, :, :], mod[:, mod_col(k) + KC:mod_col(k) + 2 * KC, :], 1.0, None,
                                  ALU.add).then_inc(small, 1)

            def modulate(k, o):
                if KC * k + o >= 4:
                    dve.wait_ge(h_lo_ready, KC * k + o - 3)
                dve.wait_ge(x_ready, KC * k + o + 1)
                dve.wait_ge(small, 2 * k + 1)
                for g, a, b in GROUPS:
                    last = dve.tensor_scalar(h_full[:, o % 4, a:b], x[:, o, a:b], scale1[:, o, g:g + 1],
                                             mod[:, mod_col(k) + o, g:g + 1], ALU.mult, ALU.add)
                last.then_inc(h_ready, 1)

            def conv_on_vector(u0):
                dve.wait_ge(pads_ready, 2)
                taps = 0
                for o in range(KC):
                    dve.wait_ge(sigm_ready, o + 1)
                    bias = params[:, COL_B1 + o:COL_B1 + o + 1]
                    dve.scalar_tensor_tensor(glu_seq[:, o, HALF:HALF + TP], bank[o % 2][:, 0:TP], bias, sigm[:, o % 2, 0:TP],
                                             ALU.add, ALU.mult)
                    if o < KC // 2:
                        g3 = lambda ap: ap.rearrange("p (g w) -> p g w", w=GW)
                        dve.scalar_tensor_tensor(glu_row[:, o, :, HALF:HALF + GW], g3(bank[o % 2][:, TP:T]), bias,
                                                 g3(sigm[:, o % 2, TP:T]), ALU.add, ALU.mult).then_inc(glu_ready, 1)
                    else:
                        dve.scalar_tensor_tensor(glu_col[:, o - KC // 2], bank[o % 2][:, TP:T], bias, sigm[:, o % 2, TP:T],
                                                 ALU.add, ALU.mult).then_inc(glu_ready, 1)
                    dve.wait_ge(glu_ready, o + 2)
                    for tap in range(TAPS):
                        w = params[:, COL_DW + tap * KC + o:COL_DW + tap * KC + o + 1]
                        dwb = params[:, COL_DWB + o:COL_DWB + o + 1]
                        src, out = glu_seq[:, o, tap:tap + TP], conv[:, o, 0:TP]
                        if tap == 0:
                            dve.tensor_scalar(out, src, w, dwb, ALU.mult, ALU.add).then_inc(tap_v, 1)
                        else:
                            dve.wait_ge(tap_v, taps)
                            dve.scalar_tensor_tensor(out, src, w, out, ALU.mult, ALU.add).then_inc(tap_v, 1)
                        taps += 1
                        if tap in (7, 23):
                            u = u0 + 2 * o + (tap > 7) + RING
                            lower_w(u, u % RING)
                    if o >= KC // 2:
                        offsets = [0] + [d for d in range(1 - GR, GR) if d]
                        for d in offsets:
                            tap = d + HALF
                            w = params[:, COL_DW + tap * KC + o:COL_DW + tap * KC + o + 1]
                            a, b = max(0, -d), min(GR, GR - d)
                            out = conv[:, o, TP + a * GW:TP + b * GW]
                            src = glu_col[:, o - KC // 2, (a + d) * GW:(b + d) * GW]
                            if d == 0:
                                dve.tensor_scalar(out, src, w, params[:, COL_DWB + o:COL_DWB + o + 1], ALU.mult, ALU.add).then_inc(tap_v, 1)
                            else:
                                dve.wait_ge(tap_v, taps)
                                dve.scalar_tensor_tensor(out, src, w, out, ALU.mult, ALU.add).then_inc(tap_v, 1)
                            taps += 1
                dve.wait_ge(conv_mean, 1)
                for o in range(KC):
                    dve.tensor_tensor(conv[:, o], conv[:, o], mean_ps[:, 0:T], ALU.subtract).then_inc(conv_centred, 1)
                dve.wait_ge(conv_dev, 1)
                dve.reciprocal(rstd[:, :], dev[:, :]).then_inc(conv_rstd, 1)
                dve.wait_ge(conv_rstd, 1)
                for o in range(KC):
                    dve.tensor_tensor(conv[:, o], conv[:, o], rstd[:, :], ALU.mult).then_inc(conv_normed, 1)

            def delta_on_vector(u0):
                with dve.Fori(0, 3 * H // 4) as i:
                    for j in range(4):
                        dve.wait_ge(unit_used, u0 + 4 * i + j + 1)
                        w = [params[:, ds(4 * i + (COL_DNCONV + tap * 3 * H + j), 1)] for tap in range(3)]
                        out, ps, n = lin[:, j % 2], bank[j], 20 * i + 5 * j
                        dve.tensor_scalar(out, ps[:, 0:T], w[1], None, ALU.mult).then_inc(lin_step, 1)
                        dve.wait_ge(lin_step, n + 1)
                        for _, a, b in GROUPS:
                            dve.scalar_tensor_tensor(out[:, a + 1:b], ps[:, a:b - 1], w[0], out[:, a + 1:b], ALU.mult, ALU.add).then_inc(lin_step, 1)
                        for g, a, b in GROUPS:
                            dve.wait_ge(lin_step, n + 2 + g)
                            dve.scalar_tensor_tensor(out[:, a:b - 1], ps[:, a + 1:b], w[2], out[:, a:b - 1], ALU.mult, ALU.add).then_inc(lin_step, 1)
                        lower_w(u0 + 4 * i + j + RING, j)
                        dve.wait_ge(silu_done, 4 * i + j + 1)
                dve.wait_ge(w_ab_ready, 1)
                dve.tensor_tensor(w_ab_lo[:, :, :], w_ab[:, :, :], w_ab_hi[:, :, :].bitcast(F32), ALU.subtract).then_inc(w_ab_ready, 1)
                dve.wait_ge(qk_norm_ready, 1)
                dve.reciprocal(qk_norm[:, :], qk_norm[:, :]).then_inc(qk_norm_ready, 1)
                dve.wait_ge(qk_norm_ready, 2)
                dve.tensor_copy(qk_rnorm_hi[:, :], qk_norm[:, :]).then_inc(qk_norm_ready, 1)
                dve.wait_ge(qk_norm_ready, 3)
                dve.tensor_tensor(qk_rnorm_lo[:, :], qk_norm[:, :], qk_rnorm_hi[:, :].bitcast(F32), ALU.subtract).then_inc(qk_norm_ready, 1)
                dve.wait_ge(ab_ready, 1)
                dve.tensor_copy(ab[:, :, :], bank[5][:, 0:12 * H].rearrange("p (t c) -> p t c", t=NT)).then_inc(gate_v, 1)
                dve.wait_ge(gate_v, 1)
                dve.tensor_tensor(pre[:, :, :], ab[:, :, 0:2 * H], dt_a[:, 0:1, :].to_broadcast([P, NT, 2 * H]), ALU.add).then_inc(gate_v, 1)
                dve.wait_ge(gate_v, 2)
                dve.tensor_scalar(pos[:, :, :], pre[:, :, :], 0.0, None, ALU.max).then_inc(gate_v, 1)
                dve.wait_ge(gate_v, 3)
                dve.wait_ge(gate_a, 4)
                dve.tensor_tensor(pos[:, :, :], pos[:, :, :], soft[:, :, :], ALU.add).then_inc(gate_v, 1)
                dve.wait_ge(gate_v, 4)
                dve.scalar_tensor_tensor(log_a[:, :, :], pos[:, :, :], -1.0, exp_a[:, 0:1, :].to_broadcast([P, NT, 2 * H]),
                                         ALU.mult, ALU.mult).then_inc(gate_v, 1)
                dve.wait_ge(gate_v, 5)
                dve.wait_ge(dn_consts, DN_CONSTS)
                dve.wait_ge(gate_a, GATE_A_BETA)
                for d in range(2):
                    dve.tensor_copy(row_src[:, :, d, d * H:(d + 1) * H], log_a[:, :, d * H:(d + 1) * H]).then_inc(gate_v, 1)
                dve.tensor_copy(row_src[:, :, 2, 2 * H:4 * H], beta[:, :, :]).then_inc(gate_v, 1)
                with dve.Fori(0, H // 4) as i:
                    for j in range(4):
                        lower_w(u0 + 3 * H + 4 * i + j + RING, j)
                dve.wait_ge(gate_t, 1)
                dve.tensor_copy(g_col[:, :, :], bank[5][:, 0:6 * H].rearrange("p (t c) -> p t c", t=NT)).then_inc(gate_v, 1)
                dve.tensor_copy(tot[:, :, :], bank[6][:, 0:6 * H].rearrange("p (t c) -> p t c", t=NT)).then_inc(gate_v, 1)
                dve.wait_ge(gate_v, 10)
                dve.tensor_tensor(end_decay[:, :, :], tot[:, :, :], g_col[:, :, :], ALU.subtract).then_inc(gate_v, 1)
                dve.wait_ge(gate_t, 2)
                dve.tensor_copy(rows_hi[:, :], bank[0][0:4 * H, 0:T]).then_inc(gate_v, 1)
                dve.wait_ge(gate_v, 12)
                dve.tensor_tensor(rows_lo[:, :], bank[0][0:4 * H, 0:T], rows_hi[:, :].bitcast(F32), ALU.subtract).then_inc(gate_v, 1)
                dve.wait_ge(gate_a, 8)
                dve.scalar_tensor_tensor(minus_beta_g[:, :, :], beta[:, :, :], -1.0, g_decay[:, :, :], ALU.mult, ALU.mult).then_inc(gate_v, 1)
                dve.wait_ge(gate_v, 14)

                def select(h, ahead):
                    one = lambda rows, n: (ident[0:rows, ahead:ahead + n * H].rearrange("p (n c) -> p n c", c=H)[:, :, ds(h, 1)]
                                           .to_broadcast([rows, n, P]))
                    dve.tensor_copy(sel_qk[:, :, :], one(2 * H, 2))
                    dve.tensor_copy(sel_row[:, :, :], one(4 * H, 4)).then_inc(sel_ready, 1)

                select(0, 0)
                tiles = lambda ap: ap[:, 0:T].rearrange("p (t c) -> p t c", c=P)
                with dve.Fori(0, H) as h:
                    dve.wait_ge(norm_spread, h + 1)
                    dve.tensor_tensor(k_head[:, :].unsqueeze(1), qk[:, ds(h + H, 1)], bank[0][:, 0:T].unsqueeze(1), ALU.mult).then_inc(qk_ready, 1)
                    dve.tensor_tensor(q_head[:, :].unsqueeze(1), qk[:, ds(h, 1)], bank[1][:, 0:T].unsqueeze(1), ALU.mult).then_inc(qk_ready, 1)
                    dve.wait_ge(rows_spread, h + 1)
                    for d in range(2):
                        for t in range(NT):
                            last = dve.scalar_tensor_tensor(qk_decay[:, d, t], bank[2 + d][:, t * P:(t + 1) * P], g_col[:, t, ds(h + d * H, 1)],
                                                            never[:, d], ALU.subtract, ALU.add)
                        last.then_inc(diff_ready, 1)
                    dve.wait_ge(kk_ready, h + 1)
                    for d in range(2):
                        dve.wait_ge(decay_ready, 4 * h + d + 1)
                        dve.scalar_tensor_tensor(decay[:, d], decay[:, d], -1.0, tiles(bank[6]), ALU.mult, ALU.mult).then_inc(a_step, 1)
                    for d in range(2):
                        dve.wait_ge(a_step, 4 * h + d + 1)
                        dve.tensor_tensor(decay[:, d], decay[:, d], tiles(bank[4 + d]), ALU.mult).then_inc(a_step, 1)
                    for n in range(LEVELS):
                        for d in range(2):
                            here = every_other(masks[:, 2 * n + d], n, d).unsqueeze(1).to_broadcast([P, NT, P >> (n + 1), 1 << n])
                            there = every_other(masks[:, 2 * n + 1 - d], n, 1 - d).unsqueeze(1).to_broadcast([P, NT, P >> (n + 1), 1 << n])
                            inv_here, inv_there = every_other(inv[:, d], n, d), every_other(inv_t[:, d], n, 1 - d)
                            if n == 0:
                                dve.wait_ge(inv_begun, h + 1)
                                dve.wait_ge(a_step, 4 * h + 2 + d + 1)
                                dve.wait_ge(p_ready, h * (2 * LEVELS) + d + 1)
                                dve.memset(carrier[:, 2 * n + d:2 * n + d + 1], 0.0)
                                dve.copy_predicated(inv_there, there, every_other(decay[:, d], n, 1 - d))
                                dve.copy_predicated(inv_here, here, every_other(tiles(bank[d]), n, d)).then_inc(t_joined, 1)
                            else:
                                dve.wait_ge(t_ready, h * (2 * (LEVELS - 1)) + 2 * (n - 1) + d + 1)
                                dve.memset(carrier[:, 2 * n + d:2 * n + d + 1], 0.0)
                                last = dve.copy_predicated(inv_there, there, every_other(tiles(bank[4 + d]), n, 1 - d))
                                last.then_inc(t_joined, 1)
                        if n == 1:
                            dve.wait_ge(k_turned, h + 1)
                            for d in range(2):
                                for k in range(2):
                                    t = SCAN[d][k]
                                    last = dve.tensor_scalar(k_decay[:, d, k], bank[6][:, t * P:(t + 1) * P], end_decay[:, t, ds(h + d * H, 1)],
                                                             None, ALU.mult)
                            last.then_inc(k_decay_ready, 1)
                        if n == 2:
                            for d in range(2):
                                dve.wait_ge(decay_ready, 4 * h + 3 + d)
                                dve.tensor_tensor(qk_decay[:, d], qk_decay[:, d], tiles(bank[7]), ALU.mult)
                            for d in range(2):
                                dve.wait_ge(q_exp_ready, 2 * h + d + 1)
                                dve.tensor_tensor(q_decay[:, d, TP:T], q_decay[:, d, TP:T], q_head[:, TP:T], ALU.mult).then_inc(q_decay_ready, 1)
                        if n == 3:
                            select(h, 1)
                    dve.wait_ge(v_beta_ready, h + 1)
                    for k in (1, 2):
                        for d in range(2):
                            t = SCAN[d][k]
                            dve.wait_ge(ks_ready, 4 * h + 2 * (k - 1) + d + 1)
                            dve.scalar_tensor_tensor(v_beta[:, d, t], bank[d][:, 0:P], minus_beta_g[:, t, ds(h + d * H, 1)],
                                                     v_beta[:, d, t], ALU.mult, ALU.add).then_inc(x_set, 1)
                        if k == 1:
                            for d in range(2):
                                dve.wait_ge(s_added, 4 * h + 2 + d + 1)
                                dve.scalar_tensor_tensor(s_new[:, d], s_old[:, d], tot_decay[:, SCAN[d][1], ds(h + d * H, 1)],
                                                         bank[4 + d][:, 0:P], ALU.mult, ALU.add).then_inc(s_updated, 1)
                dve.wait_ge(head_done, H + 1)
                dve.wait_ge(o_norm_ready, 1)
                dve.reciprocal(qk_norm[0:H, :], qk_norm[0:H, :]).then_inc(o_rnorm_ready, 1)
                for h in range(H):
                    dve.wait_ge(o_squared, h + 1)
                    dve.scalar_tensor_tensor(o_all[:, h], o_all[:, h], norm_g[:, :], z[:, h], ALU.mult, ALU.mult).then_inc(o_gated, 1)
                    dve.wait_ge(o_gated, 2 * h + 1)
                    dve.wait_ge(o_spread, h + 1)
                    if h >= 4:
                        dve.wait_ge(o_lo, h - 3)
                    dve.tensor_tensor(h_full[:, h % 4], o_all[:, h], bank[h % 2][:, 0:T], ALU.mult).then_inc(o_gated, 1)

            for n, started in enumerate((act_ready, r_ready, glu_ready)):
                dve.memset(begun[:, n:n + 1], 0.0).then_inc(started, 1)
            for t in range(5):
                dve.wait_ge(turned, t + 1)
                dve.tensor_copy(params[:, t * P:(t + 1) * P], bank[t % 4][:, 0:P]).then_inc(table_out, 1)
            for o in range(KC):
                dve.wait_ge(turned, 5 + o + 1)
                dve.tensor_copy(x[:, o], bank[o % 2][:, 0:T]).then_inc(x_ready, 1)
            for g in range(MOD_FIRST):
                copy_mod(g, 0)
                store_mod(g, 0)
            for j in range(RING):
                lower_w(j, j)
            scale_of(0)
            for o in range(KC):
                modulate(0, o)

            for s in range(stages):
                u0 = UNIT0[s]
                if is_ffn[s]:
                    f0 = FC * ffns[s]
                    def in_pair(pair, beside=None):
                        for q in range(2):
                            if q and beside is not None:
                                copy_mod(mod_in_chunk[s], beside)
                            dve.wait_ge(silu_ready, f0 + 2 * pair + q + 1)
                            dve.tensor_tensor(act_full[:, q], silu_g[:, q], bank[q][:, 0:T], ALU.mult).then_inc(act_ready, 1)
                            dve.wait_ge(act_hi_ready, f0 + 2 * pair + q + 1)
                            dve.tensor_tensor(act_lo[:, ds(2 * pair + q, 1)], act_full[:, ds(q, 1)],
                                              act_hi[:, ds(2 * pair + q, 1)].bitcast(F32), ALU.subtract).then_inc(act_lo_ready, 1)
                            for j in range(2):
                                lower_w(u0 + 4 * pair + 2 * q + j + RING, 2 * q + j)

                    if s in MOD_BESIDE_IN:
                        with dve.Fori(0, MOD_BESIDE_IN[s]) as i:
                            in_pair(2 * i)
                            in_pair(2 * i + 1, i)
                            store_mod(mod_in_chunk[s], i)
                        for pair in range(2 * MOD_BESIDE_IN[s], FC // 2):
                            in_pair(pair)
                    else:
                        with dve.Fori(0, FC // 2) as i:
                            in_pair(i)
                elif s == 1:
                    conv_on_vector(u0)
                elif s == 4:
                    delta_on_vector(u0)
                dve.wait_ge(mod_ready, 3 * s + 3)
                dve.tensor_scalar(gate[:, :, :], mod[:, mod_col(s) + 2 * KC:mod_col(s) + 3 * KC, :],
                                  0.5 if is_ffn[s] else 1.0, None, ALU.mult).then_inc(small, 1)
                dve.wait_ge(small, 2 * s + 2)
                dve.wait_ge(r_scaled, s + 1)

                def add_gated(done, count, o, ps):
                    dve.wait_ge(done, count)
                    for g, a, b in GROUPS:
                        last = dve.scalar_tensor_tensor(r[:, ds(o, 1), a:b], ps[:, a:b].unsqueeze(1), gate[:, ds(o, 1), g:g + 1],
                                                        r[:, ds(o, 1), a:b], ALU.mult, ALU.add)
                    last.then_inc(r_ready, 1)

                if is_ffn[s]:
                    v0 = u0 + 2 * FC
                    def out_body(i, units):
                        for q in range(12):
                            if q % 3 == 2:
                                add_gated(unit_used, v0 + 12 * i + q + 1, 4 * i + q // 3, bank[(q // 3) % 2])
                            if q < units:
                                lower_w(v0 + 12 * i + q + RING, q % RING)
                            if s in MOD_BESIDE_OUT and q == KC:
                                copy_mod(mod_out_chunk[s], i)
                            if s in MOD_BESIDE_OUT and q == KC + 2:
                                store_mod(mod_out_chunk[s], i)
                    if s == stages - 1:
                        out_body(0, 12)
                        out_body(1, 12 - RING)
                    else:
                        with dve.Fori(0, 2) as i:
                            out_body(i, 12)

                elif s == 1:
                    for o in range(KC):
                        add_gated(y_ready, o + 1, o, y_biased[:, o % 2])
                        if u0 + 2 * KC + o + RING < LAST_UNIT:
                            lower_w(u0 + 2 * KC + o + RING, o % RING)
                elif s == 4:
                    for o in range(KC):
                        add_gated(unit_used, u0 + DN_BLOCKS + o + 1, o, bank[2 + o % 2])
                        if u0 + DN_BLOCKS + o + RING < LAST_UNIT:
                            lower_w(u0 + DN_BLOCKS + o + RING, o % RING)
                dve.wait_ge(mean_ready, s + 1)
                for o in range(KC):
                    dve.tensor_tensor(r[:, o], r[:, o], mean_ps[:, 0:T], ALU.subtract).then_inc(centred, 1)
                dve.wait_ge(dev_ready, s + 1)
                dve.reciprocal(rstd[:, :], dev[:, :]).then_inc(rstd_ready, 1)
                if s + 1 < stages:
                    scale_of(s + 1)
                dve.wait_ge(rstd_ready, s + 1)
                dve.wait_ge(squared, KC * (s + 1))
                for o in range(KC + 2):
                    if o < KC:
                        dve.tensor_tensor(r[:, o], r[:, o], rstd[:, :], ALU.mult).then_inc(normed, 1)
                    if o >= 2 and s + 1 < stages:
                        modulate(s + 1, o - 2)

            for t in range(NT):
                for half in range(2):
                    dve.wait_ge(turned, 5 + KC + 2 * t + half + 1)
                    dve.tensor_copy(x_rows[:, t, 512 * half:512 * half + 512], bank[(2 * t + half) % 4][:, :]).then_inc(rows_ready, 1)

        @block.tensor
        def _(pe):
            def split_product(ps, w_slot, k, a_hi, a_lo, start, stop):
                pe.matmul(ps, w_hi[:, w_slot, k], a_hi, start=start, stop=False)
                pe.matmul(ps, w_hi[:, w_slot, k], a_lo, start=False, stop=False)
                return pe.matmul(ps, w_lo[:, w_slot, k], a_hi, start=False, stop=stop)

            def unit(u, slot, ps, hi, lo, chunks, first=True, last=True):
                pe.wait_ge(w_lo_ready, u + 1)
                for n, k in enumerate(chunks):
                    mm = split_product(ps, slot, n, hi[:, k], lo[:, k], first and n == 0, last and n == len(chunks) - 1)
                mm.then_inc(unit_used, 1)

            def mod_slice(g0, i, k):
                if k == 0 and not (isinstance(i, int) and g0 + i == 0):
                    pe.wait_ge(mod_copied, i + g0)
                pe.wait_ge(mod_in[k % 4], i * 32 + (32 * g0 + 16 * (k // 4 + 1)))
                for j in range(4):
                    mm = pe.matmul(mod_ps[MOD_COLS * j:MOD_COLS * (j + 1), :], cond[:, k, :], mod_raw[:, k % 4, MW * j:MW * (j + 1)],
                                   start=(k == 0), stop=(k == KC - 1))
                mm.then_inc(mod_used, 1)

            def turn_mod(g0, i):
                if not (isinstance(i, int) and g0 + i == 0):
                    pe.wait_ge(mod_ready, i + g0)
                pe.wait_ge(mod_copied, i + g0 + 1)
                for e in range(2):
                    mm = pe.transpose(mod_turned_ps[:, e * P:(e + 1) * P], mod_rows[:, e * P:(e + 1) * P], ident[:, :])
                mm.then_inc(mod_turned, 1)

            def delta_on_tensor(u0):
                with pe.Fori(0, 2 * H // 4) as i:
                    for j in range(4):
                        unit(u0 + 4 * i + j, j, bank[j][:, 0:T], h_hi, h_lo, range(KC))
                        if j:
                            pe.wait_ge(lin_step, 20 * i + 5 * j)
                for b in range(H + 1):
                    if b < H:
                        n = 2 * H + b
                        unit(u0 + n, n % RING, bank[n % 4][:, 0:T], h_hi, h_lo, range(KC))
                        pe.wait_ge(lin_step, 5 * n)
                    if b:
                        pe.wait_ge(silu_done, 2 * H + b)
                        if b >= 3:
                            pe.wait_ge(v_stored, b - 2)
                        for t in range(NT):
                            mm = pe.transpose(bank[6 + (b - 1) % 2][:, t * P:(t + 1) * P], v_silu[:, (b - 1) % 2, t * P:(t + 1) * P], ident[:, :])
                        mm.then_inc(v_turned, 1)
                pe.wait_ge(dn_consts, DN_CONSTS)
                for b in range(2 * H):
                    pe.wait_ge(qk_squared, b + 1)
                    pe.matmul(bank[4][0:2 * H, 0:T], one_hot[:, 2 * H - 1 - b:4 * H - 1 - b], square[:, b % 4],
                              start=(b == 0), stop=(b == 2 * H - 1)).then_inc(qk_summed, 1)
                pe.wait_ge(w_ab_ready, 2)
                for t in range(NT):
                    out = bank[5][:, t * 4 * H:(t + 1) * 4 * H]
                    for k in range(KC):
                        a_hi, a_lo = h_hi[:, k, t * P:(t + 1) * P], h_lo[:, k, t * P:(t + 1) * P]
                        pe.matmul(out, a_hi, w_ab_hi[:, k], start=(k == 0), stop=False)
                        pe.matmul(out, a_hi, w_ab_lo[:, k], start=False, stop=False)
                        mm = pe.matmul(out, a_lo, w_ab_hi[:, k], start=False, stop=(k == KC - 1))
                mm.then_inc(ab_ready, 1)
                pe.wait_ge(lin_step, 15 * H)
                with pe.Fori(0, H // 4) as i:
                    for j in range(4):
                        unit(u0 + 3 * H + 4 * i + j, j, bank[j][:, 0:T], h_hi, h_lo, range(KC))
                        if j:
                            pe.wait_ge(silu_done, 4 * i + (3 * H + j))
                pe.wait_ge(gate_v, 5)
                pe.wait_ge(v_stored, H)
                cols = bank[5][:, 0:6 * H].rearrange("p (t c) -> p t c", t=NT)
                for d in range(2):
                    pe.matmul(cols[:, :, d * H:(d + 1) * H], tri[:, d], log_a[:, :, d * H:(d + 1) * H], start=True, stop=True)
                pe.matmul(bank[6][:, 0:6 * H], ones[:, :], log_a[:, :, :].rearrange("p t c -> p (t c)"), start=True, stop=True).then_inc(gate_t, 1)
                pe.wait_ge(silu_done, 4 * H)
                pe.wait_ge(gate_a, GATE_A_BETA)
                pe.wait_ge(gate_v, 8)
                for t in range(NT):
                    for n, rhs in enumerate((tri[:, 0], tri[:, 1], ident[:, :])):
                        mm = pe.matmul(bank[0][0:4 * H, t * P:(t + 1) * P], row_src[:, t, n], rhs, start=(n == 0), stop=(n == 2))
                mm.then_inc(gate_t, 1)
                pe.wait_ge(gate_v, 14)
                pe.wait_ge(qk_norm_ready, 4)

                def spread(ps, sel, hi, lo):
                    pe.matmul(ps[:, 0:T], sel, hi, start=True, stop=False)
                    return pe.matmul(ps[:, 0:T], sel, lo, start=False, stop=True)

                def spread_norms():
                    spread(bank[0], sel_qk[:, 1], qk_rnorm_hi[:, :], qk_rnorm_lo[:, :])
                    spread(bank[1], sel_qk[:, 0], qk_rnorm_hi[:, :], qk_rnorm_lo[:, :]).then_inc(norm_spread, 1)

                def spread_rows():
                    for n in range(4):
                        mm = spread(bank[2 + n], sel_row[:, n], rows_hi[:, :], rows_lo[:, :])
                    mm.then_inc(rows_spread, 1)

                pe.wait_ge(sel_ready, 1)
                spread_norms()
                spread_rows()
                with pe.Fori(0, H) as h:
                    pe.wait_ge(qk_ready, 2 * h + 2)
                    pe.wait_ge(head_done, h + 1)
                    for ps, m in ((bank[6], k_head), (bank[7], q_head)):
                        for t in range(NT):
                            mm = pe.matmul(ps[:, t * P:(t + 1) * P], k_head[:, t * P:(t + 1) * P], m[:, t * P:(t + 1) * P], start=True, stop=True)
                    mm.then_inc(kk_ready, 1)
                    pe.wait_ge(inv_begun, h + 1)
                    for n in range(LEVELS):
                        for d in range(2):
                            if n == 0:
                                pe.wait_ge(a_step, 4 * h + 2 + d + 1)
                            elif n == 1:
                                pe.wait_ge(t_joined, h * (2 * LEVELS) + d + 1)
                            else:
                                pe.wait_ge(inv_copied, h * (2 * (LEVELS - 2)) + 2 * (n - 2) + d + 1)
                            for t in range(NT):
                                if n == 0:
                                    mm = pe.transpose(bank[d][:, t * P:(t + 1) * P], decay[:, d, t], ident[:, :])
                                else:
                                    mm = pe.matmul(bank[d][:, t * P:(t + 1) * P], decay[:, d, t], inv[:, d, t], start=True, stop=True)
                            mm.then_inc(p_ready, 1)
                        if n == 0:
                            for t in range(NT):
                                mm = pe.transpose(bank[6][:, t * P:(t + 1) * P], k_head[:, t * P:(t + 1) * P], ident[:, :])
                            mm.then_inc(k_turned, 1)
                        if n:
                            for d in range(2):
                                pe.wait_ge(p_copied, h * (2 * (LEVELS - 1)) + 2 * (n - 1) + d + 1)
                                for t in range(NT):
                                    mm = pe.matmul(bank[4 + d][:, t * P:(t + 1) * P], step_p[:, d, t], inv_t[:, d, t], start=True, stop=True)
                                mm.then_inc(t_ready, 1)
                        if 0 < n < LEVELS - 1:
                            for d in range(2):
                                pe.wait_ge(t_joined, h * (2 * LEVELS) + 2 * n + d + 1)
                                if n == 1:
                                    pe.wait_ge(q_exp_ready, 2 * h + d + 1)
                                for t in range(NT):
                                    mm = pe.transpose(bank[2 + d][:, t * P:(t + 1) * P], inv_t[:, d, t], ident[:, :])
                                mm.then_inc(inv_turned, 1)
                    pe.wait_ge(v_beta_ready, h + 1)
                    pe.wait_ge(k_decay_ready, h + 1)
                    pe.wait_ge(q_decay_ready, 2 * h + 2)
                    for k in range(NT):
                        for d in range(2):
                            t = SCAN[d][k]
                            if k == 0:
                                pe.wait_ge(t_joined, (h + 1) * (2 * LEVELS) - 1 + d)
                            else:
                                pe.wait_ge(x_set, 4 * h + 2 * (k - 1) + d + 1)
                            pe.matmul(bank[2 + d][:, 0:P], inv_t[:, d, t], v_beta[:, d, t], start=True, stop=True).then_inc(u_ready, 1)
                        if k == NT - 1:
                            pe.wait_ge(sel_ready, h + 2)
                            spread_norms()
                        if k == 0:
                            pe.wait_ge(state_in, 16 * h + 16)
                            for d in range(2):
                                t = SCAN[d][1]
                                pe.matmul(bank[d][:, 0:P], k_head[:, t * P:(t + 1) * P], s_old[:, d], start=True, stop=True).then_inc(ks_ready, 1)
                        for d in range(2):
                            t = SCAN[d][k]
                            pe.wait_ge(u_copied, 6 * h + 2 * k + d + 1)
                            if k < 2:
                                if k:
                                    pe.wait_ge(s_stored, 2 * h + d + 1)
                                pe.matmul(bank[4 + d][:, 0:P], k_decay[:, d, k], u_sb[:, d], start=True, stop=True).then_inc(s_added, 1)
                            out = bank[6][:, t * P:(t + 1) * P]
                            if k:
                                pe.matmul(out, (s_old, s_new)[k - 1][:, d], q_decay[:, d, t * P:(t + 1) * P],
                                          start=False, stop=False, skip_group_check=True)
                            pe.matmul(out, u_sb[:, d], qk_decay[:, d, t], start=(k == 0 and d == 0), stop=False,
                                      skip_group_check=True).then_inc(o_added, 1)
                        if k == 1:
                            for d in range(2):
                                t = SCAN[d][2]
                                pe.wait_ge(s_updated, 2 * h + d + 1)
                                pe.matmul(bank[d][:, 0:P], k_head[:, t * P:(t + 1) * P], s_new[:, d], start=True, stop=True).then_inc(ks_ready, 1)
                    spread_rows()
                for h in range(H):
                    pe.wait_ge(o_squared, h + 1)
                    pe.matmul(bank[4][0:H, 0:T], one_hot[:, 2 * H - 1 - h:3 * H - 1 - h], square[:, h % 4],
                              start=(h == 0), stop=(h == H - 1)).then_inc(o_summed, 1)
                pe.wait_ge(o_rnorm_ready, 1)
                for h in range(H):
                    if h >= 2:
                        pe.wait_ge(o_gated, 2 * (h - 1))
                    pe.matmul(bank[h % 2][:, 0:T], ident[0:H, h:h + 1].to_broadcast([H, P]), qk_norm[0:H, :],
                              start=True, stop=True).then_inc(o_spread, 1)
                pe.wait_ge(o_lo, H)
                for o in range(KC):
                    if o >= 2:
                        pe.wait_ge(r_ready, KC * 4 + o)
                    unit(u0 + DN_BLOCKS + o, o % RING, bank[2 + o % 2][:, 0:T], h_hi, h_lo, range(KC))

            pe.wait_ge(consts, 6)
            loads = (2, 2, 1, 2, 7)
            for t in range(5):
                pe.wait_ge(table_in[t], 16 * loads[t])
                if t == 4:
                    pe.wait_ge(table_out, 1)
                pe.transpose(bank[t % 4][:, 0:P], table[:, t, :], ident[:, :]).then_inc(turned, 1)
            pe.wait_ge(table_out, 5)
            for t in range(NT):
                pe.wait_ge(x_in[t], 16)
            for o in range(KC):
                if o >= 2:
                    pe.wait_ge(x_ready, o - 1)
                for t in range(NT):
                    mm = pe.transpose(bank[o % 2][:, t * P:(t + 1) * P], x_rows[:, t, o * P:(o + 1) * P], ident[:, :])
                mm.then_inc(turned, 1)
            pe.wait_ge(cond_ready, 2)
            for g in range(MOD_FIRST):
                for k in range(KC):
                    mod_slice(g, 0, k)
                turn_mod(g, 0)

            for s in range(stages):
                u0 = UNIT0[s]
                pe.wait_ge(h_lo_ready, KC * (s + 1))
                if is_ffn[s]:
                    f0 = FC * ffns[s]
                    def in_pair(pair, eighth=0, beside=None):
                        for q in range(2):
                            for j, ps in ((2 * q, bank[q]), (2 * q + 1, bank[2 + q])):
                                unit(u0 + 4 * pair + j, j, ps[:, 0:T], h_hi, h_lo, range(KC))
                                if beside is not None:
                                    for k in in_slices(eighth + j):
                                        mod_slice(mod_in_chunk[s], beside, k)
                            pe.wait_ge(act_ready, f0 + 2 * pair + q + 1)

                    if s in MOD_BESIDE_IN:
                        with pe.Fori(0, MOD_BESIDE_IN[s]) as i:
                            in_pair(2 * i, 0, i)
                            in_pair(2 * i + 1, 4, i)
                            turn_mod(mod_in_chunk[s], i)
                        for pair in range(2 * MOD_BESIDE_IN[s], FC // 2):
                            in_pair(pair)
                    else:
                        with pe.Fori(0, FC // 2) as i:
                            in_pair(i)
                    v0 = u0 + 2 * FC
                    with pe.Fori(0, 2) as i:
                        for q in range(12):
                            a, b = FFN_THIRDS[q % 3]
                            pe.wait_ge(act_lo_ready, f0 + b)
                            unit(v0 + 12 * i + q, q % RING, bank[(q // 3) % 2][:, 0:T], act_hi, act_lo, range(a, b),
                                 first=(a == 0), last=(b == FC))
                            if q % 3 == 2:
                                pe.wait_ge(r_ready, KC * s + 4 * i + q // 3 + 1)
                            for k in out_slices(s, q):
                                mod_slice(mod_out_chunk[s], i, k)
                            if s in MOD_BESIDE_OUT and q == KC + 1:
                                turn_mod(mod_out_chunk[s], i)
                elif s == 1:
                    with pe.Fori(0, KC // 2) as i:
                        for q in range(2):
                            for j, ps in ((2 * q, bank[q]), (2 * q + 1, bank[2 + q])):
                                unit(u0 + 4 * i + j, j, ps[:, 0:T], h_hi, h_lo, range(KC))
                            pe.wait_ge(glu_ready, 2 * i + q + 1)
                    for o in range(KC):
                        pe.wait_ge(tap_v, TAPS * (o + 1) + (2 * GR - 1) * max(0, o + 1 - KC // 2))
                        if o < KC // 2:
                            pe.wait_ge(tap_g, (TAPS - 1) * (o + 1))
                        mm = pe.matmul(mean_ps[:, 0:T], mean_w[:, :], conv[:, o], start=(o == 0), stop=(o == KC - 1))
                    mm.then_inc(conv_mean, 1)
                    for o in range(KC):
                        pe.wait_ge(conv_squared, o + 1)
                        pe.matmul(var_ps[:, 0:T], mean_w[:, :], square[:, o % 4], start=(o == 0), stop=(o == KC - 1)).then_inc(conv_var, 1)
                    pe.wait_ge(conv_lo, KC)
                    for o in range(KC):
                        if o:
                            pe.wait_ge(r_ready, KC * s + o)
                            pe.wait_ge(y_ready, o)
                        unit(u0 + 2 * KC + o, o % RING, bank[o % 2][:, 0:T], h_hi, h_lo, range(KC))
                elif s == 4:
                    delta_on_tensor(u0)
                pe.wait_ge(r_summed, (KC + 1) * (s + 1))
                pe.matmul(mean_ps[:, 0:T], mean_w[:, :], r_sum[:, :], start=True, stop=True).then_inc(mean_ready, 1)
                for o in range(KC):
                    pe.wait_ge(squared, KC * s + o + 1)
                    pe.matmul(var_ps[:, 0:T], mean_w[:, :], square[:, o % 4], start=(o == 0), stop=(o == KC - 1)).then_inc(var_added, 1)

            pe.wait_ge(x_ready, KC * (stages + 1))
            for t in range(NT):
                for half in range(2):
                    n = 2 * t + half
                    if n >= 4:
                        pe.wait_ge(rows_ready, n - 3)
                    for o in range(4):
                        mm = pe.transpose(bank[n % 4][:, o * P:(o + 1) * P], x[:, 4 * half + o, t * P:(t + 1) * P], ident[:, :])
                    mm.then_inc(turned, 1)


_INS = ['x_prompt', 'x_sample', 'state_delta', 'c', 'c_ctx', 'w_mod', 'b_mod', 'ln_g', 'ln_b', 'ffn_w_in', 'ffn_w_out',
        'cv_w1', 'cv_b1', 'cv_dw', 'cv_dwb', 'cv_ln_g', 'cv_ln_b', 'cv_w2', 'cv_b2',
        'dn_w_in', 'dn_conv', 'dn_a_log', 'dn_dt_bias', 'dn_norm_g', 'dn_w_out']
_OUTS = [(1, TP, D), (1, TS, D), (1, 1, 2, H, P, P)]


def kernel(**inputs):
    import concourse.bacc as bacc
    from concourse.bass_utils import run_bass_kernel_spmd

    nc = bacc.Bacc("TRN2", target_bir_lowering=False, num_devices=1)
    arrays, args = {}, []
    for name in _INS:
        a = np.ascontiguousarray(inputs[name])
        arrays["in_" + name] = a
        args.append(nc.dram_tensor("in_" + name, a.shape, mybir.dt.from_np(a.dtype), kind="ExternalInput").ap())
    for i, shape in enumerate(_OUTS):
        args.append(nc.dram_tensor(f"out_{i}", shape, F32, kind="ExternalOutput").ap())
    program(nc, *args)
    res = run_bass_kernel_spmd(nc, [arrays], core_ids=[0])
    return tuple(res.results[0][f"out_{i}"] for i in range(len(_OUTS)))
```

```python
import numpy as np
import concourse.bass as bass
from concourse import mybir

F32 = mybir.dt.float32
F32R = mybir.dt.float32r
I32 = mybir.dt.int32
ACT = mybir.ActivationFunctionType
ALU = mybir.AluOpType
ds = bass.ds

P = 128
D = 1024
KC = D // P
DEPTH = 2
DFF = 2816
FC = DFF // P
TP, TS = 128, 256
T = TP + TS
NT = T // P
GW = 64
TAPS = 31
H = 8
ALPHA = (2.0 * DEPTH) ** 0.25
LN_EPS = 1e-5
GROUPS = ((0, 0, TP), (1, TP, T))
RING = 4

DN_BLOCKS = 32
UNITS = (2 * FC + 3 * KC, 2 * KC + KC, 2 * FC + 3 * KC, 2 * FC + 3 * KC, DN_BLOCKS + KC, 2 * FC + 3 * KC)
UNIT0 = tuple(sum(UNITS[:s]) for s in range(6))
FFN_THIRDS = ((0, 8), (8, 15), (15, 22))

COL_BMOD = (0, P)
COL_LNG, COL_LNB = 72, P + 72
COL_DW = 2 * P
COL_C = 3 * P + 120
COL_DNCONV = 4 * P
COL_B1, COL_DWB, COL_CLNG, COL_CLNB, COL_B2, COL_CCTX = (4 * P + n for n in (72, 88, 96, 104, 112, 120))

MOD_FIRST = 2
MOD_BESIDE_IN = {0: 5, 2: 5}
MOD_BESIDE_OUT = {0: 2, 2: 2, 3: 2}
MOD_COLS = 32
MW = D // 4


def program(nc, x_prompt, x_sample, state_delta, c, c_ctx, w_mod, b_mod, ln_g, ln_b, ffn_w_in, ffn_w_out,
            cv_w1, cv_b1, cv_dw, cv_dwb, cv_ln_g, cv_ln_b, cv_w2, cv_b2,
            dn_w_in, dn_conv, dn_a_log, dn_dt_bias, dn_norm_g, dn_w_out,
            y_prompt, y_sample, new_state, stages=6):
    from contextlib import ExitStack, contextmanager
    ctx = ExitStack()
    with ctx:
        def sb(name, shape, dt=F32, where=ctx):
            return where.enter_context(nc.sbuf_tensor(name, shape, dt))

        def sem(name):
            return ctx.enter_context(nc.semaphore(name))

        x = sb("x", [P, KC, T])
        r = sb("r", [P, KC, T])
        h_hi = sb("h_hi", [P, KC, T], F32R)
        h_lo = sb("h_lo", [P, KC, T], F32R)
        h_full = sb("h_full", [P, 4, T])
        w_raw = sb("w_raw", [P, RING, 8, P])
        w_hi = sb("w_hi", [P, RING, 8, P], F32R)
        w_lo = sb("w_lo", [P, RING, 8, P], F32R)
        mod = sb("mod", [P, DEPTH * 72, 2])
        scale1 = sb("scale1", [P, KC, 2])
        h_scale = sb("h_scale", [P, KC, 2])
        h_shift = sb("h_shift", [P, KC, 2])
        gate = sb("gate", [P, KC, 2])
        params = sb("params", [P, 5 * P])
        cond = sb("cond", [P, KC, MOD_COLS])
        ident = sb("ident", [P, P])
        mean_w = sb("mean_w", [P, P])
        eps = sb("eps", [P, 1])
        begun = sb("begun", [P, 4])
        r_sum = sb("r_sum", [P, T])
        square = sb("square", [P, 4, T])
        k_head = sb("k_head", [P, T])
        rstd = sb("rstd", [P, T])

        with ExitStack() as region:
            mod_raw = sb("mod_raw", [P, 4, D], F32, region)
        with ExitStack() as region:
            qk_decay = sb("qk_decay", [P, 2, NT, P], F32, region)
            step_p = sb("step_p", [P, 2, NT, P], F32, region)
            v_beta = sb("v_beta", [P, 2, NT, P], F32, region)
            k_decay = sb("k_decay", [P, 2, 2, P], F32, region)
            u_sb = sb("u_sb", [P, 2, 2, P], F32, region)
            s_old = sb("s_old", [P, 2, P], F32, region)
            s_new = sb("s_new", [P, 2, P], F32, region)
            s_out = sb("s_out", [P, 2, P], F32, region)
        sb("mod_raw_place", [P, 4, D])

        with ExitStack() as region:
            act_hi = sb("act_hi", [P, FC, T], F32R, region)
            act_lo = sb("act_lo", [P, FC, T], F32R, region)
            silu_g = sb("silu_g", [P, 2, T], F32, region)
            act_full = sb("act_full", [P, 2, T], F32, region)
        with ExitStack() as region:
            x_rows = sb("x_rows", [P, NT, D], F32, region)
            table = sb("table", [P, 5, P], F32, region)

        with ExitStack() as region:
            HALF = TAPS // 2
            GR = TS // GW
            glu_seq = sb("glu_seq", [P, KC, HALF + TP + HALF], F32, region)
            glu_row = sb("glu_row", [P, KC // 2, GR, HALF + GW + HALF], F32, region)
            glu_col = sb("glu_col", [P, KC // 2, TS], F32, region)
            sigm = sb("sigm", [P, 2, T], F32, region)
            conv = sb("conv", [P, KC, T], F32, region)
            tap_odd = sb("tap_odd", [P, TP], F32, region)
            row_prod = sb("row_prod", [P, 4, GR, GW], F32, region)
            conv_full = sb("conv_full", [P, 4, T], F32, region)
            y_biased = sb("y_biased", [P, 2, T], F32, region)

        with ExitStack() as region:
            qk = sb("qk", [P, 2 * H, T], F32, region)
            v_tok = sb("v_tok", [P, NT, H, P], F32, region)
            o_all = sb("o_all", [P, H, T], F32, region)
            row_src = sb("row_src", [P, NT, 3, 4 * H], F32, region)
            rows_hi = sb("rows_hi", [4 * H, T], F32R, region)
            rows_lo = sb("rows_lo", [4 * H, T], F32R, region)
            masks = sb("masks", [P, 14, P], mybir.dt.int8, region)
            tri = sb("tri", [P, 2, P], F32, region)
            never = sb("never", [P, 2, P], F32, region)
            ones = sb("ones", [P, P], F32, region)
            one_hot = sb("one_hot", [P, 4 * H - 1], F32, region)
            sel_qk = sb("sel_qk", [2 * H, 2, P], F32R, region)
            sel_row = sb("sel_row", [4 * H, 4, P], F32R, region)
            qk_norm = sb("qk_norm", [2 * H, T], F32, region)
            qk_rnorm_hi = sb("qk_rnorm_hi", [2 * H, T], F32R, region)
            qk_rnorm_lo = sb("qk_rnorm_lo", [2 * H, T], F32R, region)
            q_scale = sb("q_scale", [2 * H, 2], F32, region)
            w_ab = sb("w_ab", [P, KC, 4 * H], F32, region)
            w_ab_hi = sb("w_ab_hi", [P, KC, 4 * H], F32R, region)
            w_ab_lo = sb("w_ab_lo", [P, KC, 4 * H], F32R, region)
            norm_g = sb("norm_g", [P, 1], F32, region)
            dt_a = sb("dt_a", [P, 2, 2 * H], F32, region)
            small_names = ("exp_a", "tot", "g_col", "end_decay", "g_decay", "tot_decay", "minus_beta_g", "pre", "soft", "pos", "log_a", "beta")
            exp_a, tot, g_col, end_decay, g_decay, tot_decay, minus_beta_g, pre, soft, pos, log_a, beta = (
                sb(n, [P, NT, 2 * H], F32, region) for n in small_names)
            ab_rows = sb("ab_rows", [4 * H, T], F32, region)
            ab = sb("ab", [P, NT, 4 * H], F32, region)
            carrier = sb("carrier", [P, 14], F32, region)
        mod_rows = square[:, 0, 0:MW]
        lin = step_p[:, :, :, :].rearrange("p d t c -> p d (t c)")
        v_silu = v_beta[:, :, :, :].rearrange("p d t c -> p d (t c)")
        z = r
        decay = square[:, 0:2, :].rearrange("p d (t c) -> p d t c", c=P)
        q_decay = square[:, 2:4, :]
        q_head = rstd
        inv = h_full[:, 0:2, :].rearrange("p d (t c) -> p d t c", c=P)
        inv_t = h_full[:, 2:4, :].rearrange("p d (t c) -> p d t c", c=P)
        SCAN = ((0, 1, 2), (0, 2, 1))
        LEVELS = 7

        def every_other(ap, n, side):
            if len(ap.shape) == 2:
                return ap.rearrange("p (a s c) -> p a s c", s=2, c=1 << n)[:, :, side]
            return ap.rearrange("p t (a s c) -> p t a s c", s=2, c=1 << n)[:, :, :, side]

        bank = [ctx.enter_context(nc.psum_tensor(f"bank{n}", [P, 512], F32)) for n in range(8)]
        mean_ps, var_ps = bank[4], bank[5]
        mod_ps = bank[6][:, 0:MW]
        mod_turned_ps = bank[7][:, 0:2 * P]

        def u_bank(k, d):
            return bank[2 + d] if k != 1 else bank[d]

        consts = sem("consts")
        table_in = [sem(f"table_in{n}") for n in range(5)]
        x_in = [sem(f"x_in{n}") for n in range(NT)]
        turned = sem("turned")
        table_out = sem("table_out")
        cond_ready = sem("cond_ready")
        w_in = [sem(f"w_in{n}") for n in range(RING)]
        w_hi_ready = sem("w_hi_ready")
        w_lo_ready = sem("w_lo_ready")
        unit_used = sem("unit_used")
        mod_in = [sem(f"mod_in{n}") for n in range(4)]
        mod_used = sem("mod_used")
        mod_copied = sem("mod_copied")
        mod_turned = sem("mod_turned")
        mod_ready = sem("mod_ready")
        small = sem("small")
        silu_ready = sem("silu_ready")
        act_ready = sem("act_ready")
        act_hi_ready = sem("act_hi_ready")
        act_lo_ready = sem("act_lo_ready")
        r_ready = sem("r_ready")
        r_scaled = sem("r_scaled")
        r_summed = sem("r_summed")
        mean_ready = sem("mean_ready")
        centred = sem("centred")
        squared = sem("squared")
        sum_g = sem("sum_g")
        sum_v = sem("sum_v")
        var_added = sem("var_added")
        dev_ready = sem("dev_ready")
        rstd_ready = sem("rstd_ready")
        normed = sem("normed")
        folded = sem("folded")
        x_ready = sem("x_ready")
        h_ready = sem("h_ready")
        h_hi_ready = sem("h_hi_ready")
        h_lo_ready = sem("h_lo_ready")
        dn_consts = sem("dn_consts")
        dn_small_in = sem("dn_small_in")
        state_in = sem("state_in")
        state_out = sem("state_out")
        lin_step = sem("lin_step")
        silu_done = sem("silu_done")
        v_turned = sem("v_turned")
        v_stored = sem("v_stored")
        qk_squared = sem("qk_squared")
        qk_summed = sem("qk_summed")
        qk_norm_ready = sem("qk_norm_ready")
        w_ab_ready = sem("w_ab_ready")
        ab_ready = sem("ab_ready")
        ab_copied = sem("ab_copied")
        gate_v = sem("gate_v")
        gate_a = sem("gate_a")
        gate_t = sem("gate_t")
        head_done = sem("head_done")
        sel_ready = sem("sel_ready")
        norm_spread = sem("norm_spread")
        rows_spread = sem("rows_spread")
        qk_ready = sem("qk_ready")
        kk_ready = sem("kk_ready")
        k_turned = sem("k_turned")
        diff_ready = sem("diff_ready")
        decay_ready = sem("decay_ready")
        q_exp_ready = sem("q_exp_ready")
        k_decay_ready = sem("k_decay_ready")
        a_step = sem("a_step")
        q_decay_ready = sem("q_decay_ready")
        inv_begun = sem("inv_begun")
        v_beta_ready = sem("v_beta_ready")
        p_ready = sem("p_ready")
        p_copied = sem("p_copied")
        t_ready = sem("t_ready")
        inv_turned = sem("inv_turned")
        inv_copied = sem("inv_copied")
        t_joined = sem("t_joined")
        ks_ready = sem("ks_ready")
        x_set = sem("x_set")
        u_ready = sem("u_ready")
        u_copied = sem("u_copied")
        s_added = sem("s_added")
        s_stored = sem("s_stored")
        s_updated = sem("s_updated")
        o_added = sem("o_added")
        o_squared = sem("o_squared")
        o_summed = sem("o_summed")
        o_norm_ready = sem("o_norm_ready")
        o_rnorm_ready = sem("o_rnorm_ready")
        o_spread = sem("o_spread")
        o_gated = sem("o_gated")
        o_hi = sem("o_hi")
        o_lo = sem("o_lo")
        pads_ready = sem("pads_ready")
        sigm_ready = sem("sigm_ready")
        glu_ready = sem("glu_ready")
        tap_v = sem("tap_v")
        row_tap = sem("row_tap")
        tap_g = sem("tap_g")
        conv_mean = sem("conv_mean")
        conv_normed = sem("conv_normed")
        conv_act = sem("conv_act")
        conv_hi = sem("conv_hi")
        conv_lo = sem("conv_lo")
        y_ready = sem("y_ready")
        rows_ready = sem("rows_ready")
        out_done = sem("out_done")

        block = ctx.enter_context(nc.Block())

        def in_view(w, cols):
            return w.rearrange("(k p) (b m) -> p k b m", p=P, m=P) if cols else w
        mod_view = [w_mod[l].rearrange("(k p) m -> p k m", p=P) for l in range(DEPTH)]
        x_src = (x_prompt[0, :, :], x_sample[0, 0:P, :], x_sample[0, P:2 * P, :])
        y_dst = (y_prompt[0, :, :], y_sample[0, 0:P, :], y_sample[0, P:2 * P, :])

        def norm_of(s):
            return s + (s > 0)

        squares_at = [square[:, n] for n in range(4)] + [h_full[:, n] for n in range(4)]
        ADDS = ((0, 1), (2, 3), (0, 2))

        DN_CONSTS = 15 + 6 * LEVELS
        GATE_A_BETA = 5
        LAST_UNIT = UNIT0[stages - 1] + UNITS[stages - 1]

        def mod_col(s):
            return 72 * (s // 3) + 24 * (s % 3)

        def ffn_of(s):
            return ffn_w_in[s // 3, (s % 3) // 2], ffn_w_out[s // 3, (s % 3) // 2]

        is_ffn = [s % 3 != 1 for s in range(6)]
        ffns = [sum(is_ffn[:s]) for s in range(7)]
        mod_in_chunk = [MOD_FIRST + sum(MOD_BESIDE_IN.get(k, 0) + MOD_BESIDE_OUT.get(k, 0) for k in range(s)) for s in range(6)]
        mod_out_chunk = [g + MOD_BESIDE_IN.get(s, 0) for s, g in enumerate(mod_in_chunk)]

        def in_slices(q):
            return (range(0, 2), *(range(n, n + 1) for n in range(2, KC)), range(0))[q]

        def out_slices(s, q):
            return range(q, q + 1) if s in MOD_BESIDE_OUT and q < KC else range(0)

        @block.sync
        def _(sp):
            def load_unit(u, slot, src, chunks=8, first=False):
                if not first:
                    sp.wait_ge(w_hi_ready, u - RING + 1)
                    sp.wait_ge(w_lo_ready, u - RING + 1)
                sp.dma_start(w_raw[:, slot, 0:chunks], src).then_inc(w_in[slot], 16)

            def load_mod(g0, i, k, first=False):
                if not first:
                    sp.wait_ge(mod_used, KC * i + (KC * g0 + k - 3))
                src = w_mod[g0 // 9, k * P:(k + 1) * P, ds(i * D + g0 % 9 * D, D)]
                sp.dma_start(mod_raw[:, k % 4], src).then_inc(mod_in[k % 4], 16)

            def ffn_in_units(s, pair, eighth=0, beside=None, first=False, which=range(4)):
                wv = ffn_of(s)[0].rearrange("(k p) m -> p k m", p=P)
                for j in range(4):
                    col = (j % 2) * DFF + (j // 2) * P
                    if j in which:
                        load_unit(UNIT0[s] + 4 * pair + j, j, wv[:, :, ds(pair * (2 * P) + col, P)], first=first)
                    if beside is not None:
                        for k in in_slices(eighth + j):
                            load_mod(mod_in_chunk[s], beside, k)

            for t in range(NT):
                sp.dma_start(x_rows[:, t, :], x_src[t]).then_inc(x_in[t], 16)
            for t in range(5):
                sp.wait_ge(consts, 6)
                rows = {0: ((b_mod[0].rearrange("(r p) -> r p", p=P), 0, 72), (ln_g.rearrange("l j (r p) -> (l j r) p", p=P), 72, 120)),
                        1: ((b_mod[1].rearrange("(r p) -> r p", p=P), 0, 72), (ln_b.rearrange("l j (r p) -> (l j r) p", p=P), 72, 120)),
                        2: ((cv_dw[0].rearrange("t (r p) -> (t r) p", p=P)[0:P], 0, P),),
                        3: ((cv_dw[0].rearrange("t (r p) -> (t r) p", p=P)[P:TAPS * KC], 0, TAPS * KC - P), (c[0].rearrange("(r p) -> r p", p=P), 120, 128)),
                        4: ((dn_conv[0].rearrange("t (r p) -> (t r) p", p=P), 0, 72), (cv_b1[0].rearrange("(r p) -> r p", p=P), 72, 88),
                            (cv_dwb[0].rearrange("(r p) -> r p", p=P), 88, 96), (cv_ln_g[0].rearrange("(r p) -> r p", p=P), 96, 104),
                            (cv_ln_b[0].rearrange("(r p) -> r p", p=P), 104, 112), (cv_b2[0].rearrange("(r p) -> r p", p=P), 112, 120),
                            (c_ctx.rearrange("(r p) -> r p", p=P), 120, 128))}[t]
                for src, a, b in rows:
                    sp.dma_start(table[a:b, t, :], src).then_inc(table_in[t], 16)
            ffn_in_units(0, 0, first=True, which=range(2))
            for g in range(MOD_FIRST):
                for k in range(KC):
                    load_mod(g, 0, k, first=(g == 0 and k < 4))
            ffn_in_units(0, 0, first=True, which=range(2, 4))
            for s in range(stages):
                u0 = UNIT0[s]
                if is_ffn[s]:
                    if s in MOD_BESIDE_IN:
                        n = 0
                        if s == 0:
                            for half in range(2):
                                ffn_in_units(s, half, 4 * half, 0, which=range(4 * half))
                            n = 1
                        with sp.Fori(n, MOD_BESIDE_IN[s]) as i:
                            for half in range(2):
                                ffn_in_units(s, 2 * i + half, 4 * half, i)
                        for pair in range(2 * MOD_BESIDE_IN[s], FC // 2):
                            ffn_in_units(s, pair)
                    else:
                        with sp.Fori(0, FC // 2) as i:
                            ffn_in_units(s, i)
                    wv = ffn_of(s)[1].rearrange("(k p) m -> p k m", p=P)
                    with sp.Fori(0, 2) as i:
                        for q in range(12):
                            a, b = FFN_THIRDS[q % 3]
                            load_unit(u0 + 2 * FC + 12 * i + q, q % RING, wv[:, a:b, ds(i * (4 * P) + (q // 3) * P, P)], b - a)
                            for k in out_slices(s, q):
                                load_mod(mod_out_chunk[s], i, k)
                elif s == 1:
                    wv = cv_w1[0].rearrange("(k p) m -> p k m", p=P)
                    with sp.Fori(0, KC // 2) as i:
                        for j in range(4):
                            load_unit(u0 + 4 * i + j, j, wv[:, :, ds(i * (2 * P) + ((j % 2) * D + (j // 2) * P), P)])
                    wv = cv_w2[0].rearrange("(k p) m -> p k m", p=P)
                    with sp.Fori(0, KC // 4) as i:
                        for j in range(4):
                            load_unit(u0 + 2 * KC + 4 * i + j, j, wv[:, :, ds(i * (4 * P) + j * P, P)])
                elif s == 4:
                    wv = dn_w_in[0].rearrange("(k p) m -> p k m", p=P)
                    for j in range(RING):
                        load_unit(u0 + j, j, wv[:, :, j * P:(j + 1) * P])
                    sp.wait_ge(mean_ready, s)
                    sp.dma_start(w_ab[:, :, :], dn_w_in[0, :, DN_BLOCKS * P:].rearrange("(k p) m -> p k m", p=P)).then_inc(dn_small_in, 16)
                    sp.dma_start(dt_a[:, 0, :], dn_dt_bias[0].rearrange("d h -> (d h)").partition_broadcast(P)).then_inc(dn_small_in, 16)
                    sp.dma_start(dt_a[:, 1, :], dn_a_log[0].rearrange("d h -> (d h)").partition_broadcast(P)).then_inc(dn_small_in, 16)
                    sp.dma_start(norm_g[:, :], dn_norm_g.rearrange("a p -> p a")).then_inc(dn_small_in, 16)
                    with sp.Fori(1, DN_BLOCKS // 4) as i:
                        for j in range(4):
                            load_unit(u0 + 4 * i + j, j, wv[:, :, ds(i * (4 * P) + j * P, P)])
                    wv = dn_w_out[0].rearrange("(k p) m -> p k m", p=P)
                    for o in range(RING):
                        load_unit(u0 + DN_BLOCKS + o, o, wv[:, :, o * P:(o + 1) * P])
                    s_src = state_delta[0, 0].rearrange("d h k v -> k h d v")
                    s_dst = new_state[0, 0].rearrange("d h k v -> k h d v")
                    for h in range(H):
                        if h:
                            sp.wait_ge(state_out, 16 * h)
                        sp.wait_ge(head_done, h + 1)
                        sp.dma_start(s_old[:, :, :], s_src[:, h]).then_inc(state_in, 16)
                        sp.wait_ge(s_stored, 2 * h + 2)
                        sp.dma_start(s_dst[:, h], s_out[:, :, :]).then_inc(state_out, 16)
                    for o in range(RING, KC):
                        load_unit(u0 + DN_BLOCKS + o, o % RING, wv[:, :, o * P:(o + 1) * P])
            for t in range(NT):
                sp.wait_ge(rows_ready, 2 * (t + 1))
                sp.dma_start(y_dst[t], x_rows[:, t, :]).then_inc(out_done, 16)
            sp.wait_ge(out_done, 16 * NT)
            if stages > 4:
                sp.wait_ge(state_out, 16 * H)

        @block.gpsimd
        def _(pool):
            pool.memset(ident[:, :], 0.0).then_inc(consts, 1)
            pool.wait_ge(consts, 1)
            pool.memset(mean_w[:, :], 1.0 / D).then_inc(consts, 1)
            pool.wait_ge(consts, 2)
            pool.memset(eps[:, :], LN_EPS).then_inc(consts, 1)
            pool.wait_ge(consts, 3)
            pool.memset(table[96:P, 0:2, :], 0.0).then_inc(consts, 1)
            pool.wait_ge(consts, 4)
            pool.memset(cond[:, :, :], 0.0).then_inc(consts, 1)
            pool.wait_ge(consts, 5)
            pool.memset(r_sum[:, :], 0.0).then_inc(r_summed, 1)
            pool.wait_ge(r_summed, 1)
            pool.affine_select(out=ident[:, :], in_=ident[:, :], compare_op=ALU.not_equal, fill=1.0, base=0,
                               pattern=[[-1, P]], channel_multiplier=1).then_inc(consts, 1)

            def lower_h(k):
                for o in range(KC):
                    pool.wait_ge(h_hi_ready, KC * k + o + 1)
                    pool.tensor_tensor(h_lo[:, o], h_full[:, o % 4], h_hi[:, o].bitcast(F32), ALU.subtract).then_inc(h_lo_ready, 1)

            def sum_squares(norm):
                for j, (a, b) in enumerate(ADDS):
                    if j < 2:
                        pool.wait_ge(squared, KC * norm + 2 * j + 2)
                    else:
                        pool.wait_ge(sum_g, 3 * norm + 2)
                    pool.tensor_tensor(squares_at[a], squares_at[a], squares_at[b], ALU.add).then_inc(sum_g, 1)

            def conv_on_pool():
                for o in range(KC // 2):
                    out = conv[:, o, TP:T].rearrange("p (g w) -> p g w", w=GW)
                    for tap in range(1, TAPS):
                        n = (TAPS - 1) * o + tap - 1
                        pool.wait_ge(row_tap, n + o + 2)
                        if n:
                            pool.wait_ge(tap_g, n)
                        pool.tensor_tensor(out, out, row_prod[:, n % 4], ALU.add).then_inc(tap_g, 1)
                sum_squares(1)
                for o in range(KC):
                    pool.wait_ge(conv_hi, o + 1)
                    pool.tensor_tensor(h_lo[:, o], conv_full[:, o % 4], h_hi[:, o].bitcast(F32), ALU.subtract).then_inc(conv_lo, 1)

            def delta_on_pool():
                done = [0]

                def each(instruction):
                    done[0] += 1
                    instruction.then_inc(dn_consts, 1)
                    pool.wait_ge(dn_consts, done[0])

                each(pool.memset(ones[:, :], 1.0))
                each(pool.memset(row_src[:, :, :, :], 0.0))
                each(pool.memset(one_hot[:, :], 0.0))
                each(pool.memset(one_hot[:, 2 * H - 1:2 * H], 1.0))
                each(pool.memset(q_scale[:, 0:1], 1.0))
                each(pool.memset(q_scale[:, 1:2], 1e-6))
                each(pool.memset(q_scale[0:H, 0:1], float(P)))
                each(pool.memset(q_scale[0:H, 1:2], P * 1e-6))
                each(pool.memset(tri[:, :, :], 1.0))
                each(pool.memset(never[:, :, :], 0.0))
                for d in range(2):
                    sign = 1 - 2 * d
                    for m, fill in ((tri, 0.0), (never, -1e30)):
                        each(pool.affine_select(out=m[:, d], in_=m[:, d], compare_op=ALU.is_ge, fill=fill, base=0,
                                                pattern=[[sign, P]], channel_multiplier=-sign))
                each(pool.memset(masks[:, :, :], 0.0))
                for n in range(LEVELS):
                    b = 1 << n
                    for up in range(2):
                        part = masks[:, 2 * n + up].rearrange("p (a c) -> p a c", c=2 * b)[:, :, up * b:(up + 1) * b]
                        first = (1 - up) * b
                        pairs = P // (2 * b)
                        each(pool.memset(part, 1.0))
                        each(pool.affine_select(out=part, in_=part, compare_op=ALU.is_ge, fill=0.0, base=-first,
                                                pattern=[[-2 * b, pairs], [0, b]], channel_multiplier=1))
                        each(pool.affine_select(out=part, in_=part, compare_op=ALU.is_ge, fill=0.0, base=first + b - 1,
                                                pattern=[[2 * b, pairs], [0, b]], channel_multiplier=-1))
                assert done[0] == DN_CONSTS
                pool.wait_ge(gate_a, GATE_A_BETA)
                pool.wait_ge(v_stored, H)
                with pool.Fori(0, H) as h:
                    pool.wait_ge(norm_spread, h + 1)
                    for m in (inv, inv_t):
                        for d in range(2):
                            i3 = ident[:, :].unsqueeze(1).to_broadcast([P, NT, P])
                            last = pool.tensor_tensor(m[:, d], i3, i3, ALU.mult)
                    last.then_inc(inv_begun, 1)
                    pool.wait_ge(inv_begun, h + 1)
                    for d in range(2):
                        for t in range(NT):
                            last = pool.tensor_tensor(v_beta[:, d, t:t + 1], v_tok[:, t, ds(h, 1)],
                                                      beta[:, t, ds(h + d * H, 1)].unsqueeze(2).to_broadcast([P, 1, P]), ALU.mult)
                    last.then_inc(v_beta_ready, 1)
                    pool.wait_ge(v_beta_ready, h + 1)
                for o in range(KC):
                    pool.wait_ge(o_hi, o + 1)
                    pool.tensor_tensor(h_lo[:, o], h_full[:, o % 4], h_hi[:, o].bitcast(F32), ALU.subtract).then_inc(o_lo, 1)
                pool.wait_ge(o_gated, 2 * H)

            lower_h(0)
            for s in range(stages):
                if s == 1:
                    pool.wait_ge(mean_ready, s)
                    pool.memset(glu_seq[:, :, :], 0.0).then_inc(pads_ready, 1)
                    pool.wait_ge(pads_ready, 1)
                    pool.memset(glu_row[:, :, :, :], 0.0).then_inc(pads_ready, 1)
                    pool.wait_ge(pads_ready, 2)
                if s:
                    pool.wait_ge(mean_ready, s)
                    pool.memset(r_sum[:, :], 0.0).then_inc(r_summed, 1)
                if s == 4:
                    delta_on_pool()
                pool.wait_ge(x_ready, KC * (s + 1))
                pool.tensor_scalar(r[:, :, :], x[:, :, :], ALPHA, 0.0, ALU.mult, ALU.add).then_inc(r_scaled, 1)
                if s == 1:
                    conv_on_pool()
                for o in range(KC - 1):
                    pool.wait_ge(r_ready, KC * s + o + 2)
                    pool.wait_ge(r_summed, KC * s + o + 1)
                    pool.tensor_tensor(r_sum[:, :], r_sum[:, :], r[:, o], ALU.add).then_inc(r_summed, 1)
                sum_squares(norm_of(s))
                if s + 1 < stages:
                    lower_h(s + 1)

        @block.scalar
        def _(act):
            def upper_w(u, slot, lap):
                if not (isinstance(u, int) and u < RING):
                    act.wait_ge(unit_used, u - RING + 1)
                act.wait_ge(w_in[slot], lap * 16)
                act.activation(w_hi[:, slot], w_raw[:, slot], ACT.Copy).then_inc(w_hi_ready, 1)

            def upper_h(k, o):
                act.wait_ge(h_ready, KC * k + o + 1)
                act.activation(h_hi[:, o], h_full[:, o % 4], ACT.Copy).then_inc(h_hi_ready, 1)

            def squares(norm, src):
                for o in range(KC):
                    act.wait_ge(centred, KC * norm + o + 1)
                    act.activation(squares_at[o], src[:, o], ACT.Square).then_inc(squared, 1)
                act.wait_ge(var_added, norm + 1)
                act.activation(rstd[:, :], var_ps[:, 0:T], ACT.Sqrt, bias=eps[:, :]).then_inc(dev_ready, 1)

            def delta_on_scalar(u0):
                with act.Fori(0, 2 * H // 4) as i:
                    for j in range(4):
                        upper_w(u0 + 4 * i + j + RING, j, i + (u0 // RING + 2))
                        act.wait_ge(lin_step, 20 * i + 5 * (j + 1))
                        act.activation(qk[:, ds(4 * i + j, 1)], lin[:, j % 2].unsqueeze(1), ACT.Silu).then_inc(silu_done, 1)
                act.wait_ge(dn_small_in, 64)
                act.activation(w_ab_hi[:, :, :], w_ab[:, :, :], ACT.Copy).then_inc(w_ab_ready, 1)
                for b in range(H + 1):
                    if b < H:
                        n = 2 * H + b
                        upper_w(u0 + n + RING, n % RING, (u0 + n) // RING + 2)
                        act.wait_ge(lin_step, 5 * (n + 1))
                        if b >= 2:
                            act.wait_ge(v_turned, b - 1)
                        act.activation(v_silu[:, b % 2], lin[:, n % 2], ACT.Silu).then_inc(silu_done, 1)
                    if b:
                        act.wait_ge(v_turned, b)
                        act.activation(v_tok[:, :, b - 1], bank[6 + (b - 1) % 2][:, 0:T].rearrange("p (t c) -> p t c", c=P),
                                       ACT.Copy).then_inc(v_stored, 1)
                for j in range(H):
                    for b in range(4 * j, 4 * j + 4) if j < 4 else ():
                        if b >= 8:
                            act.wait_ge(qk_summed, b - 7)
                        act.activation(squares_at[b % 8], qk[:, b], ACT.Square).then_inc(qk_squared, 1)
                    if j == 5:
                        act.wait_ge(dn_consts, DN_CONSTS)
                        act.wait_ge(qk_summed, 2 * H)
                        act.activation(qk_norm[:, :], bank[4][0:2 * H, 0:T], ACT.Sqrt, scale=q_scale[:, 0:1], bias=q_scale[:, 1:2]).then_inc(qk_norm_ready, 1)
                    if j == H - 1:
                        act.wait_ge(gate_v, 11)
                        act.activation(end_decay[:, :, :], end_decay[:, :, :], ACT.Exp).then_inc(gate_a, 1)
                        act.activation(g_decay[:, :, :], g_col[:, :, :], ACT.Exp).then_inc(gate_a, 1)
                        act.activation(tot_decay[:, :, :], tot[:, :, :], ACT.Exp).then_inc(gate_a, 1)
                    n = 3 * H + j
                    upper_w(u0 + n + RING, n % RING, (u0 + n) // RING + 2)
                    act.wait_ge(unit_used, u0 + n + 1)
                    act.activation(z[:, j], bank[j % 4][:, 0:T], ACT.Silu).then_inc(silu_done, 1)
                    if j == 2:
                        act.activation(exp_a[:, 0, :], dt_a[:, 1, :], ACT.Exp).then_inc(gate_a, 1)
                        act.wait_ge(gate_v, 2)
                        act.activation(soft[:, :, :], pre[:, :, :], ACT.Abs).then_inc(gate_a, 1)
                        act.wait_ge(gate_a, 2)
                        act.activation(soft[:, :, :], soft[:, :, :], ACT.Exp, scale=-1.0).then_inc(gate_a, 1)
                        act.wait_ge(gate_a, 3)
                        act.activation(soft[:, :, :], soft[:, :, :], ACT.Ln, bias=1.0).then_inc(gate_a, 1)
                        act.activation(beta[:, :, :], ab[:, :, 2 * H:4 * H], ACT.Sigmoid).then_inc(gate_a, 1)
                act.activation(begun[:, 3:4], eps[:, :], ACT.Copy).then_inc(head_done, 1)
                with act.Fori(0, H) as h:
                    for d in range(2):
                        act.wait_ge(diff_ready, 2 * h + d + 1)
                        act.activation(decay[:, d], qk_decay[:, d], ACT.Exp).then_inc(decay_ready, 1)
                    for d in range(2):
                        act.activation(qk_decay[:, d], qk_decay[:, d], ACT.Exp).then_inc(decay_ready, 1)
                    for d in range(2):
                        act.activation(q_decay[:, d, TP:T], bank[2 + d][:, TP:T], ACT.Exp).then_inc(q_exp_ready, 1)
                    for n in range(1, LEVELS):
                        for d in range(2):
                            act.wait_ge(p_ready, h * (2 * LEVELS) + 2 * n + d + 1)
                            act.activation(every_other(step_p[:, d], n, d), every_other(bank[d][:, 0:T].rearrange("p (t c) -> p t c", c=P), n, d), ACT.Copy).then_inc(p_copied, 1)
                        if n < LEVELS - 1:
                            for d in range(2):
                                act.wait_ge(inv_turned, h * (2 * (LEVELS - 2)) + 2 * (n - 1) + d + 1)
                                act.activation(every_other(inv[:, d], n + 1, d),
                                               every_other(bank[2 + d][:, 0:T].rearrange("p (t c) -> p t c", c=P), n + 1, d), ACT.Copy).then_inc(inv_copied, 1)
                    for k in range(NT):
                        for d in range(2):
                            act.wait_ge(u_ready, 6 * h + 2 * k + d + 1)
                            if k == 2:
                                act.wait_ge(o_added, 6 * h + d + 1)
                            act.activation(u_sb[:, k % 2, d], u_bank(k, d)[:, 0:P], ACT.Copy).then_inc(u_copied, 1)
                        if k == 1:
                            act.wait_ge(state_in, 16 * h + 16)
                            for d in range(2):
                                act.wait_ge(s_added, 4 * h + d + 1)
                                act.activation(s_out[:, d], bank[4 + d][:, 0:P], ACT.Copy).then_inc(s_stored, 1)
                    act.wait_ge(o_added, 6 * h + 6)
                    act.activation(o_all[:, ds(h, 1)], bank[6][:, 0:T].unsqueeze(1), ACT.Copy).then_inc(head_done, 1)
                act.wait_ge(head_done, H + 1)
                for h in range(H):
                    if h >= 4:
                        act.wait_ge(o_summed, h - 3)
                    act.activation(square[:, h % 4], o_all[:, h], ACT.Square).then_inc(o_squared, 1)
                act.wait_ge(o_summed, H)
                act.activation(qk_norm[0:H, :], bank[4][0:H, 0:T], ACT.Sqrt, scale=1.0 / P, bias=eps[0:H, :]).then_inc(o_norm_ready, 1)
                for o in range(KC):
                    act.wait_ge(o_gated, H + o + 1)
                    act.activation(h_hi[:, o], h_full[:, o % 4], ACT.Copy).then_inc(o_hi, 1)
                for o in range(KC):
                    u = u0 + DN_BLOCKS + o + RING
                    if u < LAST_UNIT:
                        upper_w(u, o % RING, u // RING + 1)

            act.wait_ge(table_out, 5)
            act.activation(cond[:, :, 0], params[:, COL_CCTX:COL_CCTX + KC], ACT.Silu).then_inc(cond_ready, 1)
            act.activation(cond[:, :, 1], params[:, COL_C:COL_C + KC], ACT.Silu).then_inc(cond_ready, 1)
            for j in range(2):
                upper_w(j, j, 1)
            for o in range(KC):
                upper_h(0, o)
            for j in range(2, RING):
                upper_w(j, j, 1)

            for s in range(stages):
                u0 = UNIT0[s]
                if is_ffn[s]:
                    f0 = FC * ffns[s]
                    with act.Fori(0, FC // 2) as i:
                        for q in range(2):
                            act.wait_ge(unit_used, u0 + 4 * i + 2 * q + 2)
                            act.activation(silu_g[:, q], bank[2 + q][:, 0:T], ACT.Silu).then_inc(silu_ready, 1)
                            act.wait_ge(act_ready, f0 + 2 * i + q + 2)
                            act.activation(act_hi[:, ds(2 * i + q, 1)], act_full[:, ds(q, 1)], ACT.Copy).then_inc(act_hi_ready, 1)
                            for j in range(2):
                                upper_w(u0 + 4 * i + 2 * q + j + RING, 2 * q + j, i + (u0 // RING + 2))
                    if s == stages - 1:
                        for q in range(3 * KC - RING):
                            upper_w(u0 + 2 * FC + q + RING, q % RING, (u0 + 2 * FC + q) // RING + 2)
                    else:
                        with act.Fori(0, 2) as i:
                            for q in range(12):
                                upper_w(u0 + 2 * FC + 12 * i + q + RING, q % RING,
                                        i * 3 + ((u0 + 2 * FC + q) // RING + 2))
                elif s == 1:
                    for o in range(KC):
                        act.wait_ge(unit_used, u0 + 2 * o + 2)
                        act.activation(sigm[:, o % 2], bank[2 + o % 2][:, 0:T], ACT.Sigmoid,
                                       bias=params[:, COL_B1 + KC + o:COL_B1 + KC + o + 1]).then_inc(sigm_ready, 1)
                        c = o // 2
                        act.wait_ge(glu_ready, c + 2)
                        for tap in (range(16), range(16, TAPS))[o % 2]:
                            n = (TAPS - 1) * c + tap - 1
                            src = glu_row[:, c, :, tap:tap + GW]
                            w = params[:, COL_DW + tap * KC + c:COL_DW + tap * KC + c + 1]
                            if tap == 0:
                                act.activation(conv[:, c, TP:T].rearrange("p (g w) -> p g w", w=GW), src, ACT.Identity, scale=w,
                                               bias=params[:, COL_DWB + c:COL_DWB + c + 1]).then_inc(row_tap, 1)
                            else:
                                if n > 3:
                                    act.wait_ge(tap_g, n - 3)
                                act.activation(row_prod[:, n % 4], src, ACT.Copy, scale=w).then_inc(row_tap, 1)
                            if tap in (4, 12, 20, 28):
                                u = u0 + 2 * o + (tap in (12, 28)) + RING
                                upper_w(u, u % RING, u // RING + 1)
                    squares(1, conv)
                    for o in range(KC):
                        act.wait_ge(conv_normed, o + 1)
                        if o >= 4:
                            act.wait_ge(conv_lo, o - 3)
                        act.activation(conv_full[:, o % 4], conv[:, o], ACT.Silu, scale=params[:, COL_CLNG + o:COL_CLNG + o + 1],
                                       bias=params[:, COL_CLNB + o:COL_CLNB + o + 1]).then_inc(conv_act, 1)
                        act.wait_ge(conv_act, o + 1)
                        act.activation(h_hi[:, o], conv_full[:, o % 4], ACT.Copy).then_inc(conv_hi, 1)
                    for o in range(KC):
                        u = u0 + 2 * KC + o
                        act.wait_ge(unit_used, u + 1)
                        if o >= 2:
                            act.wait_ge(r_ready, KC * s + o)
                        act.activation(y_biased[:, o % 2], bank[o % 2][:, 0:T], ACT.Identity,
                                       bias=params[:, COL_B2 + o:COL_B2 + o + 1]).then_inc(y_ready, 1)
                        if u + RING < LAST_UNIT:
                            upper_w(u + RING, o % RING, (u + RING) // RING + 1)
                elif s == 4:
                    delta_on_scalar(u0)
                squares(norm_of(s), r)
                for o in range(KC):
                    act.wait_ge(normed, KC * s + o + 1)
                    n = (s // 3 * 3 + s % 3) * KC + o
                    act.activation(x[:, o], r[:, o], ACT.Identity, scale=params[:, COL_LNG + n:COL_LNG + n + 1],
                                   bias=params[:, COL_LNB + n:COL_LNB + n + 1]).then_inc(x_ready, 1)
                    if s + 1 < stages:
                        upper_h(s + 1, o)

        @block.vector
        def _(dve):
            def lower_w(u, slot):
                dve.wait_ge(w_hi_ready, u + 1)
                dve.tensor_tensor(w_lo[:, slot], w_raw[:, slot], w_hi[:, slot].bitcast(F32), ALU.subtract).then_inc(w_lo_ready, 1)

            def copy_mod(g0, i):
                dve.wait_ge(mod_used, KC * i + KC * (g0 + 1))
                dve.tensor_copy(mod_rows, mod_ps).then_inc(mod_copied, 1)

            def store_mod(g0, i):
                dve.wait_ge(mod_turned, i + g0 + 1)
                pairs = lambda ap: ap.rearrange("p (j e) c -> p j e c", e=2)
                src = mod_turned_ps.rearrange("p (e j c) -> p j e c", e=2, j=4)[:, :, :, 0:2]
                bias = params[:, ds(KC * i + (COL_BMOD[g0 // 9] + g0 % 9 * KC), KC)].unsqueeze(2).to_broadcast([P, KC, 2])
                dve.tensor_tensor(pairs(mod[:, ds(KC * i + KC * g0, KC), :]), src, pairs(bias), ALU.add).then_inc(mod_ready, 1)

            def scale_of(k):
                dve.wait_ge(mod_ready, 3 * k + 2)
                dve.tensor_scalar(scale1[:, :, :], mod[:, mod_col(k) + KC:mod_col(k) + 2 * KC, :], 1.0, None,
                                  ALU.add).then_inc(small, 1)

            def fold(s):
                scale_of(s + 1)
                dve.wait_ge(small, 2 * s + 3)
                of_norm = lambda col: params[:, col + s * KC:col + (s + 1) * KC].unsqueeze(2).to_broadcast([P, KC, 2])
                dve.tensor_tensor(h_scale[:, :, :], scale1[:, :, :], of_norm(COL_LNG), ALU.mult).then_inc(folded, 1)
                dve.tensor_tensor(h_shift[:, :, :], scale1[:, :, :], of_norm(COL_LNB), ALU.mult).then_inc(folded, 1)
                dve.wait_ge(folded, 3 * s + 2)
                dve.tensor_tensor(h_shift[:, :, :], h_shift[:, :, :], mod[:, mod_col(s + 1):mod_col(s + 1) + KC, :], ALU.add).then_inc(folded, 1)

            def modulate(k, o, src, scale, shift):
                if KC * k + o >= 4:
                    dve.wait_ge(h_lo_ready, KC * k + o - 3)
                for g, a, b in GROUPS:
                    last = dve.tensor_scalar(h_full[:, o % 4, a:b], src[:, o, a:b], scale[:, o, g:g + 1],
                                             shift[:, o, g:g + 1], ALU.mult, ALU.add)
                last.then_inc(h_ready, 1)

            def deviation(norm, src, mean_there, count, meanwhile=None):
                dve.wait_ge(mean_there, count)
                for o in range(KC):
                    dve.tensor_tensor(src[:, o], src[:, o], mean_ps[:, 0:T], ALU.subtract).then_inc(centred, 1)
                for j, (a, b) in enumerate(ADDS):
                    if j < 2:
                        dve.wait_ge(squared, KC * norm + 2 * j + 6)
                    else:
                        dve.wait_ge(sum_v, 3 * norm + 2)
                    dve.tensor_tensor(squares_at[4 + a], squares_at[4 + a], squares_at[4 + b], ALU.add).then_inc(sum_v, 1)
                if meanwhile is not None:
                    meanwhile()
                dve.wait_ge(dev_ready, norm + 1)
                dve.reciprocal(rstd[:, :], rstd[:, :]).then_inc(rstd_ready, 1)
                dve.wait_ge(rstd_ready, norm + 1)

            def conv_on_vector(u0):
                dve.wait_ge(pads_ready, 2)
                taps = 0
                for o in range(KC):
                    dve.wait_ge(sigm_ready, o + 1)
                    bias = params[:, COL_B1 + o:COL_B1 + o + 1]
                    dve.scalar_tensor_tensor(glu_seq[:, o, HALF:HALF + TP], bank[o % 2][:, 0:TP], bias, sigm[:, o % 2, 0:TP],
                                             ALU.add, ALU.mult)
                    if o < KC // 2:
                        g3 = lambda ap: ap.rearrange("p (g w) -> p g w", w=GW)
                        dve.scalar_tensor_tensor(glu_row[:, o, :, HALF:HALF + GW], g3(bank[o % 2][:, TP:T]), bias,
                                                 g3(sigm[:, o % 2, TP:T]), ALU.add, ALU.mult).then_inc(glu_ready, 1)
                    else:
                        dve.scalar_tensor_tensor(glu_col[:, o - KC // 2], bank[o % 2][:, TP:T], bias, sigm[:, o % 2, TP:T],
                                                 ALU.add, ALU.mult).then_inc(glu_ready, 1)
                    dve.wait_ge(glu_ready, o + 2)
                    tap_w = lambda tap: params[:, COL_DW + tap * KC + o:COL_DW + tap * KC + o + 1]
                    dwb = params[:, COL_DWB + o:COL_DWB + o + 1]
                    last = {}

                    def add_tap(chain, out, src, tap, bias=None):
                        nonlocal taps
                        if chain not in last:
                            ops = (ALU.mult, ALU.add) if bias is not None else (ALU.mult,)
                            dve.tensor_scalar(out, src, tap_w(tap), bias, *ops).then_inc(tap_v, 1)
                        else:
                            dve.wait_ge(tap_v, last[chain])
                            dve.scalar_tensor_tensor(out, src, tap_w(tap), out, ALU.mult, ALU.add).then_inc(tap_v, 1)
                        taps += 1
                        last[chain] = taps

                    offsets = [0] + [d for d in range(1 - GR, GR) if d]
                    for tap in range(TAPS):
                        src = glu_seq[:, o, tap:tap + TP]
                        if tap % 2:
                            add_tap("odd", tap_odd[:, :], src, tap)
                        else:
                            add_tap("even", conv[:, o, 0:TP], src, tap, dwb)
                        if tap in (7, 23):
                            u = u0 + 2 * o + (tap > 7) + RING
                            lower_w(u, u % RING)
                        if o >= KC // 2 and tap % 4 == 1 and offsets:
                            d = offsets.pop(0)
                            a, b = max(0, -d), min(GR, GR - d)
                            add_tap("column", conv[:, o, TP + a * GW:TP + b * GW],
                                    glu_col[:, o - KC // 2, (a + d) * GW:(b + d) * GW], d + HALF, dwb if d == 0 else None)
                    dve.wait_ge(tap_v, taps)
                    dve.tensor_tensor(conv[:, o, 0:TP], conv[:, o, 0:TP], tap_odd[:, :], ALU.add).then_inc(tap_v, 1)
                    taps += 1
                deviation(1, conv, conv_mean, 1)
                for o in range(KC):
                    dve.tensor_tensor(conv[:, o], conv[:, o], rstd[:, :], ALU.mult).then_inc(conv_normed, 1)

            def delta_on_vector(u0):
                with dve.Fori(0, 3 * H // 4) as i:
                    for j in range(4):
                        dve.wait_ge(unit_used, u0 + 4 * i + j + 1)
                        w = [params[:, ds(4 * i + (COL_DNCONV + tap * 3 * H + j), 1)] for tap in range(3)]
                        out, ps, n = lin[:, j % 2], bank[j], 20 * i + 5 * j
                        dve.tensor_scalar(out, ps[:, 0:T], w[1], None, ALU.mult).then_inc(lin_step, 1)
                        dve.wait_ge(lin_step, n + 1)
                        for _, a, b in GROUPS:
                            dve.scalar_tensor_tensor(out[:, a + 1:b], ps[:, a:b - 1], w[0], out[:, a + 1:b], ALU.mult, ALU.add).then_inc(lin_step, 1)
                        for g, a, b in GROUPS:
                            dve.wait_ge(lin_step, n + 2 + g)
                            dve.scalar_tensor_tensor(out[:, a:b - 1], ps[:, a + 1:b], w[2], out[:, a:b - 1], ALU.mult, ALU.add).then_inc(lin_step, 1)
                        lower_w(u0 + 4 * i + j + RING, j)
                        dve.wait_ge(silu_done, 4 * i + j + 1)
                dve.wait_ge(w_ab_ready, 1)
                dve.tensor_tensor(w_ab_lo[:, :, :], w_ab[:, :, :], w_ab_hi[:, :, :].bitcast(F32), ALU.subtract).then_inc(w_ab_ready, 1)
                for j in range(H):
                    lower_w(u0 + 3 * H + j + RING, j % RING)
                    if j == 1:
                        dve.wait_ge(ab_ready, 1)
                        dve.tensor_copy(ab_rows[:, :], bank[5][0:4 * H, 0:T]).then_inc(ab_copied, 1)
                    if j == 2:
                        dve.wait_ge(ab_ready, 2)
                        dve.tensor_copy(ab[:, :, :], bank[5][:, 0:12 * H].rearrange("p (t c) -> p t c", t=NT)).then_inc(gate_v, 1)
                        dve.wait_ge(gate_v, 1)
                        dve.tensor_tensor(pre[:, :, :], ab[:, :, 0:2 * H], dt_a[:, 0:1, :].to_broadcast([P, NT, 2 * H]), ALU.add).then_inc(gate_v, 1)
                        dve.wait_ge(gate_v, 2)
                        dve.tensor_scalar(pos[:, :, :], pre[:, :, :], 0.0, None, ALU.max).then_inc(gate_v, 1)
                        dve.wait_ge(gate_v, 3)
                        dve.wait_ge(gate_a, 4)
                        dve.tensor_tensor(pos[:, :, :], pos[:, :, :], soft[:, :, :], ALU.add).then_inc(gate_v, 1)
                        dve.wait_ge(gate_v, 4)
                        dve.scalar_tensor_tensor(log_a[:, :, :], pos[:, :, :], -1.0, exp_a[:, 0:1, :].to_broadcast([P, NT, 2 * H]),
                                                 ALU.mult, ALU.mult).then_inc(gate_v, 1)
                        dve.wait_ge(gate_v, 5)
                        dve.wait_ge(dn_consts, DN_CONSTS)
                        dve.wait_ge(gate_a, GATE_A_BETA)
                        for d in range(2):
                            dve.tensor_copy(row_src[:, :, d, d * H:(d + 1) * H], log_a[:, :, d * H:(d + 1) * H]).then_inc(gate_v, 1)
                        dve.tensor_copy(row_src[:, :, 2, 2 * H:4 * H], beta[:, :, :]).then_inc(gate_v, 1)
                    if j == 5:
                        dve.wait_ge(qk_norm_ready, 1)
                        dve.reciprocal(qk_norm[:, :], qk_norm[:, :]).then_inc(qk_norm_ready, 1)
                        dve.wait_ge(qk_norm_ready, 2)
                        dve.tensor_copy(qk_rnorm_hi[:, :], qk_norm[:, :]).then_inc(qk_norm_ready, 1)
                        dve.wait_ge(qk_norm_ready, 3)
                        dve.tensor_tensor(qk_rnorm_lo[:, :], qk_norm[:, :], qk_rnorm_hi[:, :].bitcast(F32), ALU.subtract).then_inc(qk_norm_ready, 1)
                    if j == 6:
                        dve.wait_ge(gate_t, 1)
                        dve.tensor_copy(g_col[:, :, :], bank[5][:, 0:6 * H].rearrange("p (t c) -> p t c", t=NT)).then_inc(gate_v, 1)
                        dve.tensor_copy(tot[:, :, :], bank[6][:, 0:6 * H].rearrange("p (t c) -> p t c", t=NT)).then_inc(gate_v, 1)
                        dve.wait_ge(gate_v, 10)
                        dve.tensor_tensor(end_decay[:, :, :], tot[:, :, :], g_col[:, :, :], ALU.subtract).then_inc(gate_v, 1)
                        dve.wait_ge(gate_t, 2)
                        dve.tensor_copy(rows_hi[:, :], bank[0][0:4 * H, 0:T]).then_inc(gate_v, 1)
                        dve.wait_ge(gate_v, 12)
                        dve.tensor_tensor(rows_lo[:, :], bank[0][0:4 * H, 0:T], rows_hi[:, :].bitcast(F32), ALU.subtract).then_inc(gate_v, 1)
                dve.wait_ge(gate_a, 8)
                dve.scalar_tensor_tensor(minus_beta_g[:, :, :], beta[:, :, :], -1.0, g_decay[:, :, :], ALU.mult, ALU.mult).then_inc(gate_v, 1)
                dve.wait_ge(gate_v, 14)

                def select(h, ahead):
                    one = lambda rows, n: (ident[0:rows, ahead:ahead + n * H].rearrange("p (n c) -> p n c", c=H)[:, :, ds(h, 1)]
                                           .to_broadcast([rows, n, P]))
                    dve.tensor_copy(sel_qk[:, :, :], one(2 * H, 2))
                    dve.tensor_copy(sel_row[:, :, :], one(4 * H, 4)).then_inc(sel_ready, 1)

                select(0, 0)
                tiles = lambda ap: ap[:, 0:T].rearrange("p (t c) -> p t c", c=P)
                with dve.Fori(0, H) as h:
                    dve.wait_ge(norm_spread, h + 1)
                    dve.tensor_tensor(k_head[:, :].unsqueeze(1), qk[:, ds(h + H, 1)], bank[0][:, 0:T].unsqueeze(1), ALU.mult).then_inc(qk_ready, 1)
                    dve.tensor_tensor(q_head[:, :].unsqueeze(1), qk[:, ds(h, 1)], bank[1][:, 0:T].unsqueeze(1), ALU.mult).then_inc(qk_ready, 1)
                    dve.wait_ge(rows_spread, 2 * h + 1)
                    for d in range(2):
                        for t in range(NT):
                            last = dve.scalar_tensor_tensor(qk_decay[:, d, t], bank[2 + d][:, t * P:(t + 1) * P], g_col[:, t, ds(h + d * H, 1)],
                                                            never[:, d], ALU.subtract, ALU.add)
                        last.then_inc(diff_ready, 1)
                    dve.wait_ge(kk_ready, h + 1)
                    for d in range(2):
                        dve.wait_ge(decay_ready, 4 * h + d + 1)
                        dve.scalar_tensor_tensor(decay[:, d], decay[:, d], -1.0, tiles(bank[6]), ALU.mult, ALU.mult).then_inc(a_step, 1)
                    for d in range(2):
                        dve.wait_ge(a_step, 4 * h + d + 1)
                        dve.tensor_tensor(decay[:, d], decay[:, d], tiles(bank[4 + d]), ALU.mult).then_inc(a_step, 1)
                    for n in range(LEVELS):
                        for d in range(2):
                            here = every_other(masks[:, 2 * n + d], n, d).unsqueeze(1).to_broadcast([P, NT, P >> (n + 1), 1 << n])
                            there = every_other(masks[:, 2 * n + 1 - d], n, 1 - d).unsqueeze(1).to_broadcast([P, NT, P >> (n + 1), 1 << n])
                            inv_here, inv_there = every_other(inv[:, d], n, d), every_other(inv_t[:, d], n, 1 - d)
                            if n == 0:
                                dve.wait_ge(inv_begun, h + 1)
                                dve.wait_ge(a_step, 4 * h + 2 + d + 1)
                                dve.wait_ge(p_ready, h * (2 * LEVELS) + d + 1)
                                dve.memset(carrier[:, 2 * n + d:2 * n + d + 1], 0.0)
                                dve.copy_predicated(inv_there, there, every_other(decay[:, d], n, 1 - d))
                                dve.copy_predicated(inv_here, here, every_other(tiles(bank[d]), n, d)).then_inc(t_joined, 1)
                            else:
                                dve.wait_ge(t_ready, h * (2 * (LEVELS - 1)) + 2 * (n - 1) + d + 1)
                                dve.memset(carrier[:, 2 * n + d:2 * n + d + 1], 0.0)
                                last = dve.copy_predicated(inv_there, there, every_other(tiles(bank[4 + d]), n, 1 - d))
                                last.then_inc(t_joined, 1)
                        if n == 1:
                            dve.wait_ge(k_turned, h + 1)
                            for d in range(2):
                                for k in range(2):
                                    t = SCAN[d][k]
                                    last = dve.tensor_scalar(k_decay[:, d, k], bank[6][:, t * P:(t + 1) * P], end_decay[:, t, ds(h + d * H, 1)],
                                                             None, ALU.mult)
                            last.then_inc(k_decay_ready, 1)
                        if n == 2:
                            for d in range(2):
                                dve.wait_ge(decay_ready, 4 * h + 3 + d)
                                dve.tensor_tensor(qk_decay[:, d], qk_decay[:, d], tiles(bank[7]), ALU.mult)
                            for d in range(2):
                                dve.wait_ge(q_exp_ready, 2 * h + d + 1)
                                dve.tensor_tensor(q_decay[:, d, TP:T], q_decay[:, d, TP:T], q_head[:, TP:T], ALU.mult).then_inc(q_decay_ready, 1)
                        if n == 3:
                            select(h, 1)
                    dve.wait_ge(v_beta_ready, h + 1)
                    for k in (1, 2):
                        for d in range(2):
                            t = SCAN[d][k]
                            dve.wait_ge(ks_ready, 4 * h + 2 * (k - 1) + d + 1)
                            dve.scalar_tensor_tensor(v_beta[:, d, t], bank[d][:, 0:P], minus_beta_g[:, t, ds(h + d * H, 1)],
                                                     v_beta[:, d, t], ALU.mult, ALU.add).then_inc(x_set, 1)
                        if k == 1:
                            for d in range(2):
                                dve.wait_ge(s_added, 4 * h + 2 + d + 1)
                                dve.scalar_tensor_tensor(s_new[:, d], s_old[:, d], tot_decay[:, SCAN[d][1], ds(h + d * H, 1)],
                                                         bank[4 + d][:, 0:P], ALU.mult, ALU.add).then_inc(s_updated, 1)
                dve.wait_ge(head_done, H + 1)
                for h in range(H):
                    dve.wait_ge(o_squared, h + 1)
                    dve.scalar_tensor_tensor(o_all[:, h], o_all[:, h], norm_g[:, :], z[:, h], ALU.mult, ALU.mult).then_inc(o_gated, 1)
                dve.wait_ge(o_norm_ready, 1)
                dve.reciprocal(qk_norm[0:H, :], qk_norm[0:H, :]).then_inc(o_rnorm_ready, 1)
                dve.wait_ge(o_gated, H)
                for h in range(H):
                    dve.wait_ge(o_spread, h + 1)
                    if h >= 4:
                        dve.wait_ge(o_lo, h - 3)
                    dve.tensor_tensor(h_full[:, h % 4], o_all[:, h], bank[h % 2][:, 0:T], ALU.mult).then_inc(o_gated, 1)

            for n, started in enumerate((act_ready, r_ready, glu_ready)):
                dve.memset(begun[:, n:n + 1], 0.0).then_inc(started, 1)
            for t in range(5):
                dve.wait_ge(turned, t + 1)
                dve.tensor_copy(params[:, t * P:(t + 1) * P], bank[t % 4][:, 0:P]).then_inc(table_out, 1)
            for o in range(KC):
                dve.wait_ge(turned, 5 + o + 1)
                dve.tensor_copy(x[:, o], bank[o % 2][:, 0:T]).then_inc(x_ready, 1)
            for j in range(2):
                lower_w(j, j)
            for g in range(MOD_FIRST):
                copy_mod(g, 0)
                store_mod(g, 0)
            scale_of(0)
            dve.wait_ge(small, 1)
            for o in range(KC):
                modulate(0, o, x, scale1, mod[:, mod_col(0):mod_col(0) + KC])
            for j in range(2, RING):
                lower_w(j, j)

            for s in range(stages):
                u0 = UNIT0[s]
                if is_ffn[s]:
                    f0 = FC * ffns[s]
                    def in_pair(pair, beside=None):
                        for q in range(2):
                            if q and beside is not None:
                                copy_mod(mod_in_chunk[s], beside)
                            dve.wait_ge(silu_ready, f0 + 2 * pair + q + 1)
                            dve.tensor_tensor(act_full[:, q], silu_g[:, q], bank[q][:, 0:T], ALU.mult).then_inc(act_ready, 1)
                            dve.wait_ge(act_hi_ready, f0 + 2 * pair + q + 1)
                            dve.tensor_tensor(act_lo[:, ds(2 * pair + q, 1)], act_full[:, ds(q, 1)],
                                              act_hi[:, ds(2 * pair + q, 1)].bitcast(F32), ALU.subtract).then_inc(act_lo_ready, 1)
                            for j in range(2):
                                lower_w(u0 + 4 * pair + 2 * q + j + RING, 2 * q + j)

                    if s in MOD_BESIDE_IN:
                        with dve.Fori(0, MOD_BESIDE_IN[s]) as i:
                            in_pair(2 * i)
                            in_pair(2 * i + 1, i)
                            store_mod(mod_in_chunk[s], i)
                        for pair in range(2 * MOD_BESIDE_IN[s], FC // 2):
                            in_pair(pair)
                    else:
                        with dve.Fori(0, FC // 2) as i:
                            in_pair(i)
                elif s == 1:
                    conv_on_vector(u0)
                elif s == 4:
                    delta_on_vector(u0)
                dve.wait_ge(mod_ready, 3 * s + 3)
                dve.tensor_scalar(gate[:, :, :], mod[:, mod_col(s) + 2 * KC:mod_col(s) + 3 * KC, :],
                                  0.5 if is_ffn[s] else 1.0, None, ALU.mult).then_inc(small, 1)
                dve.wait_ge(small, 2 * s + 2)
                dve.wait_ge(r_scaled, s + 1)

                def add_gated(done, count, o, ps):
                    dve.wait_ge(done, count)
                    for g, a, b in GROUPS:
                        last = dve.scalar_tensor_tensor(r[:, ds(o, 1), a:b], ps[:, a:b].unsqueeze(1), gate[:, ds(o, 1), g:g + 1],
                                                        r[:, ds(o, 1), a:b], ALU.mult, ALU.add)
                    last.then_inc(r_ready, 1)

                if is_ffn[s]:
                    v0 = u0 + 2 * FC
                    def out_body(i, units):
                        for q in range(12):
                            if q % 3 == 2:
                                add_gated(unit_used, v0 + 12 * i + q + 1, 4 * i + q // 3, bank[(q // 3) % 2])
                            if q < units:
                                lower_w(v0 + 12 * i + q + RING, q % RING)
                            if s in MOD_BESIDE_OUT and q == KC:
                                copy_mod(mod_out_chunk[s], i)
                            if s in MOD_BESIDE_OUT and q == KC + 2:
                                store_mod(mod_out_chunk[s], i)
                    if s == stages - 1:
                        out_body(0, 12)
                        out_body(1, 12 - RING)
                    else:
                        with dve.Fori(0, 2) as i:
                            out_body(i, 12)

                elif s == 1:
                    for o in range(KC):
                        add_gated(y_ready, o + 1, o, y_biased[:, o % 2])
                        if u0 + 2 * KC + o + RING < LAST_UNIT:
                            lower_w(u0 + 2 * KC + o + RING, o % RING)
                elif s == 4:
                    for o in range(KC):
                        add_gated(unit_used, u0 + DN_BLOCKS + o + 1, o, bank[2 + o % 2])
                        if u0 + DN_BLOCKS + o + RING < LAST_UNIT:
                            lower_w(u0 + DN_BLOCKS + o + RING, o % RING)
                more = s + 1 < stages
                deviation(norm_of(s), r, mean_ready, s + 1, meanwhile=(lambda: fold(s)) if more else None)
                if more:
                    dve.wait_ge(folded, 3 * s + 3)
                def normalise(o):
                    dve.tensor_tensor(r[:, o], r[:, o], rstd[:, :], ALU.mult).then_inc(normed, 1)

                normalise(0)
                for o in range(KC):
                    if 0 < o < KC - 1:
                        normalise(o + 1)
                    if more:
                        dve.wait_ge(normed, KC * s + o + 1)
                        modulate(s + 1, o, r, h_scale, h_shift)
                    if o == 0:
                        normalise(1)

            for t in range(NT):
                for half in range(2):
                    dve.wait_ge(turned, 5 + KC + 2 * t + half + 1)
                    dve.tensor_copy(x_rows[:, t, 512 * half:512 * half + 512], bank[(2 * t + half) % 4][:, :]).then_inc(rows_ready, 1)

        @block.tensor
        def _(pe):
            def split_product(ps, w_slot, k, a_hi, a_lo, start, stop):
                pe.matmul(ps, w_hi[:, w_slot, k], a_hi, start=start, stop=False)
                pe.matmul(ps, w_hi[:, w_slot, k], a_lo, start=False, stop=False)
                return pe.matmul(ps, w_lo[:, w_slot, k], a_hi, start=False, stop=stop)

            def unit(u, slot, ps, hi, lo, chunks, first=True, last=True):
                pe.wait_ge(w_lo_ready, u + 1)
                for n, k in enumerate(chunks):
                    mm = split_product(ps, slot, n, hi[:, k], lo[:, k], first and n == 0, last and n == len(chunks) - 1)
                mm.then_inc(unit_used, 1)

            def units_of_input(u, slots, ready, count):
                pe.wait_ge(w_lo_ready, u + 2)
                for k in range(KC):
                    pe.wait_ge(ready, count + k + 1)
                    for slot, ps in slots:
                        mm = split_product(ps[:, 0:T], slot, k, h_hi[:, k], h_lo[:, k], k == 0, k == KC - 1)
                        if k == KC - 1:
                            mm.then_inc(unit_used, 1)

            def variance(norm):
                for j, done in enumerate((sum_g, sum_v)):
                    pe.wait_ge(done, 3 * norm + 3)
                    mm = pe.matmul(var_ps[:, 0:T], mean_w[:, :], squares_at[4 * j], start=(j == 0), stop=(j == 1))
                mm.then_inc(var_added, 1)

            def mod_slice(g0, i, k):
                if k == 0 and not (isinstance(i, int) and g0 + i == 0):
                    pe.wait_ge(mod_copied, i + g0)
                pe.wait_ge(mod_in[k % 4], i * 32 + (32 * g0 + 16 * (k // 4 + 1)))
                for j in range(4):
                    mm = pe.matmul(mod_ps[MOD_COLS * j:MOD_COLS * (j + 1), :], cond[:, k, :], mod_raw[:, k % 4, MW * j:MW * (j + 1)],
                                   start=(k == 0), stop=(k == KC - 1))
                mm.then_inc(mod_used, 1)

            def turn_mod(g0, i):
                if not (isinstance(i, int) and g0 + i == 0):
                    pe.wait_ge(mod_ready, i + g0)
                pe.wait_ge(mod_copied, i + g0 + 1)
                for e in range(2):
                    mm = pe.transpose(mod_turned_ps[:, e * P:(e + 1) * P], mod_rows[:, e * P:(e + 1) * P], ident[:, :])
                mm.then_inc(mod_turned, 1)

            def delta_on_tensor(u0):
                with pe.Fori(0, 2 * H // 4) as i:
                    for j in range(4):
                        if j == 0:
                            units_of_input(u0 + 4 * i, ((0, bank[0]), (1, bank[1])), h_lo_ready, KC * 4)
                        elif j >= 2:
                            unit(u0 + 4 * i + j, j, bank[j][:, 0:T], h_hi, h_lo, range(KC))
                        if j:
                            pe.wait_ge(lin_step, 20 * i + 5 * j)
                for b in range(H + 1):
                    if b < H:
                        n = 2 * H + b
                        unit(u0 + n, n % RING, bank[n % 4][:, 0:T], h_hi, h_lo, range(KC))
                        pe.wait_ge(lin_step, 5 * n)
                    if b:
                        pe.wait_ge(silu_done, 2 * H + b)
                        if b >= 3:
                            pe.wait_ge(v_stored, b - 2)
                        for t in range(NT):
                            mm = pe.transpose(bank[6 + (b - 1) % 2][:, t * P:(t + 1) * P], v_silu[:, (b - 1) % 2, t * P:(t + 1) * P], ident[:, :])
                        mm.then_inc(v_turned, 1)
                pe.wait_ge(dn_consts, DN_CONSTS)
                for j in range(H):
                    if j == 3:
                        pe.wait_ge(lin_step, 15 * H)
                    elif j >= 4:
                        pe.wait_ge(silu_done, 3 * H + j - 3)
                    n = 3 * H + j
                    unit(u0 + n, n % RING, bank[j % 4][:, 0:T], h_hi, h_lo, range(KC))
                    for b in range(4 * j, 4 * j + 4) if j < 4 else ():
                        pe.wait_ge(qk_squared, b + 1)
                        pe.matmul(bank[4][0:2 * H, 0:T], one_hot[:, 2 * H - 1 - b:4 * H - 1 - b], squares_at[b % 8],
                                  start=(b == 0), stop=(b == 2 * H - 1)).then_inc(qk_summed, 1)
                    if j == 0:
                        pe.wait_ge(w_ab_ready, 2)
                        for k in range(KC):
                            out = bank[5][0:4 * H, 0:T]
                            pe.matmul(out, w_ab_hi[:, k], h_hi[:, k], start=(k == 0), stop=False)
                            pe.matmul(out, w_ab_hi[:, k], h_lo[:, k], start=False, stop=False)
                            mm = pe.matmul(out, w_ab_lo[:, k], h_hi[:, k], start=False, stop=(k == KC - 1))
                        mm.then_inc(ab_ready, 1)
                    if j == 1:
                        pe.wait_ge(ab_copied, 1)
                        for t in range(NT):
                            mm = pe.transpose(bank[5][:, t * 4 * H:(t + 1) * 4 * H], ab_rows[:, t * P:(t + 1) * P], ident[0:4 * H, 0:4 * H])
                        mm.then_inc(ab_ready, 1)
                    if j == 6:
                        pe.wait_ge(gate_v, 5)
                        pe.wait_ge(v_stored, H)
                        cols = bank[5][:, 0:6 * H].rearrange("p (t c) -> p t c", t=NT)
                        for d in range(2):
                            pe.matmul(cols[:, :, d * H:(d + 1) * H], tri[:, d], log_a[:, :, d * H:(d + 1) * H], start=True, stop=True)
                        pe.matmul(bank[6][:, 0:6 * H], ones[:, :], log_a[:, :, :].rearrange("p t c -> p (t c)"), start=True, stop=True).then_inc(gate_t, 1)
                        pe.wait_ge(silu_done, 3 * H + 5)
                        pe.wait_ge(gate_v, 8)
                        for t in range(NT):
                            for n, rhs in enumerate((tri[:, 0], tri[:, 1], ident[:, :])):
                                mm = pe.matmul(bank[0][0:4 * H, t * P:(t + 1) * P], row_src[:, t, n], rhs, start=(n == 0), stop=(n == 2))
                        mm.then_inc(gate_t, 1)
                pe.wait_ge(gate_v, 13)
                pe.wait_ge(qk_norm_ready, 4)

                def spread(ps, sel, hi, lo):
                    pe.matmul(ps[:, 0:T], sel, hi, start=True, stop=False)
                    return pe.matmul(ps[:, 0:T], sel, lo, start=False, stop=True)

                def spread_norms():
                    spread(bank[0], sel_qk[:, 1], qk_rnorm_hi[:, :], qk_rnorm_lo[:, :])
                    spread(bank[1], sel_qk[:, 0], qk_rnorm_hi[:, :], qk_rnorm_lo[:, :]).then_inc(norm_spread, 1)

                def spread_rows():
                    for n in range(4):
                        mm = spread(bank[2 + n], sel_row[:, n], rows_hi[:, :], rows_lo[:, :])
                        if n % 2:
                            mm.then_inc(rows_spread, 1)

                pe.wait_ge(sel_ready, 1)
                pe.wait_ge(silu_done, 4 * H)
                spread_norms()
                spread_rows()
                with pe.Fori(0, H) as h:
                    pe.wait_ge(qk_ready, 2 * h + 2)
                    pe.wait_ge(head_done, h + 1)
                    for ps, m in ((bank[6], k_head), (bank[7], q_head)):
                        for t in range(NT):
                            mm = pe.matmul(ps[:, t * P:(t + 1) * P], k_head[:, t * P:(t + 1) * P], m[:, t * P:(t + 1) * P], start=True, stop=True)
                    mm.then_inc(kk_ready, 1)
                    pe.wait_ge(inv_begun, h + 1)
                    for n in range(LEVELS):
                        for d in range(2):
                            if n == 0:
                                pe.wait_ge(a_step, 4 * h + 2 + d + 1)
                            elif n == 1:
                                pe.wait_ge(t_joined, h * (2 * LEVELS) + d + 1)
                            else:
                                pe.wait_ge(inv_copied, h * (2 * (LEVELS - 2)) + 2 * (n - 2) + d + 1)
                            for t in range(NT):
                                if n == 0:
                                    mm = pe.transpose(bank[d][:, t * P:(t + 1) * P], decay[:, d, t], ident[:, :])
                                else:
                                    mm = pe.matmul(bank[d][:, t * P:(t + 1) * P], decay[:, d, t], inv[:, d, t], start=True, stop=True)
                            mm.then_inc(p_ready, 1)
                        if n == 0:
                            for t in range(NT):
                                mm = pe.transpose(bank[6][:, t * P:(t + 1) * P], k_head[:, t * P:(t + 1) * P], ident[:, :])
                            mm.then_inc(k_turned, 1)
                        if n:
                            for d in range(2):
                                pe.wait_ge(p_copied, h * (2 * (LEVELS - 1)) + 2 * (n - 1) + d + 1)
                                for t in range(NT):
                                    mm = pe.matmul(bank[4 + d][:, t * P:(t + 1) * P], step_p[:, d, t], inv_t[:, d, t], start=True, stop=True)
                                mm.then_inc(t_ready, 1)
                        if 0 < n < LEVELS - 1:
                            for d in range(2):
                                pe.wait_ge(t_joined, h * (2 * LEVELS) + 2 * n + d + 1)
                                if n == 1:
                                    pe.wait_ge(q_exp_ready, 2 * h + d + 1)
                                for t in range(NT):
                                    mm = pe.transpose(bank[2 + d][:, t * P:(t + 1) * P], inv_t[:, d, t], ident[:, :])
                                mm.then_inc(inv_turned, 1)
                    pe.wait_ge(v_beta_ready, h + 1)
                    pe.wait_ge(k_decay_ready, h + 1)
                    pe.wait_ge(q_decay_ready, 2 * h + 2)
                    pe.wait_ge(state_in, 16 * h + 16)
                    for d in range(2):
                        t = SCAN[d][1]
                        pe.matmul(bank[d][:, 0:P], k_head[:, t * P:(t + 1) * P], s_old[:, d], start=True, stop=True).then_inc(ks_ready, 1)

                    def solve(k, ready, count):
                        for d in range(2):
                            pe.wait_ge(ready, count + d)
                            pe.matmul(u_bank(k, d)[:, 0:P], inv_t[:, d, SCAN[d][k]], v_beta[:, d, SCAN[d][k]],
                                      start=True, stop=True).then_inc(u_ready, 1)

                    def outputs(k, d):
                        t = SCAN[d][k]
                        pe.wait_ge(u_copied, 6 * h + 2 * k + d + 1)
                        if k < 2:
                            if k:
                                pe.wait_ge(s_stored, 2 * h + d + 1)
                            pe.matmul(bank[4 + d][:, 0:P], k_decay[:, d, k], u_sb[:, k % 2, d], start=True, stop=True).then_inc(s_added, 1)
                        out = bank[6][:, t * P:(t + 1) * P]
                        if k:
                            pe.matmul(out, (s_old, s_new)[k - 1][:, d], q_decay[:, d, t * P:(t + 1) * P],
                                      start=False, stop=False, skip_group_check=True)
                        pe.matmul(out, u_sb[:, k % 2, d], qk_decay[:, d, t], start=(k == 0 and d == 0), stop=False,
                                  skip_group_check=True).then_inc(o_added, 1)

                    solve(0, t_joined, (h + 1) * (2 * LEVELS) - 1)
                    solve(1, x_set, 4 * h + 1)
                    for k in range(2):
                        for d in range(2):
                            outputs(k, d)
                    for d in range(2):
                        t = SCAN[d][2]
                        pe.wait_ge(s_updated, 2 * h + d + 1)
                        pe.matmul(bank[d][:, 0:P], k_head[:, t * P:(t + 1) * P], s_new[:, d], start=True, stop=True).then_inc(ks_ready, 1)
                    solve(2, x_set, 4 * h + 3)
                    pe.wait_ge(sel_ready, h + 2)
                    spread_norms()
                    for d in range(2):
                        outputs(2, d)
                    spread_rows()
                for h in range(H):
                    pe.wait_ge(o_squared, h + 1)
                    pe.matmul(bank[4][0:H, 0:T], one_hot[:, 2 * H - 1 - h:3 * H - 1 - h], square[:, h % 4],
                              start=(h == 0), stop=(h == H - 1)).then_inc(o_summed, 1)
                pe.wait_ge(o_rnorm_ready, 1)
                for h in range(H):
                    if h >= 2:
                        pe.wait_ge(o_gated, H + h - 1)
                    pe.matmul(bank[h % 2][:, 0:T], ident[0:H, h:h + 1].to_broadcast([H, P]), qk_norm[0:H, :],
                              start=True, stop=True).then_inc(o_spread, 1)
                units_of_input(u0 + DN_BLOCKS, ((0, bank[2]), (1, bank[3])), o_lo, 0)
                for o in range(2, KC):
                    pe.wait_ge(r_ready, KC * 4 + o)
                    unit(u0 + DN_BLOCKS + o, o % RING, bank[2 + o % 2][:, 0:T], h_hi, h_lo, range(KC))

            pe.wait_ge(consts, 6)
            loads = (2, 2, 1, 2, 7)
            for t in range(5):
                pe.wait_ge(table_in[t], 16 * loads[t])
                if t == 4:
                    pe.wait_ge(table_out, 1)
                pe.transpose(bank[t % 4][:, 0:P], table[:, t, :], ident[:, :]).then_inc(turned, 1)
            pe.wait_ge(table_out, 5)
            for t in range(NT):
                pe.wait_ge(x_in[t], 16)
            for o in range(KC):
                if o >= 2:
                    pe.wait_ge(x_ready, o - 1)
                for t in range(NT):
                    mm = pe.transpose(bank[o % 2][:, t * P:(t + 1) * P], x_rows[:, t, o * P:(o + 1) * P], ident[:, :])
                mm.then_inc(turned, 1)
            pe.wait_ge(cond_ready, 2)
            for g in range(MOD_FIRST):
                for k in range(KC):
                    mod_slice(g, 0, k)
                turn_mod(g, 0)

            for s in range(stages):
                u0 = UNIT0[s]
                if is_ffn[s]:
                    f0 = FC * ffns[s]
                    def in_pair(pair, eighth=0, beside=None):
                        for q in range(2):
                            for j, ps in ((2 * q, bank[q]), (2 * q + 1, bank[2 + q])):
                                if j == 0:
                                    units_of_input(u0 + 4 * pair, ((0, bank[0]), (1, bank[2])), h_lo_ready, KC * s)
                                elif j >= 2:
                                    unit(u0 + 4 * pair + j, j, ps[:, 0:T], h_hi, h_lo, range(KC))
                                if beside is not None:
                                    for k in in_slices(eighth + j):
                                        mod_slice(mod_in_chunk[s], beside, k)
                            pe.wait_ge(act_ready, f0 + 2 * pair + q + 1)

                    if s in MOD_BESIDE_IN:
                        with pe.Fori(0, MOD_BESIDE_IN[s]) as i:
                            in_pair(2 * i, 0, i)
                            in_pair(2 * i + 1, 4, i)
                            turn_mod(mod_in_chunk[s], i)
                        for pair in range(2 * MOD_BESIDE_IN[s], FC // 2):
                            in_pair(pair)
                    else:
                        with pe.Fori(0, FC // 2) as i:
                            in_pair(i)
                    v0 = u0 + 2 * FC
                    with pe.Fori(0, 2) as i:
                        for q in range(12):
                            a, b = FFN_THIRDS[q % 3]
                            pe.wait_ge(act_lo_ready, f0 + b)
                            unit(v0 + 12 * i + q, q % RING, bank[(q // 3) % 2][:, 0:T], act_hi, act_lo, range(a, b),
                                 first=(a == 0), last=(b == FC))
                            if q % 3 == 2:
                                pe.wait_ge(r_ready, KC * s + 4 * i + q // 3 + 1)
                            for k in out_slices(s, q):
                                mod_slice(mod_out_chunk[s], i, k)
                            if s in MOD_BESIDE_OUT and q == KC + 1:
                                turn_mod(mod_out_chunk[s], i)
                elif s == 1:
                    with pe.Fori(0, KC // 2) as i:
                        for q in range(2):
                            for j, ps in ((2 * q, bank[q]), (2 * q + 1, bank[2 + q])):
                                if j == 0:
                                    units_of_input(u0 + 4 * i, ((0, bank[0]), (1, bank[2])), h_lo_ready, KC * s)
                                elif j >= 2:
                                    unit(u0 + 4 * i + j, j, ps[:, 0:T], h_hi, h_lo, range(KC))
                            pe.wait_ge(glu_ready, 2 * i + q + 1)
                    for o in range(KC):
                        pe.wait_ge(tap_v, (TAPS + 1) * (o + 1) + (2 * GR - 1) * max(0, o + 1 - KC // 2))
                        if o < KC // 2:
                            pe.wait_ge(tap_g, (TAPS - 1) * (o + 1))
                        mm = pe.matmul(mean_ps[:, 0:T], mean_w[:, :], conv[:, o], start=(o == 0), stop=(o == KC - 1))
                    mm.then_inc(conv_mean, 1)
                    variance(1)
                    for o in range(KC):
                        if o >= 2:
                            pe.wait_ge(y_ready, o - 1)
                        if o == 0:
                            units_of_input(u0 + 2 * KC, ((0, bank[0]), (1, bank[1])), conv_lo, 0)
                        elif o >= 2:
                            unit(u0 + 2 * KC + o, o % RING, bank[o % 2][:, 0:T], h_hi, h_lo, range(KC))
                elif s == 4:
                    delta_on_tensor(u0)
                pe.wait_ge(r_summed, KC * (s + 1))
                pe.matmul(mean_ps[:, 0:T], mean_w[:, :], r_sum[:, :], start=True, stop=False)
                pe.wait_ge(r_ready, KC * (s + 1) + 1)
                pe.matmul(mean_ps[:, 0:T], mean_w[:, :], r[:, KC - 1], start=False, stop=True).then_inc(mean_ready, 1)
                variance(norm_of(s))

            pe.wait_ge(x_ready, KC * (stages + 1))
            for t in range(NT):
                for half in range(2):
                    n = 2 * t + half
                    if n >= 4:
                        pe.wait_ge(rows_ready, n - 3)
                    for o in range(4):
                        mm = pe.transpose(bank[n % 4][:, o * P:(o + 1) * P], x[:, 4 * half + o, t * P:(t + 1) * P], ident[:, :])
                    mm.then_inc(turned, 1)


_INS = ['x_prompt', 'x_sample', 'state_delta', 'c', 'c_ctx', 'w_mod', 'b_mod', 'ln_g', 'ln_b', 'ffn_w_in', 'ffn_w_out',
        'cv_w1', 'cv_b1', 'cv_dw', 'cv_dwb', 'cv_ln_g', 'cv_ln_b', 'cv_w2', 'cv_b2',
        'dn_w_in', 'dn_conv', 'dn_a_log', 'dn_dt_bias', 'dn_norm_g', 'dn_w_out']
_OUTS = [(1, TP, D), (1, TS, D), (1, 1, 2, H, P, P)]


def kernel(**inputs):
    import concourse.bacc as bacc
    from concourse.bass_utils import run_bass_kernel_spmd

    nc = bacc.Bacc("TRN2", target_bir_lowering=False, num_devices=1)
    arrays, args = {}, []
    for name in _INS:
        a = np.ascontiguousarray(inputs[name])
        arrays["in_" + name] = a
        args.append(nc.dram_tensor("in_" + name, a.shape, mybir.dt.from_np(a.dtype), kind="ExternalInput").ap())
    for i, shape in enumerate(_OUTS):
        args.append(nc.dram_tensor(f"out_{i}", shape, F32, kind="ExternalOutput").ap())
    program(nc, *args)
    res = run_bass_kernel_spmd(nc, [arrays], core_ids=[0])
    return tuple(res.results[0][f"out_{i}"] for i in range(len(_OUTS)))
```
